# Optimizing a Trainium2 kernel written in Bass

```python
import math
import jax, jax.numpy as jnp
from jax import lax
import numpy as np
import jax
import jax.numpy as jnp

D_MODEL = 1024
BATCH = 1
SEQ = 256
DEPTH = 1

N_META = 16
NORM_EPS = 1e-6
HG_HEADS = 8
HG_DK = D_MODEL // HG_HEADS
HG_DV = D_MODEL // HG_HEADS
HG_WIDTH = HG_HEADS * HG_DK
HG_CHUNK = 16
MLA_HEADS = 8
QK_NOPE = 128
QK_ROPE = 64
V_HEAD = 128
Q_LORA = 256
KV_LORA = 256
ROPE_THETA = 10000.0
ATTN_BLOCK = 128
FFN_HIDDEN = ((8 * D_MODEL + 3 * 256 - 1) // (3 * 256)) * 256
IN_SIZES = (HG_WIDTH, HG_WIDTH, HG_WIDTH, HG_WIDTH,
            Q_LORA, KV_LORA, QK_ROPE,
            D_MODEL, D_MODEL)
IN_COLS = sum(IN_SIZES)


def rms_norm(x, g):
    xf = x.astype(jnp.float32)
    y = xf * lax.rsqrt(jnp.mean(xf * xf, axis=-1, keepdims=True) + NORM_EPS)
    return (y * g.astype(jnp.float32)).astype(x.dtype)

def rope_tables(length):
    pos = jnp.arange(length, dtype=jnp.float32)
    inv_freq = 1.0 / (ROPE_THETA ** (jnp.arange(0, QK_ROPE, 2, dtype=jnp.float32) / QK_ROPE))
    ang = pos[:, None] * inv_freq[None, :]
    return jnp.cos(ang), jnp.sin(ang)

def apply_rope(t, cos, sin):
    t32 = t.astype(jnp.float32)
    t1, t2 = jnp.split(t32, 2, axis=-1)
    return jnp.concatenate([t1 * cos - t2 * sin, t2 * cos + t1 * sin], axis=-1).astype(t.dtype)

def hgrn2_chunk_scan(q, k, v, logf):
    B, L, H, _ = q.shape
    n = L // HG_CHUNK

    def to_chunks(t):
        return t.reshape(B, n, HG_CHUNK, H, t.shape[-1]).transpose(1, 0, 3, 2, 4)

    xs = (to_chunks(q), to_chunks(k), to_chunks(v), to_chunks(logf))
    causal = jnp.tril(jnp.ones((HG_CHUNK, HG_CHUNK), dtype=bool))[:, :, None]

    def step(S, inp):
        qb, kb, vb, gb = inp
        b = jnp.cumsum(gb, axis=2)
        o_inter = jnp.einsum('bhtk,bhkv->bhtv', qb * jnp.exp(b), S)
        diff = b[:, :, :, None, :] - b[:, :, None, :, :]
        decay = jnp.exp(jnp.where(causal, diff, -jnp.inf))
        A = jnp.einsum('bhtsk,bhsk->bhts', decay * qb[:, :, :, None, :], kb)
        o_intra = jnp.einsum('bhts,bhsv->bhtv', A, vb)
        b_last = b[:, :, -1:, :]
        S_new = jnp.exp(b_last[:, :, 0, :])[..., None] * S + jnp.einsum(
            'bhsk,bhsv->bhkv', kb * jnp.exp(b_last - b), vb)
        return S_new, o_inter + o_intra

    S0 = jnp.zeros((B, H, q.shape[-1], v.shape[-1]), jnp.float32)
    _, ys = lax.scan(step, S0, xs)
    return ys.transpose(1, 0, 3, 2, 4).reshape(B, L, H, v.shape[-1])

def hgrn2_mixer(q, f_pre, i, g, lb, norm_g):
    B, L, _ = q.shape
    split = lambda t: t.reshape(B, L, HG_HEADS, -1).astype(jnp.float32)
    qh = jax.nn.silu(split(q))
    lbh = lb.astype(jnp.float32).reshape(HG_HEADS, HG_DK)
    fgate = lbh + (1.0 - lbh) * jax.nn.sigmoid(split(f_pre))
    o = hgrn2_chunk_scan(qh, 1.0 - fgate, split(i), jnp.log(fgate))
    o = rms_norm(o, norm_g) * jax.nn.silu(split(g))
    return o.reshape(B, L, HG_WIDTH).astype(q.dtype)

def mla_mixer(c_q, c_kv, k_pe, q_norm_g, w_q_b, kv_norm_g, w_kv_b, cos, sin):
    B, L, _ = c_q.shape
    q = (rms_norm(c_q, q_norm_g) @ w_q_b).reshape(B, L, MLA_HEADS, QK_NOPE + QK_ROPE)
    q_nope = q[..., :QK_NOPE]
    q_pe = apply_rope(q[..., QK_NOPE:], cos[:, None, :], sin[:, None, :])
    kv = (rms_norm(c_kv, kv_norm_g) @ w_kv_b).reshape(B, L, MLA_HEADS, QK_NOPE + V_HEAD)
    k_nope, v = kv[..., :QK_NOPE], kv[..., QK_NOPE:]
    k_pe = apply_rope(k_pe, cos, sin)
    scale = (QK_NOPE + QK_ROPE) ** -0.5
    bounds = [(0, N_META)] + [(N_META + s, min(N_META + s + ATTN_BLOCK, L))
                              for s in range(0, L - N_META, ATTN_BLOCK)]
    outs = []
    for start, end in bounds:
        s = (jnp.einsum('bqhd,bkhd->bhqk', q_nope[:, start:end], k_nope[:, :end])
             + jnp.einsum('bqhr,bkr->bhqk', q_pe[:, start:end], k_pe[:, :end]))
        s = s.astype(jnp.float32) * scale
        qpos = jnp.arange(start, end)[:, None]
        kpos = jnp.arange(end)[None, :]
        s = jnp.where(kpos <= qpos, s, -jnp.inf)
        p = jax.nn.softmax(s, axis=-1).astype(v.dtype)
        outs.append(jnp.einsum('bhqk,bkhd->bqhd', p, v[:, :end]))
    o = jnp.concatenate(outs, axis=1)
    return o.reshape(B, L, MLA_HEADS * V_HEAD)

def first_inputs(seed: int = 0) -> dict:
    key = jax.random.key(seed)
    ks = jax.random.split(key, 20)
    nrm = lambda k, shape, scale: jax.random.normal(k, shape, jnp.float32) * scale
    gain = lambda k, shape: 1.0 + 0.02 * jax.random.normal(k, shape, jnp.float32)
    return {
        "x": nrm(ks[0], (BATCH, SEQ, D_MODEL), 1.0),
        "meta_tokens": nrm(ks[1], (N_META, D_MODEL), 1.0),
        "w_in": nrm(ks[2], (DEPTH, D_MODEL, IN_COLS), D_MODEL ** -0.5),
        "b_gate": nrm(ks[3], (DEPTH, 2 * D_MODEL), 0.01),
        "lb_logits": nrm(ks[4], (DEPTH + 1, HG_WIDTH), 0.1),
        "hg_norm_g": gain(ks[5], (DEPTH, HG_DV)),
        "w_hg_o": nrm(ks[6], (DEPTH, HG_WIDTH, D_MODEL), HG_WIDTH ** -0.5),
        "q_a_norm_g": gain(ks[7], (DEPTH, Q_LORA)),
        "w_q_b": nrm(ks[8], (DEPTH, Q_LORA, MLA_HEADS * (QK_NOPE + QK_ROPE)), Q_LORA ** -0.5),
        "kv_a_norm_g": gain(ks[9], (DEPTH, KV_LORA)),
        "w_kv_b": nrm(ks[10], (DEPTH, KV_LORA, MLA_HEADS * (QK_NOPE + V_HEAD)), KV_LORA ** -0.5),
        "w_mla_o": nrm(ks[11], (DEPTH, MLA_HEADS * V_HEAD, D_MODEL), (MLA_HEADS * V_HEAD) ** -0.5),
        "w_out": nrm(ks[12], (DEPTH, D_MODEL, D_MODEL), D_MODEL ** -0.5),
        "mix_pre_g": gain(ks[13], (DEPTH, D_MODEL)),
        "mix_post_g": gain(ks[14], (DEPTH, D_MODEL)),
        "ffn_pre_g": gain(ks[15], (DEPTH, D_MODEL)),
        "ffn_post_g": gain(ks[16], (DEPTH, D_MODEL)),
        "w_ffn_in": nrm(ks[17], (DEPTH, D_MODEL, 2 * FFN_HIDDEN), D_MODEL ** -0.5),
        "w_ffn_out": nrm(ks[18], (DEPTH, FFN_HIDDEN, D_MODEL), FFN_HIDDEN ** -0.5),
    }

def first_block(x, meta_tokens, w_in, b_gate, lb_logits, hg_norm_g, w_hg_o, q_a_norm_g, w_q_b,
              kv_a_norm_g, w_kv_b, w_mla_o, w_out, mix_pre_g, mix_post_g, ffn_pre_g, ffn_post_g,
              w_ffn_in, w_ffn_out):
    B = x.shape[0]
    meta = jnp.broadcast_to(meta_tokens[None].astype(x.dtype), (B, N_META, D_MODEL))
    h = jnp.concatenate([meta, x], axis=1)
    L = h.shape[1]
    cos, sin = rope_tables(L)
    lower_bounds = jnp.cumsum(jax.nn.softmax(lb_logits.astype(jnp.float32), axis=0), axis=0)
    splits = []
    acc = 0
    for sz in IN_SIZES[:-2]:
        acc += sz
        splits.append(acc)
    for l in range(DEPTH):
        u = rms_norm(h, mix_pre_g[l])
        proj = u @ w_in[l]
        hq, hf, hi, hg, cq, ckv, kpe, gates = jnp.split(proj, splits, axis=-1)
        y_a = hgrn2_mixer(hq, hf, hi, hg, lower_bounds[l], hg_norm_g[l]) @ w_hg_o[l]
        y_b = mla_mixer(cq, ckv, kpe, q_a_norm_g[l], w_q_b[l], kv_a_norm_g[l], w_kv_b[l],
                        cos, sin) @ w_mla_o[l]
        gate_a, gate_b = jnp.split(jax.nn.sigmoid(gates + b_gate[l]), 2, axis=-1)
        mixed = (gate_a * y_a + gate_b * y_b) @ w_out[l]
        h = h + rms_norm(mixed, mix_post_g[l])
        u = rms_norm(h, ffn_pre_g[l])
        gt, up = jnp.split(u @ w_ffn_in[l], 2, axis=-1)
        h = h + rms_norm((jax.nn.silu(gt) * up) @ w_ffn_out[l], ffn_post_g[l])
    return h[:, N_META:, :]


N_MIXERS = 4
N_HEADS = 16
GROUP_HEADS = N_HEADS // N_MIXERS
HEAD_DIM = D_MODEL // N_HEADS
GROUP_WIDTH = GROUP_HEADS * HEAD_DIM

MOBA_BLOCK = 256
MOBA_TOPK = 3

NSA_KV_HEADS = 1
NSA_CMP_LEN = 32
NSA_CMP_STRIDE = 16
NSA_CMP_HIDDEN = 2 * HEAD_DIM
NSA_SEL_BLOCK = 64
NSA_SEL_TOPN = 16
NSA_WINDOW = 512

DIFF_QK_DIM = HEAD_DIM // 2

SWA_KV_HEADS = 2
SWA_WINDOW = 128

D_FF = 4 * D_MODEL
CONV_WIDTH = 3

Q_BLOCK = 128
GATHER_Q_BLOCK = 32
NEG_INF = -1e30
TINY = 1e-30
FORCED_SCORE = 1e4

NSA_KV_WIDTH = NSA_KV_HEADS * HEAD_DIM
SWA_KV_WIDTH = SWA_KV_HEADS * HEAD_DIM
IN_SPLITS = (GROUP_WIDTH, GROUP_WIDTH, GROUP_WIDTH,
             GROUP_WIDTH, NSA_KV_WIDTH, NSA_KV_WIDTH, NSA_KV_WIDTH,
             NSA_KV_WIDTH, NSA_KV_WIDTH, NSA_KV_WIDTH, 3 * GROUP_HEADS,
             GROUP_WIDTH, GROUP_WIDTH, GROUP_WIDTH,
             GROUP_WIDTH, SWA_KV_WIDTH, SWA_KV_WIDTH)
D_IN = sum(IN_SPLITS)


def _rms_norm(x, gain):
    xf = x.astype(jnp.float32)
    y = xf * lax.rsqrt(jnp.mean(xf * xf, axis=-1, keepdims=True) + NORM_EPS)
    return (y * gain.astype(jnp.float32)).astype(x.dtype)

def _alibi_slopes(mixer):
    slopes = np.power(np.float32(2.0), np.arange(1, N_HEADS + 1, dtype=np.float32) * np.float32(-8.0 / N_HEADS))
    return jnp.asarray(slopes[mixer::N_MIXERS], dtype=jnp.float32)

def _masked_softmax(s, mask, sink=None):
    s = jnp.where(mask, s, NEG_INF)
    m = jnp.max(s, axis=-1, keepdims=True)
    if sink is not None:
        m = jnp.maximum(m, sink)
    p = jnp.where(mask, jnp.exp(s - m), 0.0)
    denom = jnp.sum(p, axis=-1, keepdims=True)
    if sink is not None:
        denom = denom + jnp.exp(sink - m)
    return p / jnp.maximum(denom, TINY)

def _heads(t, n):
    b, s, _ = t.shape
    return t.reshape(b, s, n, -1).transpose(0, 2, 1, 3)

def _merge(t):
    b, h, s, d = t.shape
    return t.transpose(0, 2, 1, 3).reshape(b, s, h * d)

def _to_chunks(t, qb, axis):
    shp = t.shape
    t = t.reshape(shp[:axis] + (shp[axis] // qb, qb) + shp[axis + 1:])
    return jnp.moveaxis(t, axis, 0)

def _from_chunks(t, axis):
    t = jnp.moveaxis(t, 0, axis)
    shp = t.shape
    return t.reshape(shp[:axis] + (shp[axis] * shp[axis + 1],) + shp[axis + 2:])

def _gather_blocks(blocks, idx):
    g = jax.vmap(jax.vmap(lambda bl, i: bl[i]))(blocks, idx)
    b, h, q, k, l, d = g.shape
    return g.reshape(b, h, q, k * l, d)

def _banded_attention(q, k, v, slopes, window, sinks=None):
    b, g, r, s, dh = q.shape
    nb = s // Q_BLOCK
    n_prev = -(-window // Q_BLOCK)

    def bands(t):
        tp = jnp.pad(t, ((0, 0), (0, 0), (n_prev * Q_BLOCK, 0), (0, 0))).reshape(b, g, nb + n_prev, Q_BLOCK, dh)
        return jnp.concatenate([tp[:, :, p:p + nb] for p in range(n_prev + 1)], axis=3)

    kb, vb = bands(k), bands(v)
    qpos = jnp.arange(s).reshape(nb, Q_BLOCK)
    kpos = (jnp.arange(nb)[:, None] - n_prev) * Q_BLOCK + jnp.arange((n_prev + 1) * Q_BLOCK)
    dist = qpos[:, :, None] - kpos[:, None, :]
    mask = (kpos[:, None, :] >= 0) & (dist >= 0) & (dist < window)
    qr = q.reshape(b, g, r, nb, Q_BLOCK, dh)
    sc = jnp.einsum('bgrnqd,bgnkd->bgrnqk', qr, kb).astype(jnp.float32) * (dh ** -0.5)
    sc = sc - slopes[:, :, None, None, None] * dist.astype(jnp.float32)
    sink = None if sinks is None else sinks.astype(jnp.float32)[:, :, None, None, None]
    p = _masked_softmax(sc, mask, sink)
    o = jnp.einsum('bgrnqk,bgnkd->bgrnqd', p.astype(vb.dtype), vb)
    return o.reshape(b, g, r, s, dh)

def _moba_attention(q, k, v, slopes):
    b, h, s, dh = q.shape
    nb = -(-s // MOBA_BLOCK)
    pad = nb * MOBA_BLOCK - s
    kp = jnp.pad(k, ((0, 0), (0, 0), (0, pad), (0, 0))).reshape(b, h, nb, MOBA_BLOCK, dh)
    vp = jnp.pad(v, ((0, 0), (0, 0), (0, pad), (0, 0))).reshape(b, h, nb, MOBA_BLOCK, dh)
    pos = jnp.arange(s)
    qblk = pos // MOBA_BLOCK
    own = jnp.broadcast_to(qblk[None, None, :, None], (b, h, s, 1))
    n_top = min(MOBA_TOPK, nb - 1)
    if n_top > 0:
        kmean = jnp.mean(kp.astype(jnp.float32), axis=3)
        gate = jnp.einsum('bhsd,bhnd->bhsn', q.astype(jnp.float32), kmean)
        past = jnp.arange(nb)[None, :] < qblk[:, None]
        gate = jnp.where(past, gate, NEG_INF)
        top_val, top_idx = lax.top_k(gate, n_top)
        sel_idx = jnp.concatenate([top_idx, own], axis=-1)
        sel_ok = jnp.concatenate([top_val > 0.5 * NEG_INF, jnp.ones(own.shape, dtype=bool)], axis=-1)
    else:
        sel_idx = own
        sel_ok = jnp.ones(own.shape, dtype=bool)
    scale = dh ** -0.5
    offs = jnp.arange(MOBA_BLOCK)

    def chunk(args):
        qc, ic, okc, tc = args
        kg = _gather_blocks(kp, ic)
        vg = _gather_blocks(vp, ic)
        kpos = (ic[..., None] * MOBA_BLOCK + offs).reshape(ic.shape[:3] + (-1,))
        ok = jnp.repeat(okc, MOBA_BLOCK, axis=-1)
        sc = jnp.einsum('bhqd,bhqkd->bhqk', qc, kg).astype(jnp.float32) * scale
        sc = sc - slopes[None, :, None, None] * (tc[:, None] - kpos).astype(jnp.float32)
        p = _masked_softmax(sc, ok & (kpos <= tc[:, None]))
        return jnp.einsum('bhqk,bhqkd->bhqd', p.astype(vg.dtype), vg)

    out = lax.map(chunk, (_to_chunks(q, GATHER_Q_BLOCK, 2), _to_chunks(sel_idx, GATHER_Q_BLOCK, 2),
                          _to_chunks(sel_ok, GATHER_Q_BLOCK, 2), pos.reshape(-1, GATHER_Q_BLOCK)))
    return _from_chunks(out, 2)

def _nsa_compress(x, pos_emb, w1, b1, w2):
    b, g, s, dh = x.shape
    n_sub = NSA_CMP_LEN // NSA_CMP_STRIDE
    c = x.reshape(b, g, s // NSA_CMP_STRIDE, NSA_CMP_STRIDE, dh)
    nc = c.shape[2] - n_sub + 1
    win = jnp.concatenate([c[:, :, i:i + nc] for i in range(n_sub)], axis=3)
    hid = jax.nn.gelu(jnp.einsum('bgnld,ldf->bgnf', win + pos_emb, w1) + b1)
    return jnp.einsum('bgnf,fd->bgnd', hid, w2)

def _cmp_to_sel_matrix(nc, nsel):
    cs = np.arange(nc)[:, None] * NSA_CMP_STRIDE
    bs = np.arange(nsel)[None, :] * NSA_SEL_BLOCK
    ov = np.clip(np.minimum(cs + NSA_CMP_LEN, bs + NSA_SEL_BLOCK) - np.maximum(cs, bs), 0, None)
    return (ov / NSA_CMP_LEN).astype(np.float32)

def _nsa_attention(q, k_cmp, v_cmp, k_slc, v_slc, k_win, v_win, gates, slopes, cmp_k, cmp_v):
    b, h, s, dh = q.shape
    g = NSA_KV_HEADS
    r = h // g
    qg = q.reshape(b, g, r, s, dh)
    sl = slopes.reshape(g, r)
    kc = _nsa_compress(k_cmp, *cmp_k)
    vc = _nsa_compress(v_cmp, *cmp_v)
    nc = kc.shape[2]
    cmp_end = jnp.arange(nc) * NSA_CMP_STRIDE + NSA_CMP_LEN - 1
    nsel = s // NSA_SEL_BLOCK
    n_top = min(NSA_SEL_TOPN, nsel)
    overlap = jnp.asarray(_cmp_to_sel_matrix(nc, nsel))
    ks = k_slc.reshape(b, g, nsel, NSA_SEL_BLOCK, dh)
    vs = v_slc.reshape(b, g, nsel, NSA_SEL_BLOCK, dh)
    blk_ids = jnp.arange(nsel)
    offs = jnp.arange(NSA_SEL_BLOCK)
    scale = dh ** -0.5

    def chunk(args):
        qc, tc = args
        sc = jnp.einsum('bgrqd,bgnd->bgrqn', qc, kc).astype(jnp.float32) * scale
        sc = sc - sl[:, :, None, None] * (tc[:, None] - cmp_end).astype(jnp.float32)
        p_c = _masked_softmax(sc, cmp_end <= tc[:, None])
        o_c = jnp.einsum('bgrqn,bgnd->bgrqd', p_c.astype(vc.dtype), vc)
        imp = jnp.einsum('bgrqn,ns->bgqs', p_c, overlap)
        qblk = tc // NSA_SEL_BLOCK
        forced = (blk_ids == 0) | (blk_ids == qblk[:, None]) | (blk_ids == qblk[:, None] - 1)
        score = jnp.where(forced, FORCED_SCORE, imp)
        score = jnp.where(blk_ids * NSA_SEL_BLOCK <= tc[:, None], score, NEG_INF)
        top_val, top_idx = lax.top_k(score, n_top)
        ok = jnp.repeat(top_val > 0.5 * NEG_INF, NSA_SEL_BLOCK, axis=-1)
        kg = _gather_blocks(ks, top_idx)
        vg = _gather_blocks(vs, top_idx)
        kpos = (top_idx[..., None] * NSA_SEL_BLOCK + offs).reshape(top_idx.shape[:3] + (-1,))
        dist = (tc[:, None] - kpos)[:, :, None]
        s2 = jnp.einsum('bgrqd,bgqkd->bgrqk', qc, kg).astype(jnp.float32) * scale
        s2 = s2 - sl[:, :, None, None] * dist.astype(jnp.float32)
        p_s = _masked_softmax(s2, ok[:, :, None] & (dist >= 0))
        o_s = jnp.einsum('bgrqk,bgqkd->bgrqd', p_s.astype(vg.dtype), vg)
        return o_c, o_s

    o_c, o_s = lax.map(chunk, (_to_chunks(qg, GATHER_Q_BLOCK, 3), jnp.arange(s).reshape(-1, GATHER_Q_BLOCK)))
    o_c = _from_chunks(o_c, 3).reshape(b, h, s, dh)
    o_s = _from_chunks(o_s, 3).reshape(b, h, s, dh)
    o_w = _banded_attention(qg, k_win, v_win, sl, NSA_WINDOW).reshape(b, h, s, dh)
    return gates[..., 0:1] * o_c + gates[..., 1:2] * o_s + gates[..., 2:3] * o_w

def _diff_attention(q1, q2, k1, k2, v, slopes, lq1, lk1, lq2, lk2, subln, lambda_init):
    b, h, s, dq = q1.shape
    scale = dq ** -0.5
    lam = (jnp.exp(jnp.sum(lq1.astype(jnp.float32) * lk1.astype(jnp.float32)))
           - jnp.exp(jnp.sum(lq2.astype(jnp.float32) * lk2.astype(jnp.float32))) + lambda_init)
    kpos = jnp.arange(s)

    def chunk(args):
        a1, a2, tc = args
        dist = (tc[:, None] - kpos).astype(jnp.float32)
        mask = dist >= 0
        bias = -slopes[:, None, None] * dist
        s1 = jnp.einsum('bhqd,bhkd->bhqk', a1, k1).astype(jnp.float32) * scale + bias
        s2 = jnp.einsum('bhqd,bhkd->bhqk', a2, k2).astype(jnp.float32) * scale + bias
        p = _masked_softmax(s1, mask) - lam * _masked_softmax(s2, mask)
        return jnp.einsum('bhqk,bhkd->bhqd', p.astype(v.dtype), v)

    o = lax.map(chunk, (_to_chunks(q1, Q_BLOCK, 2), _to_chunks(q2, Q_BLOCK, 2), kpos.reshape(-1, Q_BLOCK)))
    o = _from_chunks(o, 2)
    return _rms_norm(o, subln) * (1.0 - lambda_init)

def _swa_attention(q, k, v, slopes, sinks):
    b, h, s, dh = q.shape
    g = SWA_KV_HEADS
    r = h // g
    o = _banded_attention(q.reshape(b, g, r, s, dh), k, v, slopes.reshape(g, r), SWA_WINDOW, sinks.reshape(g, r))
    return o.reshape(b, h, s, dh)

def _conv_ffn(x, w_gate, w_up, conv_w, conv_b, w_down):
    a = x @ w_gate
    a = lax.conv_general_dilated(a, conv_w[:, None, :], window_strides=(1,), padding=[(CONV_WIDTH - 1, 0)],
                                 dimension_numbers=('NWC', 'WIO', 'NWC'), feature_group_count=a.shape[-1]) + conv_b
    return (jax.nn.gelu(a, approximate=True) * (x @ w_up)) @ w_down

def second_inputs(seed: int = 0) -> dict:
    key = jax.random.key(seed)
    keys = iter(jax.random.split(key, 40))

    def nrm(shape, scale):
        return jax.random.normal(next(keys), shape, jnp.float32) * scale

    L = DEPTH
    return {
        'x': nrm((BATCH, SEQ, D_MODEL), 1.0),
        'attn_pre_norm': 1.0 + nrm((L, D_MODEL), 0.02),
        'attn_post_norm': 1.0 + nrm((L, D_MODEL), 0.02),
        'ffn_pre_norm': 1.0 + nrm((L, D_MODEL), 0.02),
        'ffn_post_norm': 1.0 + nrm((L, D_MODEL), 0.02),
        'w_in': nrm((L, D_MODEL, D_IN), D_MODEL ** -0.5),
        'w_out': nrm((L, D_MODEL, D_MODEL), D_MODEL ** -0.5),
        'nsa_cmp_pos_k': nrm((L, NSA_CMP_LEN, HEAD_DIM), 0.1),
        'nsa_cmp_w1_k': nrm((L, NSA_CMP_LEN, HEAD_DIM, NSA_CMP_HIDDEN), (NSA_CMP_LEN * HEAD_DIM) ** -0.5),
        'nsa_cmp_b1_k': nrm((L, NSA_CMP_HIDDEN), 0.01),
        'nsa_cmp_w2_k': nrm((L, NSA_CMP_HIDDEN, HEAD_DIM), NSA_CMP_HIDDEN ** -0.5),
        'nsa_cmp_pos_v': nrm((L, NSA_CMP_LEN, HEAD_DIM), 0.1),
        'nsa_cmp_w1_v': nrm((L, NSA_CMP_LEN, HEAD_DIM, NSA_CMP_HIDDEN), (NSA_CMP_LEN * HEAD_DIM) ** -0.5),
        'nsa_cmp_b1_v': nrm((L, NSA_CMP_HIDDEN), 0.01),
        'nsa_cmp_w2_v': nrm((L, NSA_CMP_HIDDEN, HEAD_DIM), NSA_CMP_HIDDEN ** -0.5),
        'diff_lambda_q1': nrm((L, DIFF_QK_DIM), 0.1),
        'diff_lambda_k1': nrm((L, DIFF_QK_DIM), 0.1),
        'diff_lambda_q2': nrm((L, DIFF_QK_DIM), 0.1),
        'diff_lambda_k2': nrm((L, DIFF_QK_DIM), 0.1),
        'diff_subln': 1.0 + nrm((L, HEAD_DIM), 0.02),
        'swa_sinks': nrm((L, GROUP_HEADS), 0.5),
        'ffn_w_gate': nrm((L, D_MODEL, D_FF), D_MODEL ** -0.5),
        'ffn_w_up': nrm((L, D_MODEL, D_FF), D_MODEL ** -0.5),
        'ffn_conv_w': nrm((L, CONV_WIDTH, D_FF), CONV_WIDTH ** -0.5),
        'ffn_conv_b': nrm((L, D_FF), 0.01),
        'ffn_w_down': nrm((L, D_FF, D_MODEL), D_FF ** -0.5),
    }

def second_block(x, attn_pre_norm, attn_post_norm, ffn_pre_norm, ffn_post_norm, w_in, w_out,
              nsa_cmp_pos_k, nsa_cmp_w1_k, nsa_cmp_b1_k, nsa_cmp_w2_k,
              nsa_cmp_pos_v, nsa_cmp_w1_v, nsa_cmp_b1_v, nsa_cmp_w2_v,
              diff_lambda_q1, diff_lambda_k1, diff_lambda_q2, diff_lambda_k2, diff_subln,
              swa_sinks, ffn_w_gate, ffn_w_up, ffn_conv_w, ffn_conv_b, ffn_w_down):
    b, s, _ = x.shape
    splits = np.cumsum(IN_SPLITS)[:-1].tolist()
    for l in range(DEPTH):
        h = _rms_norm(x, attn_pre_norm[l])
        (mq, mk, mv, nq, nkc, nvc, nks, nvs, nkw, nvw, ngate,
         dq, dk, dv, sq, sk, sv) = jnp.split(h @ w_in[l], splits, axis=-1)
        o_moba = _moba_attention(_heads(mq, GROUP_HEADS), _heads(mk, GROUP_HEADS), _heads(mv, GROUP_HEADS),
                                 _alibi_slopes(0))
        gates = jax.nn.sigmoid(ngate.reshape(b, s, GROUP_HEADS, 3).transpose(0, 2, 1, 3))
        o_nsa = _nsa_attention(_heads(nq, GROUP_HEADS), _heads(nkc, NSA_KV_HEADS), _heads(nvc, NSA_KV_HEADS),
                               _heads(nks, NSA_KV_HEADS), _heads(nvs, NSA_KV_HEADS),
                               _heads(nkw, NSA_KV_HEADS), _heads(nvw, NSA_KV_HEADS), gates, _alibi_slopes(1),
                               (nsa_cmp_pos_k[l], nsa_cmp_w1_k[l], nsa_cmp_b1_k[l], nsa_cmp_w2_k[l]),
                               (nsa_cmp_pos_v[l], nsa_cmp_w1_v[l], nsa_cmp_b1_v[l], nsa_cmp_w2_v[l]))
        dq4 = _heads(dq, GROUP_HEADS)
        dk4 = _heads(dk, GROUP_HEADS)
        lambda_init = 0.8 - 0.6 * math.exp(-0.3 * l)
        o_diff = _diff_attention(dq4[..., :DIFF_QK_DIM], dq4[..., DIFF_QK_DIM:],
                                 dk4[..., :DIFF_QK_DIM], dk4[..., DIFF_QK_DIM:], _heads(dv, GROUP_HEADS),
                                 _alibi_slopes(2), diff_lambda_q1[l], diff_lambda_k1[l],
                                 diff_lambda_q2[l], diff_lambda_k2[l], diff_subln[l], lambda_init)
        o_swa = _swa_attention(_heads(sq, GROUP_HEADS), _heads(sk, SWA_KV_HEADS), _heads(sv, SWA_KV_HEADS),
                               _alibi_slopes(3), swa_sinks[l])
        mix = jnp.concatenate([_merge(o_moba), _merge(o_nsa), _merge(o_diff), _merge(o_swa)], axis=-1)
        x = x + _rms_norm(mix @ w_out[l], attn_post_norm[l])
        h = _rms_norm(x, ffn_pre_norm[l])
        x = x + _rms_norm(_conv_ffn(h, ffn_w_gate[l], ffn_w_up[l], ffn_conv_w[l], ffn_conv_b[l], ffn_w_down[l]),
                          ffn_post_norm[l])
    return x


def setup_inputs(seed=0):
    out = dict(first_inputs(seed))
    for name, value in second_inputs(seed + 1).items():
        if name != "x":
            out[name + "_2"] = value
    return out


def reference(
    x, meta_tokens, w_in, b_gate, lb_logits, hg_norm_g, w_hg_o, q_a_norm_g, w_q_b, kv_a_norm_g,
    w_kv_b, w_mla_o, w_out, mix_pre_g, mix_post_g, ffn_pre_g, ffn_post_g, w_ffn_in, w_ffn_out,
    attn_pre_norm_2, attn_post_norm_2, ffn_pre_norm_2, ffn_post_norm_2, w_in_2, w_out_2,
    nsa_cmp_pos_k_2, nsa_cmp_w1_k_2, nsa_cmp_b1_k_2, nsa_cmp_w2_k_2, nsa_cmp_pos_v_2,
    nsa_cmp_w1_v_2, nsa_cmp_b1_v_2, nsa_cmp_w2_v_2, diff_lambda_q1_2, diff_lambda_k1_2,
    diff_lambda_q2_2, diff_lambda_k2_2, diff_subln_2, swa_sinks_2, ffn_w_gate_2, ffn_w_up_2,
    ffn_conv_w_2, ffn_conv_b_2, ffn_w_down_2,
):
    x = first_block(
        x, meta_tokens, w_in, b_gate, lb_logits, hg_norm_g, w_hg_o, q_a_norm_g, w_q_b,
        kv_a_norm_g, w_kv_b, w_mla_o, w_out, mix_pre_g, mix_post_g, ffn_pre_g, ffn_post_g,
        w_ffn_in, w_ffn_out,
    )
    return second_block(
        x, attn_pre_norm_2, attn_post_norm_2, ffn_pre_norm_2, ffn_post_norm_2, w_in_2, w_out_2,
        nsa_cmp_pos_k_2, nsa_cmp_w1_k_2, nsa_cmp_b1_k_2, nsa_cmp_w2_k_2, nsa_cmp_pos_v_2,
        nsa_cmp_w1_v_2, nsa_cmp_b1_v_2, nsa_cmp_w2_v_2, diff_lambda_q1_2, diff_lambda_k1_2,
        diff_lambda_q2_2, diff_lambda_k2_2, diff_subln_2, swa_sinks_2, ffn_w_gate_2, ffn_w_up_2,
        ffn_conv_w_2, ffn_conv_b_2, ffn_w_down_2,
    )


_drawn_inputs = setup_inputs


def setup_inputs(seed=0):
    import zlib

    import numpy as np

    out = dict(_drawn_inputs(seed))
    spreads = {}
    factors = {'b_gate': 8.0,
     'lb_logits': 4.298,
     'q_a_norm_g': 8.0,
     'kv_a_norm_g': 6.545,
     'mix_post_g': 2.757,
     'ffn_pre_g': 2.751,
     'ffn_post_g': 3.948,
     'attn_pre_norm_2': 3.36,
     'attn_post_norm_2': 17.121,
     'ffn_pre_norm_2': 13.314,
     'ffn_post_norm_2': 96.056,
     'nsa_cmp_pos_k_2': 29.227,
     'nsa_cmp_b1_k_2': 200.0,
     'nsa_cmp_pos_v_2': 13.855,
     'nsa_cmp_b1_v_2': 200.0,
     'diff_lambda_q1_2': 8.0,
     'diff_lambda_k1_2': 4.932,
     'diff_lambda_q2_2': 8.0,
     'diff_lambda_k2_2': 7.206,
     'diff_subln_2': 31.865,
     'swa_sinks_2': 200.0,
     'ffn_conv_b_2': 37.917,
     'hg_norm_g': 4.969}
    for name, (base, spread) in spreads.items():
        noise = np.random.default_rng([zlib.crc32(name.encode()), seed]).standard_normal(out[name].shape)
        drawn = base * np.exp(spread * noise) if base else spread * noise
        out[name] = jnp.asarray(drawn.astype(out[name].dtype))
    for name, factor in factors.items():
        out[name] = (out[name] * factor).astype(out[name].dtype)
    return out
```

```python
import numpy as np
import concourse.bass as bass
from concourse import mybir
from concourse.alu_op_type import AluOpType as ALU
from contextlib import ExitStack

FP = mybir.dt.float32
FR = mybir.dt.float32r
U8 = mybir.dt.uint8
ACT = mybir.ActivationFunctionType
AX = mybir.AxisListType

D = 1024
NM = 16
T1 = 272
HID1 = 22
HID2 = 32
LAG = 2
EPS = 1e-6
NEG = -1e30
NRAW = 4
NUNIT = 4
SLABW = 2048
IN1 = dict(hq=0, hf=1024, hi=2048, hg=3072, cq=4096, ckv=4352, kpe=4608, gate=4672)
_o2 = np.cumsum([0, 256, 256, 256, 256, 64, 64, 64, 64, 64, 64, 12, 256, 256, 256, 256, 128, 128])
IN2 = dict(zip(["mq", "mk", "mv", "nq", "nkc", "nvc", "nks", "nvs", "nkw", "nvw", "ng",
                "dq", "dk", "dv", "sq", "sk", "sv"], [int(v) for v in _o2]))
SLOPES = [float(v) for v in
          np.power(np.float32(2.0), np.arange(1, 17, dtype=np.float32) * np.float32(-0.5))]



def stream_blocks():
    b = []

    def a_tile(name, kt, cols):
        for k in range(kt):
            b.append((name, 128 * k, list(cols)))

    def rng(o, n=128):
        return list(range(o, o + n))

    w = "w_in"
    for n in range(8):
        a_tile(w, 8, rng(IN1["hf"] + 128 * n))
    for nh in range(2):
        for k in range(8):
            for j in range(4):
                b.append((w, 128 * k, rng(IN1["hi"] + 512 * nh + 128 * j)))
    for n in range(8):
        a_tile(w, 8, rng(IN1["hq"] + 128 * n))
    for n in range(8):
        a_tile(w, 8, rng(IN1["hg"] + 128 * n))
    kp = rng(IN1["kpe"], 64)
    sw = kp[32:] + kp[:32]
    for n in range(2):
        a_tile(w, 8, rng(IN1["ckv"] + 128 * n))
    a_tile(w, 8, kp + kp)
    a_tile(w, 8, sw + sw)
    for n in range(2):
        a_tile(w, 8, rng(IN1["cq"] + 128 * n))
    for n in range(8):
        a_tile("w_kv_b", 2, rng(256 * n))
    for k in range(2):
        for nh in range(2):
            for j in range(4):
                b.append(("w_kv_b", 128 * k, rng(256 * (4 * nh + j) + 128)))
    for n in range(8):
        a_tile("w_q_b", 2, rng(192 * n))
    for n in range(4):
        p0 = rng(192 * 2 * n + 128, 64)
        p1 = rng(192 * (2 * n + 1) + 128, 64)
        a_tile("w_q_b", 2, p0 + p1)
        a_tile("w_q_b", 2, p0[32:] + p0[:32] + p1[32:] + p1[:32])
    for n in range(16):
        a_tile(w, 8, rng(IN1["gate"] + 128 * n))
    for n in range(8):
        a_tile("w_hg_o", 8, rng(128 * n))
    for n in range(8):
        a_tile("w_mla_o", 8, rng(128 * n))
    for k in range(8):
        for j in range(8):
            b.append(("w_out", 128 * k, rng(128 * j)))

    def ffn(first, up_name, up_off, down, nt):
        for i in range(nt + LAG):
            if i < nt:
                a_tile(first, 8, rng(128 * i))
                a_tile(up_name, 8, rng(up_off + 128 * i))
            if i >= LAG:
                for j in range(8):
                    b.append((down, 128 * (i - LAG), rng(128 * j)))

    ffn("w_ffn_in", "w_ffn_in", 128 * HID1, "w_ffn_out", HID1)
    w = "w_in_2"
    o = IN2
    for n in range(2):
        a_tile(w, 8, rng(o["mq"] + 128 * n))
    for n in range(2):
        a_tile(w, 8, rng(o["mk"] + 128 * n))
    for k in range(8):
        for c in (o["mv"], o["mv"] + 128, o["dv"], o["dv"] + 128):
            b.append((w, 128 * k, rng(c)))
    a_tile(w, 8, rng(o["nkc"]))
    for n in range(2):
        a_tile(w, 8, rng(o["nq"] + 128 * n))
    a_tile(w, 8, rng(o["nks"], 64) * 2)
    for k in range(8):
        b.append((w, 128 * k, rng(o["nvs"], 64) + rng(o["nvw"], 64)))
        b.append((w, 128 * k, rng(o["sv"])))
        b.append((w, 128 * k, rng(o["ng"], 12) + [-1] * 116))
        b.append((w, 128 * k, rng(o["nkw"], 64) * 2))
    for c in (o["dq"], o["dq"] + 128, o["dk"], o["dk"] + 128, o["sq"], o["sq"] + 128):
        a_tile(w, 8, rng(c))
    for g in range(2):
        a_tile(w, 8, rng(o["sk"] + 64 * g, 64) * 2)
    for k in range(8):
        for j in range(8):
            b.append(("w_out_2", 128 * k, rng(128 * j)))
    ffn("ffn_w_gate_2", "ffn_w_up_2", 0, "ffn_w_down_2", HID2)
    return b


BLOCKS = stream_blocks()
NSLAB = -(-len(BLOCKS) // 16)

SM = {}
_at = 0
for _n, _w in [("mix_pre", 8), ("ffn_pre", 8), ("attn_pre", 8), ("ffn_pre2", 8), ("b_gate", 16),
               ("lb0", 8), ("lb1", 8), ("hg_g", 1), ("q_g", 2), ("kv_g", 2), ("conv_w", 96),
               ("conv_b", 32), ("cmp_b1", 2), ("cmp_pos", 32), ("w2k", 128), ("w2v", 64),
               ("subln", 64), ("lam", 128), ("sinks", 4)]:
    SM[_n] = (_at, _w)
    _at += _w
NSM = _at

CO = {}
_at = 0
for _n, _w in [("ident", 128), ("ones", 128), ("esel", 16), ("cos", T1), ("sin", T1),
               ("m0", 144), ("m1", T1), ("dmc", 384), ("dms", 384), ("cmpb", 120)]:
    CO[_n] = (_at, _w)
    _at += _w
NCO = _at


def constants():
    c = np.zeros((128, NCO), np.float32)

    def put(n, v):
        c[:, CO[n][0]:CO[n][0] + CO[n][1]] = v

    p = np.arange(128)
    put("ident", np.eye(128))
    put("ones", 1.0)
    e = np.zeros((128, 16))
    e[:, 8] = 1.0
    put("esel", e)
    inv = (np.float32(1.0) / (np.float32(10000.0) ** (np.arange(0, 64, 2, dtype=np.float32) / np.float32(64))))
    ang = (np.arange(T1, dtype=np.float32)[:, None] * inv[None, :].astype(np.float32)).astype(np.float32)
    cs, sn = np.cos(ang).astype(np.float32), np.sin(ang).astype(np.float32)
    put("cos", cs.T[p % 32])
    put("sin", sn.T[p % 32] * np.where((p % 64) < 32, -1.0, 1.0)[:, None])
    q = p[:, None] + NM
    put("m0", np.where(np.arange(144)[None] <= q, 0.0, NEG))
    put("m1", np.where(np.arange(T1)[None] <= q + 128, 0.0, NEG))
    dist0 = p[:, None] - np.arange(128)[None]
    dist1 = p[:, None] + 128 - np.arange(256)[None]
    d = np.concatenate([dist0, dist1], 1)
    put("dmc", np.where(d >= 0, -d, NEG))
    put("dms", np.where((d >= 0) & (d < 128), -d, NEG))
    cb = np.zeros((128, 2, 4, 15))
    end = np.arange(15) * 16 + 31
    for t in range(2):
        for h in range(4):
            dist = (p[:, None] + 128 * t) - end[None]
            cb[:, t, h] = np.where(dist >= 0, -SLOPES[1 + 4 * h] * dist * 8.0, NEG)
    put("cmpb", cb.reshape(128, 120))
    lev = np.zeros((128, 7, 128), np.float32)
    s, t = p[:, None], p[None]
    for j in range(7):
        lev[:, j] = ((s >> (j + 1)) == (t >> (j + 1))) & (((s >> j) & 1) == 0) & (((t >> j) & 1) == 1)
    return c, lev.reshape(128, 7 * 128)


class Tok:

    def __init__(self, eng, fn, after, sem=None, val=0):
        self.eng, self.fn, self.after = eng, fn, after
        self.sem, self.val, self.used, self.inc = sem, val, sem is not None, 16 if sem is not None else 1


def flat(x):
    if x is None:
        return []
    if isinstance(x, Tok):
        return [x]
    out = []
    for y in x:
        out += flat(y)
    return out


class Queues:

    def __init__(self, sems):
        self.q = {e: [] for e in ("pe", "act", "dve", "pool", "sp")}
        self.sems = sems

    def op(self, eng, fn, after=(), sem=None, val=0):
        t = Tok(eng, fn, flat(after), sem, val)
        for a in t.after:
            a.used = True
        self.q[eng].append(t)
        return t

    def now(self):
        return [self.q[e][-1] for e in ("pe", "act", "dve", "pool") if self.q[e]]

    def count(self):
        for e, q in self.q.items():
            n = 0
            for t in q:
                if t.inc == 1 and t.used:
                    n += 1
                    t.sem, t.val = self.sems[e], n

    def emit(self, name, eng):
        seen = {}
        for t in self.q[name]:
            need = {}
            for a in t.after:
                if a.sem.name not in need or need[a.sem.name][1] < a.val:
                    need[a.sem.name] = (a.sem, a.val)
            for k, (s, v) in need.items():
                if seen.get(k, 0) < v:
                    eng.wait_ge(s, v)
                    seen[k] = v
            ins = t.fn(eng)
            if t.used:
                ins.then_inc(t.sem, t.inc)


class Slot:

    def __init__(self, ap):
        self.ap, self.free, self.busy = ap, [], False


class Ring:
    def __init__(self, slots):
        self.slots, self.n = slots, 0

    def get(self):
        s = self.slots[self.n % len(self.slots)]
        self.n += 1
        assert not s.busy, "slot taken before it was given back"
        s.busy = True
        return s


def give(s, *toks):
    s.free, s.busy = flat(toks), False


def weave(*gens):
    live = [g if isinstance(g, tuple) else (g, 1) for g in gens]
    while live:
        for item in list(live):
            for _ in range(item[1]):
                try:
                    next(item[0])
                except StopIteration:
                    live.remove(item)
                    break


def pool_of(jobs, width):
    jobs = list(jobs)
    live = []
    while jobs or live:
        while jobs and len(live) < width:
            live.append(jobs.pop(0))
        for g in list(live):
            try:
                next(g)
            except StopIteration:
                live.remove(g)
            yield


def program(nc, dr):
    ctx = ExitStack()
    with ctx:
        def sb(name, cols, dt=FP):
            return ctx.enter_context(nc.sbuf_tensor(name, [128, cols], dt))

        Q = Queues({e: ctx.enter_context(nc.semaphore("done_" + e)) for e in ("pe", "act", "dve", "pool", "sp")})
        PE, AC, DV, PO, SP = "pe", "act", "dve", "pool", "sp"

        def mm(out, l, r, start, stop, after=(), skip=False):
            return Q.op(PE, lambda e: e.matmul(out, l, r, start=start, stop=stop, skip_group_check=skip), after)

        def tr(out, i, after=()):
            k = i.shape[0]
            return Q.op(PE, lambda e: e.transpose(out, i, ident[0:k, 0:k]), after)

        def tt(out, a, b, op, after=(), eng=DV):
            return Q.op(eng, lambda e: e.tensor_tensor(out, a, b, op), after)

        def ts(out, a, s1, s2, op0, op1=None, after=(), eng=DV):
            if op1 is None:
                return Q.op(eng, lambda e: e.tensor_scalar(out, a, s1, None, op0), after)
            return Q.op(eng, lambda e: e.tensor_scalar(out, a, s1, s2, op0, op1), after)

        def stt(out, a, s, b, op0, op1, after=()):
            return Q.op(DV, lambda e: e.scalar_tensor_tensor(out, a, s, b, op0, op1), after)

        def ttr(out, a, b, op0, op1, init, acc, after=()):
            return Q.op(DV, lambda e: e.tensor_tensor_reduce(out=out, in0=a, in1=b, scale=1.0, scalar=init,
                                                             op0=op0, op1=op1, accum_out=acc), after)

        def red(out, a, op, after=()):
            return Q.op(DV, lambda e: e.tensor_reduce(out, a, AX.X, op), after)

        def vcp(out, a, after=()):
            return Q.op(DV, lambda e: e.tensor_copy(out, a), after)

        def rcp(out, a, after=()):
            return Q.op(DV, lambda e: e.reciprocal(out, a), after)

        def act(out, a, f, after=(), bias=0.0, scale=1.0, acc=None):
            return Q.op(AC, lambda e: e.activation(out, a, f, bias=bias, scale=scale, accum_out=acc), after)

        def acp(out, a, after=(), scale=1.0):
            return act(out, a, ACT.Copy if isinstance(scale, float) else ACT.Identity, after, scale=scale)

        def load(dst, src, after=(), eng=SP):
            s = ctx.enter_context(nc.semaphore(f"ld{len(loads)}"))
            loads.append(s)
            return Q.op(eng, lambda e: e.dma_start(dst, src), after, sem=s, val=16)

        loads = []

        def rf(ap):
            return ap.bitcast(FP)

        cst = sb("cst", NCO)
        lev = sb("lev", 7 * 128, U8)
        sm = sb("sm", NSM)
        st = sb("st", 256)
        post = sb("post", 1024)
        X = sb("X", 2048)
        raw = [sb(f"raw{i}", SLABW) for i in range(NRAW)]
        WH = [sb(f"wh{i}", 1024, FR) for i in range(NUNIT)]
        WL = [sb(f"wl{i}", 1024, FR) for i in range(NUNIT)]
        R1 = sb("R1", 2 * 8 * T1, FR)
        R2 = sb("R2", 4096, FR)
        R3 = sb("R3", 4096, FR)
        NFA = 16384 + 512
        FA = sb("FA", NFA)
        banks = [Slot(ctx.enter_context(nc.psum_tensor(f"pb{i}", [128, 512], FP))) for i in range(8)]

        def C(n):
            return cst[:, CO[n][0]:CO[n][0] + CO[n][1]]

        def S_(n):
            return sm[:, SM[n][0]:SM[n][0] + SM[n][1]]

        def sc(n, i):
            return sm[:, SM[n][0] + i:SM[n][0] + i + 1]

        ident = C("ident")
        ones = C("ones")

        def fa(off, n, p=128):
            assert off + n <= NFA, (off, n)
            return FA[0:p, off:off + n]

        stn = [0]

        def stat(n=1):
            if stn[0] + n > 256:
                stn[0] = 0
            stn[0] += n
            return st[:, stn[0] - n:stn[0]]

        t_x = load(X[:, :].rearrange("p (c d) -> p c d", c=2), dr["x"].rearrange("o (c p) d -> p (o c) d", p=128))
        XM = fa(0, 1024, 16)
        t_xm = load(XM, dr["meta"])
        t_cst = load(cst[:, :], dr["cst"])
        t_sm = load(sm[:, :], dr["sm"])

        NU = 2 * NSLAB
        slab_sem = [ctx.enter_context(nc.semaphore(f"slab{i}")) for i in range(NRAW)]
        slab_tok, split_tok, unit_free = {}, {}, {}

        def load_slab(s):
            if s >= NSLAB:
                return
            after = [split_tok[2 * (s - NRAW)], split_tok[2 * (s - NRAW) + 1]] if s >= NRAW else []
            dst, src = raw[s % NRAW][:, :], dr["w"][s]
            slab_tok[s] = Q.op(SP, lambda e: e.dma_start(dst, src), after,
                               sem=slab_sem[s % NRAW], val=16 * (s // NRAW + 1))

        def split(u):
            if u >= NU:
                return
            s, h = u // 2, u % 2
            r = raw[s % NRAW][:, 1024 * h:1024 * h + 1024]
            hi, lo = WH[u % NUNIT][:, :], WL[u % NUNIT][:, :]
            a = act(hi, r, ACT.Copy, [slab_tok[s], unit_free.get(u - NUNIT)])
            b = tt(lo, r, rf(hi), ALU.subtract, [a])
            split_tok[u] = [a, b]
            if h == 1:
                load_slab(s + NRAW)

        for s in range(NRAW):
            load_slab(s)
        t_lev = load(fa(5120, 896), dr["lev"])
        t_lev = Q.op(PO, lambda e: e.tensor_copy(lev[:, :], fa(5120, 896)), [t_lev])
        cur = [0]

        def take(n=1):
            i = cur[0]
            u, o = i // 8, i % 8
            assert o + n <= 8
            cur[0] += n
            sl = slice(128 * o, 128 * o + 128 * n)
            return WH[u % NUNIT][:, sl], WL[u % NUNIT][:, sl], split_tok[u], (u if o + n == 8 else None)

        def done(u, tok):
            if u is not None:
                unit_free[u] = [tok]
                split(u + NUNIT)

        for u in range(NUNIT):
            split(u)

        def prod3(out, lh, ll, rh, rl, first, last, after, skip=False):
            mm(out, lh, rh, first, False, after, skip)
            mm(out, lh, rl, False, False, (), skip)
            return mm(out, ll, rh, False, last, (), skip)

        def gemm_a(ntiles, kt, act_h, act_l, T, ready, evac, ring):
            for n in range(ntiles):
                bk = ring.get()
                for k in range(kt):
                    wh, wl, wt, end = take()
                    t = prod3(bk.ap[:, 0:T], wh, wl, act_h(k), act_l(k), k == 0, k == kt - 1,
                              [wt, bk.free if k == 0 else None, ready(k)])
                    done(end, t)
                evac(n, bk, t)
                yield

        def rstd(ssq, dim, after, p=128, n=1):
            v = stat(n)[0:p]
            r = stat(n)[0:p]
            a = ts(v, ssq, 1.0 / dim, EPS, ALU.mult, ALU.add, after)
            a = act(v, v, ACT.Sqrt, [a])
            return r, rcp(r, v, [a])

        def split_act(val, h, l, after, scale=1.0):
            a = acp(h, val, after, scale)
            if isinstance(scale, float):
                b = tt(l, val, rf(h), ALU.subtract, [a])
            else:
                b = stt(l, val, scale, rf(h), ALU.mult, ALU.subtract, [a])
            return a, b

        def prenorm(tiles, gain, UH, UL, T, xn, xn_free, ring):
            nt = []
            for (x, c0, p, rdy), y in zip(tiles, xn):
                ss = stat()[0:p]
                a = act(y, x, ACT.Square, [rdy, xn_free], acc=ss)
                r, b = rstd(ss, D, [a], p)
                nt.append(ts(y, x, r, None, ALU.mult, None, [b]))
            out = []
            for k in range(8):
                bk = ring.get()
                for i, ((x, c0, p, rdy), y) in enumerate(zip(tiles, xn)):
                    t = tr(bk.ap[:, c0:c0 + p], y[:, 128 * k:128 * k + 128], [nt, bk.free if i == 0 else None])
                a, b = split_act(bk.ap[:, 0:T], UH(k), UL(k), [t, t_sm], sc(gain, k))
                give(bk, b)
                out.append([a, b])
            return out

        def postnorm(acc, t_acc, gtok, xready):
            res = []
            for c in range(2):
                s2 = stat(2)
                sc_ = fa(0, 512) if c == 0 else fa(512, 512)
                a0 = act(sc_, acc[c][0].ap[:, :], ACT.Square, t_acc, acc=s2[:, 0:1])
                a1 = act(sc_, acc[c][1].ap[:, :], ACT.Square, [t_acc, a0], acc=s2[:, 1:2])
                s1 = stat()
                b = tt(s1, s2[:, 0:1], s2[:, 1:2], ALU.add, [a0, a1])
                r, b = rstd(s1, D, [b])
                for h in range(2):
                    bk = acc[c][h]
                    b1 = stt(bk.ap[:, :], bk.ap[:, :], r, post[:, 512 * h:512 * h + 512], ALU.mult, ALU.mult,
                             [b, gtok, a1])
                    xs = X[:, 1024 * c + 512 * h:1024 * c + 512 * h + 512]
                    b2 = tt(xs, bk.ap[:, :], xs, ALU.add, [b1, xready])
                    give(bk, b2)
                res.append(b2)
            return res

        ringA = Ring(banks)
        UH1 = R1[:, 0:8 * T1].rearrange("p (k t) -> p k t", k=8)
        UL1 = R1[:, 8 * T1:16 * T1].rearrange("p (k t) -> p k t", k=8)
        x0, x1 = X[:, 0:1024], X[:, 1024:2048]
        xn = [fa(1024, 1024, 16), fa(2048, 1024), fa(3072, 1024)]
        t_u = prenorm([(XM, 0, 16, t_xm), (x0, 16, 128, t_x), (x1, 144, 128, [t_x, t_cst])], "mix_pre",
                      lambda k: UH1[:, k, :], lambda k: UL1[:, k, :], T1, xn, None, ringA)
        u_done = t_u

        o = 0
        Fr = fa(o, 2048).rearrange("p (h t) -> p h t", h=8); oF = o; o += 2048
        Kr = fa(o, 2048).rearrange("p (h t) -> p h t", h=8); oK = o; o += 2048
        Qr = fa(o, 2048).rearrange("p (h t) -> p h t", h=8); oQ = o; o += 2048
        SG = fa(o, 2048).rearrange("p (h t) -> p h t", h=8); o += 2048
        Vt = fa(o, 2048).rearrange("p (c n) -> p c n", c=2); oV = o; o += 2048
        AT = fa(o, 2048).rearrange("p (x t) -> p x t", x=16); oA = o; o += 2048
        Vm = fa(o, 1024, 16); o += 1024
        KT = fa(o, 1024); KmT = fa(o, 1024, 16); o += 1024
        Fm = fa(o, 128).rearrange("p (h t) -> p h t", h=8); o += 128
        Km = fa(o, 128).rearrange("p (h t) -> p h t", h=8); o += 128
        Tt = [None] + [fa(o + 2048 - (4096 >> j), 2048 >> j) for j in range(1, 8)]; o += 2048
        sgr = Ring([Slot(Tt[1][:, i * T1:(i + 1) * T1]) for i in range(3)])
        lbt = fa(o, 24); o += 24
        assert o <= NFA

        mxl, e0, e1 = lbt[:, 0:8], lbt[:, 8:16], lbt[:, 16:24]
        start1 = Q.now()
        a = tt(mxl, S_("lb0"), S_("lb1"), ALU.max, [t_sm])
        a = [tt(e0, S_("lb0"), mxl, ALU.subtract, [a]), tt(e1, S_("lb1"), mxl, ALU.subtract, [a])]
        a = act(lbt[:, 8:24], lbt[:, 8:24], ACT.Exp, a)
        a = tt(e1, e0, e1, ALU.add, [a])
        a = rcp(e1, e1, [a])
        a = tt(e0, e0, e1, ALU.mult, [a])
        t_lb = ts(e1, e0, -1.0, 1.0, ALU.mult, ALU.add, [a])

        tF, tK, tKm, tQ, tG = {}, {}, {}, {}, {}
        first_f = [u_done, Q.now()]

        def ev_f(n, bk, t):
            s = sgr.get()
            a = act(s.ap, bk.ap[:, 0:T1], ACT.Sigmoid, [t, s.free, first_f])
            give(bk, a)
            b1 = ts(Fr[:, n, :], s.ap[:, NM:T1], e1[:, n:n + 1], e0[:, n:n + 1], ALU.mult, ALU.add, [a, t_lb, first_f])
            b2 = ts(Fm[:, n, :], s.ap[:, 0:NM], e1[:, n:n + 1], e0[:, n:n + 1], ALU.mult, ALU.add)
            b3 = ts(Kr[:, n, :], Fr[:, n, :], -1.0, 1.0, ALU.mult, ALU.add, [b1])
            b4 = ts(Km[:, n, :], Fm[:, n, :], -1.0, 1.0, ALU.mult, ALU.add, [b2])
            give(s, b2)
            tF[n], tK[n], tKm[n] = b2, b3, b4

        UHk, ULk = (lambda k: UH1[:, k, :]), (lambda k: UL1[:, k, :])
        UHr, ULr = (lambda k: UH1[:, k, NM:T1]), (lambda k: UL1[:, k, NM:T1])
        ready_u = lambda k: t_u[k]
        for _ in gemm_a(8, 8, UHk, ULk, T1, ready_u, ev_f, ringA):
            pass
        tV = []
        for nh in range(2):
            bk = [ringA.get() for _ in range(3)]
            cols = [(0, 128), (16, 128), (144, 128)]
            for k in range(8):
                wh, wl, wt, end = take(4)
                for i, (c0, m) in enumerate(cols):
                    t = prod3(bk[i].ap[:, :], UH1[:, k, c0:c0 + m], UL1[:, k, c0:c0 + m], wh, wl, k == 0, k == 7,
                              [wt, bk[i].free])
                done(end, t)
            a = acp(Vm[:, 512 * nh:512 * nh + 512], bk[0].ap[0:16, :], [t, first_f])
            give(bk[0], a)
            for c in range(2):
                a = acp(Vt[:, c, 512 * nh:512 * nh + 512], bk[c + 1].ap[:, :], [t, first_f])
                give(bk[c + 1], a)
            tV.append(a)

        def ev_silu(dst, tks):
            def ev(n, bk, t):
                s = sgr.get()
                a = act(s.ap[:, 0:256], bk.ap[:, 0:256], ACT.Sigmoid, [t, s.free])
                b = tt(dst[:, n, :], bk.ap[:, 0:256], s.ap[:, 0:256], ALU.mult, [a])
                give(bk, b)
                give(s, b)
                tks[n] = b
            return ev

        for _ in gemm_a(8, 8, UHr, ULr, 256, ready_u, ev_silu(Qr, tQ), ringA):
            pass

        ringB = Ring([banks[i] for i in (4, 5, 6, 7)])
        ringA = Ring([banks[i] for i in (0, 1, 2)])
        bSSQ = banks[3]
        S1 = fa(oF, 1024)
        S2 = fa(oF + 1024, 1024)
        t_S1, t_S2, t_KT, t_Q7 = {}, {}, {}, {}
        ssq_bank = bSSQ.ap

        def half(ap, j):
            return ap.rearrange("p (b two s) -> p b two s", two=2, s=1 << j)

        def bcast(ap, n):
            p, b = ap.shape
            return ap.rearrange("p (b o) -> p b o", o=1).broadcast_to([p, b, n])

        def meta_part():
            t = [tF[n] for n in range(8)] + [tKm[n] for n in range(8)]
            kf = Km.rearrange("p h t -> p (h t)")
            tot = Fm.rearrange("p h t -> p (h t)")
            for j in range(4):
                v = half(kf, j)
                tv = tot.rearrange("p (b two) -> p b two", two=2)
                w = tt(v[:, :, 0, :], v[:, :, 0, :], tv[:, :, 1:2].broadcast_to([128, v.shape[1], 1 << j]), ALU.mult, t)
                if j < 3:
                    nt = KT[:, 64 * j:64 * j + (64 >> j)]
                    t = [w, tt(nt, tv[:, :, 0], tv[:, :, 1], ALU.mult, t)]
                    tot = nt
                else:
                    t = [w]
                yield
            for g in range(2):
                bk = ringB.get()
                for i in range(4):
                    w = tr(bk.ap[0:16, 128 * i:128 * i + 128], Km[:, 4 * g + i, :], [t, bk.free])
                c = vcp(KmT[:, 512 * g:512 * g + 512], bk.ap[0:16, :], [w])
                give(bk, c)
                yield
                bk = ringB.get()
                for i in range(4):
                    h = 4 * g + i
                    w = mm(bk.ap[:, 128 * i:128 * i + 128], KmT[:, 128 * h:128 * h + 128], Vm[:, 128 * h:128 * h + 128],
                           True, True, [c, bk.free, tV])
                t_S1[g] = (bk, w)
                yield

        def meta_store(g, after):
            bk, w = t_S1[g]
            c = vcp(S1[:, 512 * g:512 * g + 512], bk.ap[:, :], [w, after])
            give(bk, c)
            t_S1[g] = c

        def hgrn_group(g):
            hs = range(4 * g, 4 * g + 4)
            kf = Kr[:, 4 * g:4 * g + 4, :].rearrange("p h t -> p (h t)")
            qf = Qr[:, 4 * g:4 * g + 4, :].rearrange("p h t -> p (h t)")
            ff = Fr[:, 4 * g:4 * g + 4, :].rearrange("p h t -> p (h t)")
            tk, tq = [tK[h] for h in hs], [tQ[h] for h in hs]
            tot, ttot = ff, [tF[h] for h in hs]
            av = AT[:, 8 * g:8 * g + 8, :]
            last = None
            for lv in range(-1, 7):
                cps = []
                for b in range(2):
                    bk = ringB.get()
                    for i in range(4):
                        x = 4 * b + i
                        w = mm(bk.ap[:, 128 * i:128 * i + 128], kf[:, 128 * x:128 * x + 128],
                               qf[:, 128 * x:128 * x + 128], True, True, [tk, tq, bk.free])
                    dst = av[:, 4 * b:4 * b + 4, :]
                    src = bk.ap[:, :].rearrange("p (x t) -> p x t", x=4)
                    if lv < 0:
                        m = ident.rearrange("p (o t) -> p o t", o=1).broadcast_to([128, 4, 128])
                        c = tt(dst, src, m, ALU.mult, [w])
                    else:
                        m = lev[:, 128 * lv:128 * lv + 128].rearrange("p (o t) -> p o t", o=1).broadcast_to([128, 4, 128])
                        dd, mmk, ss = dst, m, src
                        c = Q.op(DV, lambda e, dd=dd, mmk=mmk, ss=ss: e.copy_predicated(dd, mmk, ss), [w, t_lev, last])
                    give(bk, c)
                    cps.append(c)
                yield
                last = cps
                if lv < 0:
                    tq = [tt(qf, qf, ff, ALU.mult, [w, tq, ttot])]
                else:
                    j = lv
                    kv, qv = half(kf, j), half(qf, j)
                    tv = tot.rearrange("p (b two) -> p b two", two=2)
                    nb = kv.shape[1]
                    tk = [tt(kv[:, :, 0, :], kv[:, :, 0, :], tv[:, :, 1:2].broadcast_to([128, nb, 1 << j]), ALU.mult, [w, ttot, tk])]
                    tq = [tt(qv[:, :, 1, :], qv[:, :, 1, :], tv[:, :, 0:1].broadcast_to([128, nb, 1 << j]), ALU.mult, [w, ttot, tq])]
                    nt = Tt[j + 1][:, (1024 >> (j + 1)) * g:(1024 >> (j + 1)) * (g + 1)]
                    ttot = [tt(nt, tv[:, :, 0], tv[:, :, 1], ALU.mult, [ttot])]
                    tot = nt
                    if j == 0:
                        f_dead[g] = [tk, tq, ttot]
                yield
            bk = ringB.get()
            for i in range(4):
                w = tr(bk.ap[:, 128 * i:128 * i + 128], Kr[:, 4 * g + i, 0:128], [tk, bk.free])
            c = acp(KT[:, 512 * g:512 * g + 512], bk.ap[:, :], [w, m_dead])
            give(bk, c)
            k_dead[g] = w
            yield
            bk = ringB.get()
            for i in range(4):
                h = 4 * g + i
                w = mm(bk.ap[:, 128 * i:128 * i + 128], KT[:, 128 * h:128 * h + 128], Vt[:, 0, 128 * h:128 * h + 128],
                       True, True, [c, bk.free])
            s2 = S2[:, 512 * g:512 * g + 512].rearrange("p (h v) -> p h v", h=4)
            s1 = S1[:, 512 * g:512 * g + 512].rearrange("p (h v) -> p h v", h=4)
            tv = tot.rearrange("p (h c) -> p h c", c=2)
            c = tt(s2, s1, tv[:, :, 0:1].broadcast_to([128, 4, 128]), ALU.mult, [ttot, t_S1[g], f_dead[0], f_dead[1]])
            c = tt(s2, s2, bk.ap[:, :].rearrange("p (h v) -> p h v", h=4), ALU.add, [c, w])
            give(bk, c)
            t_S2[g] = c
            t_Q7[g] = [tq, last]
            yield

        f_dead, k_dead = {}, {}
        OT = Kr
        tO, tSq = {}, {}

        def hgrn_out(g):
            for b in range(2):
                bk = ringB.get()
                for i in range(2):
                    h = 4 * g + 2 * b + i
                    for c in range(2):
                        dst = bk.ap[:, 256 * i + 128 * c:256 * i + 128 * c + 128]
                        mm(dst, Vt[:, c, 128 * h:128 * h + 128], AT[:, 2 * h + c, :], True, False, [bk.free, t_Q7[g], tV])
                        S = S1 if c == 0 else S2
                        w = mm(dst, S[:, 128 * h:128 * h + 128], Qr[:, h, 128 * c:128 * c + 128], False, True,
                               [t_S1[g], t_S2[g]])
                h0 = 4 * g + 2 * b
                sq = sqr.get()
                a = act(sq.ap, bk.ap[:, :], ACT.Square, [w, sq.free])
                c = stt(OT[:, h0:h0 + 2, :].rearrange("p h t -> p (h t)"), bk.ap[:, :], sc("hg_g", 0),
                        SG[:, h0:h0 + 2, :].rearrange("p h t -> p (h t)"), ALU.mult, ALU.mult,
                        [a, tG[h0], tG[h0 + 1], k_dead[0], k_dead[1]])
                give(bk, c)
                tO[h0] = c
                for i in range(2):
                    h = h0 + i
                    es = cst[:, CO["esel"][0] + 8 - h:CO["esel"][0] + 16 - h]
                    w = mm(ssq_bank[0:8, 0:256], es, sq.ap[:, 256 * i:256 * i + 256], h == 0, h == 7, [a, bSSQ.free])
                give(sq, w)
                tSq[0] = w
                yield

        g1 = gemm_a(8, 8, UHr, ULr, 256, ready_u, ev_silu(SG, tG), ringA)
        for _ in meta_part():
            next(g1, None)
        m_dead = Q.now()
        for _ in g1:
            pass
        tmark = Q.now()

        def both():
            ga, gb = hgrn_group(0), hgrn_group(1)
            n = 0
            live = [ga, gb]
            stored = False
            while live:
                for x in list(live):
                    try:
                        next(x)
                    except StopIteration:
                        live.remove(x)
                n += 1
                if not stored and 0 in f_dead and 1 in f_dead:
                    meta_store(0, [f_dead[0], f_dead[1]])
                    meta_store(1, [f_dead[0], f_dead[1]])
                    stored = True
                yield

        held = [t_S1[0][0], t_S1[1][0]]
        ringB = Ring([b for b in (banks[4], banks[5], banks[6], banks[7], banks[0], banks[1]) if b not in held][:4])
        CK = post[:, 0:2 * T1]
        CQ = sb("CQ", 512)
        KP = sb("KP", T1)
        tCK, tCQ, tKP = {}, {}, {}

        def ev_c(n, bk, t):
            if n < 2:
                a = acp(CK[:, T1 * n:T1 * n + T1], bk.ap[:, 0:T1], [t])
                give(bk, a)
                tCK[n] = a
            elif n == 2:
                b = tt(KP[:, :], bk.ap[:, 0:T1], C("cos"), ALU.mult, [t])
                give(bk, b)
                tKP[0] = b
            else:
                s = kps.get()
                b = tt(s.ap, bk.ap[:, 0:T1], C("sin"), ALU.mult, [t, s.free])
                give(bk, b)
                b = tt(KP[:, :], KP[:, :], s.ap, ALU.add, [b, tKP[0]])
                give(s, b)
                tKP[0] = b

        kps = Ring([Slot(post[:, 2 * T1:3 * T1])])

        def ev_cq(n, bk, t):
            a = acp(CQ[:, 256 * n:256 * n + 256], bk.ap[:, 0:256], [t])
            give(bk, a)
            tCQ[n] = a

        ringA = Ring([banks[2]])
        ringA2 = Ring([b for b in (banks[0], banks[1], banks[2]) if b not in ringB.slots][:1])

        def lat():
            yield from gemm_a(4, 8, UHk, ULk, T1, ready_u, ev_c, ringA)
            yield from gemm_a(2, 8, UHr, ULr, 256, ready_u, ev_cq, ringA)

        weave((both(), 2), (lat(), 1))
        sqr = Ring([Slot(Tt[1][:, 0:512]), Slot(Tt[1][:, 512:1024])])
        sqr.slots[0].free = sqr.slots[1].free = Q.now()
        for g in range(2):
            for _ in hgrn_out(g):
                pass
        r8 = AT[0:8, 0:2, :].rearrange("p x t -> p (x t)")
        a = ts(r8, ssq_bank[0:8, 0:256], 1.0 / 128, EPS, ALU.mult, ALU.add, [tSq[0]])
        give(bSSQ, a)
        a = act(r8, r8, ACT.Sqrt, [a])
        a = rcp(r8, r8, [a])
        OHh = R2[:, 0:2048].rearrange("p (k t) -> p k t", k=8)
        OHl = R2[:, 2048:4096].rearrange("p (k t) -> p k t", k=8)
        tOH = {}
        for h0 in range(0, 8, 2):
            bk = ringB.get()
            for i in range(2):
                w = mm(bk.ap[:, 256 * i:256 * i + 256], ident[0:8, h0 + i:h0 + i + 1].broadcast_to([8, 128]), r8,
                       True, True, [a, bk.free])
            ov = OT[:, h0:h0 + 2, :].rearrange("p h t -> p (h t)")
            b = tt(ov, ov, bk.ap[:, :], ALU.mult, [w, tO[h0]])
            give(bk, b)
            x = split_act(ov, OHh[:, h0:h0 + 2, :].rearrange("p h t -> p (h t)"),
                          OHl[:, h0:h0 + 2, :].rearrange("p h t -> p (h t)"), [b])
            tOH[h0] = tOH[h0 + 1] = x

        ph = Q.now()
        o = 0
        KN = fa(o, 8 * T1).rearrange("p (h t) -> p h t", h=8); o += 8 * T1
        QN = fa(o, 2048).rearrange("p (h t) -> p h t", h=8); o += 2048
        QP = fa(o, 1024).rearrange("p (h t) -> p h t", h=4); o += 1024
        VM = fa(o, 2048).rearrange("p (c n) -> p c n", c=2); o += 2048
        VMm = fa(o, 1024, 16); o += 1024
        sP = []
        for i in range(3):
            sP.append(Slot((fa(o, 416), fa(o + 416, 384), fa(o + 800, 256, 16)))); o += 1056
        tmp = [Slot(fa(o + i * T1, T1)) for i in range(2)]; o += 2 * T1
        GO = o
        GA = fa(o, 4096).rearrange("p (n t) -> p n t", n=16); o += 4096
        assert o <= NFA, o
        for s in sP + tmp:
            s.free = ph
        ringP = Ring(sP)
        ringT = Ring(tmp)
        ringA = Ring([banks[i] for i in (0, 1, 2, 3)])
        ringB = Ring([banks[i] for i in (4, 5, 6, 7)])

        def latent_norm(src, T, n_t, gain, H, L):
            bk = ringA.get()
            s = ringT.get()
            for n in range(2):
                a = act(s.ap[:, 0:T], src[:, T * n:T * n + T], ACT.Square, [s.free, n_t[n], bk.free])
                w = mm(bk.ap[:, 0:T], ones, s.ap[:, 0:T], n == 0, n == 1, [a, bk.free])
                s.free = [w]
            a = ts(s.ap[:, 0:T], bk.ap[:, 0:T], 1.0 / 256, EPS, ALU.mult, ALU.add, [w])
            give(bk, a)
            a = act(s.ap[:, 0:T], s.ap[:, 0:T], ACT.Sqrt, [a])
            a = rcp(s.ap[:, 0:T], s.ap[:, 0:T], [a])
            res = []
            for n in range(2):
                v = src[:, T * n:T * n + T]
                b = stt(v, v, sc(gain, n), s.ap[:, 0:T], ALU.mult, ALU.mult, [a])
                res.append(split_act(v, H(n), L(n), [b]))
            give(s, b)
            return res

        ckh = R3[:, 0:2 * T1].rearrange("p (k t) -> p k t", k=2)
        ckl = R3[:, 2 * T1:4 * T1].rearrange("p (k t) -> p k t", k=2)
        cqh = R3[:, 1088:1600].rearrange("p (k t) -> p k t", k=2)
        cql = R3[:, 1600:2112].rearrange("p (k t) -> p k t", k=2)
        t_ck = latent_norm(CK, T1, tCK, "kv_g", lambda n: ckh[:, n, :], lambda n: ckl[:, n, :])
        t_cq = latent_norm(CQ, 256, tCQ, "q_g", lambda n: cqh[:, n, :], lambda n: cql[:, n, :])
        tKN, tQN, tQP = {}, {}, {}

        def ev_copy(dst, T, tks, first):
            def ev(n, bk, t):
                a = acp(dst[:, n, :], bk.ap[:, 0:T], [t, first])
                give(bk, a)
                tks[n] = a
            return ev

        for _ in gemm_a(8, 2, lambda k: ckh[:, k, :], lambda k: ckl[:, k, :], T1, lambda k: t_ck[k],
                        ev_copy(KN, T1, tKN, ph), ringA):
            pass
        bks = [ringA.get() for _ in range(4)] + [ringB.get() for _ in range(2)]
        for k in range(2):
            for nh in range(2):
                wh, wl, wt, end = take(4)
                for i, c0 in enumerate((0, 16, 144)):
                    bk = bks[3 * nh + i]
                    t = prod3(bk.ap[:, :], ckh[:, k, c0:c0 + 128], ckl[:, k, c0:c0 + 128], wh, wl, k == 0, k == 1,
                              [wt, bk.free, t_ck])
                done(end, t)
        for nh in range(2):
            a = acp(VMm[:, 512 * nh:512 * nh + 512], bks[3 * nh].ap[0:16, :], [t, ph])
            give(bks[3 * nh], a)
            for c in range(2):
                a = acp(VM[:, c, 512 * nh:512 * nh + 512], bks[3 * nh + c + 1].ap[:, :], [t, ph])
                give(bks[3 * nh + c + 1], a)
        tVM = a
        for _ in gemm_a(8, 2, lambda k: cqh[:, k, :], lambda k: cql[:, k, :], 256, lambda k: t_cq[k],
                        ev_copy(QN, 256, tQN, ph), ringA):
            pass

        def ev_rope(n, bk, t):
            i = n // 2
            if n % 2 == 0:
                b = tt(QP[:, i, :], bk.ap[:, 0:256], C("cos")[:, NM:T1], ALU.mult, [t, ph])
                give(bk, b)
                tQP[i] = b
            else:
                s = ringT.get()
                b = tt(s.ap[:, 0:256], bk.ap[:, 0:256], C("sin")[:, NM:T1], ALU.mult, [t, s.free])
                give(bk, b)
                b = tt(QP[:, i, :], QP[:, i, :], s.ap[:, 0:256], ALU.add, [b, tQP[i]])
                give(s, b)
                tQP[i] = b

        for _ in gemm_a(8, 2, lambda k: cqh[:, k, :], lambda k: cql[:, k, :], 256, lambda k: t_cq[k], ev_rope, ringA):
            pass
        c_dead = Q.now()
        OMh = R3[:, 0:2048].rearrange("p (k t) -> p k t", k=8)
        OMl = R3[:, 2048:4096].rearrange("p (k t) -> p k t", k=8)
        tOM = {}

        def softmax_rows(psum, nk, bias, S, scale, after, fscale=None):
            mx, nm_, sm_, ri = stat(), stat(), stat(), stat()
            b = ttr(S, psum, bias, ALU.add, ALU.max, 2 * NEG, mx, after)
            b2 = ts(nm_, mx, -scale, None, ALU.mult, None, [b])
            a = act(S, S, ACT.Exp, [b2], bias=nm_, scale=scale, acc=sm_)
            return b, a, sm_, ri

        MS = float(192 ** -0.5)

        def mla_head(h):
            sl = ringP.get()
            S, PT, PTm = sl.ap
            base = 64 * (h % 2)
            w_ = (144, 272)
            off = (0, 144)
            tp = []
            for c in range(2):
                bk = ringB.get()
                nk = w_[c]
                mm(bk.ap[:, 0:nk], QN[:, h, 128 * c:128 * c + 128], KN[:, h, 0:nk], True, False,
                   [bk.free, tKN[h], tQN[h]])
                w = mm(bk.ap[:, 0:nk], QP[base:base + 64, h // 2, 128 * c:128 * c + 128], KP[base:base + 64, 0:nk],
                       False, True, [tKP[0], tQP[h // 2]])
                Sc = S[:, off[c]:off[c] + nk]
                b, a, sm_, ri = softmax_rows(bk.ap[:, 0:nk], nk, C("m0") if c == 0 else C("m1"), Sc, MS, [w, sl.free])
                give(bk, b)
                yield
                b = rcp(ri, sm_, [a])
                tp.append(ts(Sc, Sc, ri, None, ALU.mult, None, [b]))
            bk, bm = ringB.get(), ringB.get()
            tr(bk.ap[:, 0:128], S[:, 16:144], [tp[0], bk.free])
            tr(bm.ap[0:16, 0:128], S[:, 0:16], [bm.free])
            yield
            tr(bk.ap[:, 128:256], S[:, 160:288], [tp[1]])
            tr(bk.ap[:, 256:384], S[:, 288:416])
            w = tr(bm.ap[0:16, 128:256], S[:, 144:160])
            a1 = acp(PT, bk.ap[:, 0:384], [w])
            a2 = vcp(PTm, bm.ap[0:16, 0:256], [w])
            give(bk, a1)
            give(bm, a2)
            yield
            bk = ringB.get()
            vh = slice(128 * h, 128 * h + 128)
            mm(bk.ap[:, 0:256], VM[:, 0, vh], PT[:, 0:256], True, False, [a1, a2, bk.free, tVM])
            mm(bk.ap[:, 0:256], VMm[:, vh], PTm, False, False)
            w = mm(bk.ap[:, 128:256], VM[:, 1, vh], PT[:, 256:384], False, True)
            x = split_act(bk.ap[:, 0:256], OMh[:, h, :], OMl[:, h, :], [w, c_dead])
            give(bk, x)
            give(sl, w)
            tOM[h] = x
            yield

        tGate = {}

        def ev_gate(n, bk, t):
            a = act(GA[:, n, :], bk.ap[:, 0:256], ACT.Sigmoid, [t, ph], bias=sc("b_gate", n))
            give(bk, a)
            tGate[n] = a

        weave((pool_of([mla_head(h) for h in range(8)], 2), 2),
              (gemm_a(16, 8, UHr, ULr, 256, ready_u, ev_gate, ringA), 1))
        ga_dead = Q.now()
        MXh = R1[:, 0:2048].rearrange("p (k t) -> p k t", k=8)
        MXl = R1[:, 2048:4096].rearrange("p (k t) -> p k t", k=8)
        tYa, tMX = {}, {}

        def ev_ya(n, bk, t):
            b = tt(GA[:, n, :], GA[:, n, :], bk.ap[:, 0:256], ALU.mult, [t, tGate[n]])
            give(bk, b)
            tYa[n] = b

        def ev_yb(n, bk, t):
            g = GA[:, 8 + n, :]
            b = tt(g, g, bk.ap[:, 0:256], ALU.mult, [t, tGate[8 + n]])
            give(bk, b)
            b = tt(g, g, GA[:, n, :], ALU.add, [b, tYa[n]])
            tMX[n] = split_act(g, MXh[:, n, :], MXl[:, n, :], [b, ga_dead])

        for _ in gemm_a(8, 8, lambda k: OHh[:, k, :], lambda k: OHl[:, k, :], 256, lambda k: tOH[k], ev_ya, ringA):
            pass
        for _ in gemm_a(8, 8, lambda k: OMh[:, k, :], lambda k: OMl[:, k, :], 256, lambda k: tOM[k], ev_yb, ringA):
            pass

        def gemm_b(ACC, k, kt, H, L, rdy):
            for h in range(2):
                wh, wl, wt, end = take(4)
                for c in range(2):
                    t = prod3(ACC[c][h].ap[:, :], H[:, 128 * c:128 * c + 128], L[:, 128 * c:128 * c + 128], wh, wl,
                              k == 0, k == kt - 1, [wt, rdy, ACC[c][h].free if k == 0 else None])
                done(end, t)
            return t

        ACC = [[banks[4], banks[5]], [banks[6], banks[7]]]
        ringA = Ring([banks[i] for i in (0, 1, 2, 3)])

        def out_proj(H, L, rdy, gname):
            g = load(post[:, :], dr[gname], [Q.now()])
            for k in range(8):
                t = gemm_b(ACC, k, 8, H[:, k, :], L[:, k, :], rdy(k))
            return postnorm(ACC, [t, Q.now()], g, None)

        t_h = out_proj(MXh, MXl, lambda k: tMX[k], "mix_post")
        U2h = R2[:, 0:2048].rearrange("p (k t) -> p k t", k=8)
        U2l = R2[:, 2048:4096].rearrange("p (k t) -> p k t", k=8)

        def norm2(gain, xr):
            ph = Q.now()
            return prenorm([(x0, 0, 128, xr), (x1, 128, 128, xr)], gain,
                           lambda k: U2h[:, k, :], lambda k: U2l[:, k, :], 256,
                           [fa(1024, 1024), fa(2048, 1024)], ph, ringA)

        t_u2 = norm2("ffn_pre", t_h)

        def ffn(nt, t_u2, hidden, gname):
            g = load(post[:, :], dr[gname], [Q.now()])
            ph = Q.now()
            hid = Ring([Slot((R3[:, 512 * i:512 * i + 256], R3[:, 512 * i + 256:512 * i + 512])) for i in range(8)])
            scr = Ring([Slot((fa(4096 + 512 * i, 256), fa(4096 + 512 * i + 256, 256))) for i in range(4)])
            for s in hid.slots + scr.slots:
                s.free = ph
            made = {}
            for i in range(nt + LAG):
                if i < nt:
                    pair = []
                    gen = gemm_a(2, 8, lambda k: U2h[:, k, :], lambda k: U2l[:, k, :], 256, lambda k: t_u2[k],
                                 lambda n, bk, t: pair.append((bk, t)), ringA)
                    for _ in gen:
                        pass
                    s = scr.get()
                    hs = hid.get()
                    (bg, tg), (bu, tu) = pair
                    b = hidden(i, bg, tg, bu, tu, s)
                    give(s, b)
                    x = split_act(s.ap[1], hs.ap[0], hs.ap[1], [b, hs.free])
                    give(s, x)
                    made[i] = (hs, x)
                if i >= LAG:
                    k = i - LAG
                    hs, x = made[k]
                    t = gemm_b(ACC, k, nt, hs.ap[0], hs.ap[1], [x])
                    give(hs, t)
            return postnorm(ACC, [t, Q.now()], g, None)

        def hidden1(i, bg, tg, bu, tu, s):
            a = act(s.ap[0], bg.ap[:, 0:256], ACT.Silu, [tg, s.free])
            give(bg, a)
            b = tt(s.ap[1], s.ap[0], bu.ap[:, 0:256], ALU.mult, [a, tu])
            give(bu, b)
            return b

        t_x2 = ffn(HID1, t_u2, hidden1, "ffn_post")

        t_u2 = norm2("attn_pre", t_x2)
        ph = Q.now()
        o = 0
        mq = fa(o, 512).rearrange("p (n t) -> p n t", n=2); o += 512
        mk = fa(o, 512).rearrange("p (n t) -> p n t", n=2); o += 512
        TM1 = fa(o, 1024).rearrange("p (c n) -> p c n", c=2); o += 1024
        TM2 = fa(o, 768).rearrange("p (c n) -> p c n", c=2); o += 768
        nkc = fa(o, 256); o += 256
        nq = fa(o, 512).rearrange("p (n t) -> p n t", n=2); o += 512
        nks = fa(o, 256); o += 256
        nkw = fa(o, 256); o += 256
        dqk = fa(o, 1024).rearrange("p (n t) -> p n t", n=4); o += 1024
        sqk = fa(o, 1024).rearrange("p (n t) -> p n t", n=4); o += 1024
        BI = fa(o, 4 * 384 + 0); o += 1536
        BI2 = fa(o, 4 * 384); o += 1536
        win = fa(o, 480).rearrange("p (l n) -> p l n", l=32); o += 480
        hk = fa(o, 30); kcT = fa(o + 32, 15); vc = fa(o + 48, 64, 15); o += 112
        oc = fa(o, 512).rearrange("p (c n) -> p c n", c=2); o += 512
        odn = fa(o, 512).rearrange("p (c n) -> p c n", c=2); o += 512
        Sc_ = fa(o, 120); o += 120
        PcT = fa(o, 1024, 15).rearrange("p (h t) -> p h t", h=4); o += 1024
        gat = fa(o, 24); o += 24
        lamt = fa(o, 80); o += 80
        sl2 = []
        for i in range(4):
            sl2.append(Slot((fa(o, 384), fa(o + 384, 384)))); o += 768
        assert o <= NFA, o
        oX1 = o; o += 1024
        assert o <= NFA, o
        for s in sl2:
            s.free = ph
        ringP = Ring(sl2)
        MIh = R3[:, 0:2048].rearrange("p (k t) -> p k t", k=8)
        MIl = R3[:, 2048:4096].rearrange("p (k t) -> p k t", k=8)
        tk = {}

        def tiles(names):
            def ev(n, bk, t):
                name, dst = names[n]
                a = acp(dst, bk.ap[:, 0:256], [t, ph])
                give(bk, a)
                tk[name] = a
            return gemm_a(len(names), 8, lambda k: U2h[:, k, :], lambda k: U2l[:, k, :], 256, lambda k: t_u2[k], ev, ringA)

        tBI = {}

        def biases(m, dst, base, scale, after):
            r = []
            for h in range(4):
                r.append(ts(dst[:, 384 * h:384 * h + 384], base, SLOPES[m + 4 * h] / scale, None, ALU.mult, None,
                            after, eng=PO))
            tBI[m] = r

        biases(0, BI, C("dmc"), 0.125, ph)
        biases(1, BI2, C("dmc"), 0.125, ph)

        def proj_a():
            yield from tiles([("mq0", mq[:, 0, :]), ("mq1", mq[:, 1, :]), ("mk0", mk[:, 0, :]), ("mk1", mk[:, 1, :])])
            bk = [ringA.get() for _ in range(2)]
            for k in range(8):
                wh, wl, wt, end = take(4)
                for c in range(2):
                    t = prod3(bk[c].ap[:, :], U2h[:, k, 128 * c:128 * c + 128], U2l[:, k, 128 * c:128 * c + 128],
                              wh, wl, k == 0, k == 7, [wt, bk[c].free])
                done(end, t)
            for c in range(2):
                a = acp(TM1[:, c, :], bk[c].ap[:, :], [t])
                give(bk[c], a)
            tk["tm1"] = a
            yield

        def proj_b():
            yield from tiles([("nkc", nkc), ("nq0", nq[:, 0, :]), ("nq1", nq[:, 1, :]), ("nks", nks)])
            bk = [ringA.get() for _ in range(3)]
            for k in range(8):
                wh, wl, wt, end = take(4)
                for c in range(2):
                    prod3(bk[c].ap[:, 0:268], U2h[:, k, 128 * c:128 * c + 128], U2l[:, k, 128 * c:128 * c + 128],
                          wh[:, 0:268], wl[:, 0:268], k == 0, k == 7, [wt, bk[c].free])
                t = prod3(bk[2].ap[:, 0:256], wh[:, 384:512], wl[:, 384:512], U2h[:, k, :], U2l[:, k, :],
                          k == 0, k == 7, [bk[2].free])
                done(end, t)
            for c in range(2):
                a = acp(TM2[:, c, 0:256], bk[c].ap[:, 0:256], [t])
                a = act(gat[:, 12 * c:12 * c + 12], bk[c].ap[:, 256:268], ACT.Sigmoid, [t])
                give(bk[c], a)
            tk["tm2"] = a
            a = acp(nkw, bk[2].ap[:, 0:256], [t])
            give(bk[2], a)
            tk["nkw"] = a
            yield

        def proj_c():
            yield from tiles([(f"d{i}", dqk[:, i, :]) for i in range(4)] + [(f"s{i}", sqk[:, i, :]) for i in range(4)])

        ringB = Ring([banks[i] for i in (4, 5, 6)])
        bPV = Ring([banks[7]])

        def maps(sl, q, k, bias, scale, after, tbias):
            S = sl.ap[0]
            out = []
            for c in range(2):
                nk = 128 + 128 * c
                bk = ringB.get()
                w = mm(bk.ap[:, 0:nk], q[:, 128 * c:128 * c + 128], k[:, 0:nk], True, True, [bk.free, after])
                Sc = S[:, 128 * c:128 * c + nk]
                mx, nm_, sm_ = stat(), stat(), stat()
                b = ttr(Sc, bk.ap[:, 0:nk], bias[:, 128 * c:128 * c + nk], ALU.add, ALU.max, 2 * NEG, mx,
                        [w, sl.free, tbias])
                give(bk, b)
                out.append((Sc, mx, nm_, sm_, b))
            return out

        def transp(sl, tp):
            S, PT = sl.ap
            bk = ringB.get()
            tr(bk.ap[:, 0:128], S[:, 0:128], [tp, bk.free])
            tr(bk.ap[:, 128:256], S[:, 128:256])
            w = tr(bk.ap[:, 256:384], S[:, 256:384])
            a = acp(PT, bk.ap[:, 0:384], [w])
            give(bk, a)
            return a

        def plain_exp(m, scale):
            r = []
            for (Sc, mx, nm_, sm_, b) in m:
                b = ts(nm_, mx, -scale, None, ALU.mult, None, [b])
                r.append(act(Sc, Sc, ACT.Exp, [b], bias=nm_, scale=scale, acc=sm_))
            return r

        pv_state = {}

        def pv(sl, a, V, h, kt, first, last, extra=None):
            PT = sl.ap[1]
            key = kt
            if key not in pv_state:
                pv_state[key] = [bPV.get(), []]
            bk, ws = pv_state[key]
            base = 64 * (h % 2)
            out = bk.ap[base:base + 64, 0:256]
            mm(out, V[0], PT[:, 0:256], first, False, [a, bk.free])
            w = mm(bk.ap[base:base + 64, 128:256], V[1], PT[:, 256:384], False, last)
            give(sl, w)
            return w

        def pv_end(kt, w, parity, tks):
            bk, ws = pv_state[kt]
            ws.append(w)
            if len(ws) == 2:
                x = split_act(bk.ap[:, 0:256], MIh[:, kt, :], MIl[:, kt, :], [ws, mi_free])
                give(bk, x)
                tks[kt] = x

        tMI = {}
        mi_free = ph

        def moba_head(h):
            sl = ringP.get()
            b0 = 64 * (h % 2)
            m = maps(sl, mq[b0:b0 + 64, h // 2, :], mk[b0:b0 + 64, h // 2, :], BI[:, 384 * h:384 * h + 384], 0.125,
                     [tk[f"mq{h // 2}"], tk[f"mk{h // 2}"]], tBI[0])
            yield
            e = plain_exp(m, 0.125)
            yield
            tp = []
            for (Sc, mx, nm_, sm_, b), a in zip(m, e):
                ri = stat()
                b = rcp(ri, sm_, [a])
                tp.append(ts(Sc, Sc, ri, None, ALU.mult, None, [b]))
            yield
            a = transp(sl, tp)
            yield
            V = [TM1[:, c, 64 * h:64 * h + 64] for c in range(2)]
            w = pv(sl, [a, tk["tm1"]], V, h, h // 2, True, True)
            pv_end(h // 2, w, h % 2, tMI)
            yield

        def swa_head(h):
            sl = ringP.get()
            b0 = 64 * (h % 2)
            m = maps(sl, sqk[b0:b0 + 64, h // 2, :], sqk[b0:b0 + 64, 2 + h // 2, :], BI2[:, 384 * h:384 * h + 384],
                     0.125, [tk[f"s{h // 2}"], tk[f"s{2 + h // 2}"]], tBI[3])
            yield
            tp = []
            sk = sc("sinks", h)
            ex = []
            for (Sc, mx, nm_, sm_, b) in m:
                b = ts(mx, mx, 0.125, None, ALU.mult, None, [b])
                b = tt(mx, mx, sk, ALU.max, [b])
                b = ts(nm_, mx, -1.0, None, ALU.mult, None, [b])
                a = act(Sc, Sc, ACT.Exp, [b], bias=nm_, scale=0.125, acc=sm_)
                es = stat()
                a2 = act(es, sk, ACT.Exp, [b], bias=nm_, scale=1.0)
                ex.append((a, a2, es))
            yield
            for (Sc, mx, nm_, sm_, b), (a, a2, es) in zip(m, ex):
                ri = stat()
                b = tt(es, es, sm_, ALU.add, [a, a2])
                b = rcp(ri, es, [b])
                tp.append(ts(Sc, Sc, ri, None, ALU.mult, None, [b]))
            yield
            a = transp(sl, tp)
            yield
            g = h // 2
            V = [TM2[:, c, 128 + 64 * g:128 + 64 * g + 64] for c in range(2)]
            w = pv(sl, [a, tk["tm2"]], V, h, 6 + h // 2, True, True)
            pv_end(6 + h // 2, w, h % 2, tMI)
            yield

        def nsa_maps(h, k, kname, gi, voff, first, last):
            sl = ringP.get()
            b0 = 64 * (h % 2)
            m = maps(sl, nq[b0:b0 + 64, h // 2, :], k[b0:b0 + 64, :], BI2[:, 384 * h:384 * h + 384], 0.125,
                     [tk[f"nq{h // 2}"], tk[kname]], tBI[1])
            yield
            e = plain_exp(m, 0.125)
            yield
            tp = []
            for c, ((Sc, mx, nm_, sm_, b), a) in enumerate(zip(m, e)):
                ri = stat()
                b = rcp(ri, sm_, [a])
                b = tt(ri, ri, gat[:, 12 * c + 3 * h + gi:12 * c + 3 * h + gi + 1], ALU.mult, [b, tk["tm2"]])
                tp.append(ts(Sc, Sc, ri, None, ALU.mult, None, [b]))
            yield
            a = transp(sl, tp)
            yield
            V = [TM2[:, c, voff:voff + 64] for c in range(2)]
            w = pv(sl, [a, tk["tm2"]], V, h, 2 + h // 2, first, last)
            return w

        def nsa_head(h):
            yield from nsa_maps(h, nks, "nks", 1, 0, True, False)
            yield
            w = yield from nsa_maps(h, nkw, "nkw", 2, 64, False, False)
            bk, ws = pv_state[2 + h // 2]
            base = 64 * (h % 2)
            w = mm(bk.ap[base:base + 64, 0:256], vc, PcT[:, h, :], False, True, [tk["pct"]])
            pv_end(2 + h // 2, w, h % 2, tMI)
            yield

        def nsa_cmp():
            pos = S_("cmp_pos")
            nv = nkc.rearrange("p (n l) -> p l n", l=16)
            ws = []
            for i in range(2):
                ws.append(tt(win[:, 16 * i:16 * i + 16, :], nv[:, :, i:i + 15],
                             pos[:, 16 * i:16 * i + 16].rearrange("p (l o) -> p l o", o=1).broadcast_to([128, 16, 15]),
                             ALU.add, [tk["nkc"], ph]))
            yield
            bk = [ringB.get(), ringB.get()]
            for q in range(4):
                c = load_w1(q)
                for half_ in range(2):
                    p0 = 64 * half_
                    for l8 in range(8):
                        l = 8 * q + l8
                        t = mm(bk[half_].ap[:, 0:15], w1b[q % 2][p0:p0 + 64, 128 * l8:128 * l8 + 128],
                               win[p0:p0 + 64, l, :], l == 0, l == 31, [c, ws, bk[half_].free])
                w1_free[q] = [t]
                yield
            for i in range(2):
                a = act(hk[:, 15 * i:15 * i + 15], bk[i].ap[:, 0:15], ACT.Gelu_apprx_tanh, [t, ph],
                        bias=sc("cmp_b1", i))
                give(bk[i], a)
            yield
            bk = ringB.get()
            w = mm(bk.ap[:, 0:15], S_("w2k"), hk[:, 0:15], True, True, [a, bk.free])
            w = mm(bk.ap[0:15, 64:128], hk[:, 15:30], S_("w2v"), True, True)
            a = acp(kcT, bk.ap[:, 0:15], [w, ph])
            a = acp(vc, bk.ap[0:15, 64:128], [w, ph])
            give(bk, a)
            yield
            sv = Sc_.rearrange("p (c h n) -> p c h n", c=2, h=4)
            cb = C("cmpb").rearrange("p (c h n) -> p c h n", c=2, h=4)
            sf = Sc_.rearrange("p (x n) -> p x n", n=15)
            mx, s8 = stat(8), stat(8)
            bs = []
            for par in range(2):
                bk = ringB.get()
                for c in range(2):
                    for hp in range(2):
                        x = 2 * c + hp
                        w = mm(bk.ap[:, 16 * x:16 * x + 15],
                               nq[64 * par:64 * par + 64, hp, 128 * c:128 * c + 128],
                               kcT[64 * par:64 * par + 64, :], True, True, [a, bk.free, tk["nq0"], tk["nq1"]])
                pv_ = bk.ap[:, 0:64].rearrange("p (x n) -> p x n", n=16)[:, :, 0:15]
                bs.append(tt(sf[:, par:8:2, :], pv_, C("cmpb").rearrange("p (x n) -> p x n", n=15)[:, par:8:2, :],
                             ALU.add, [w, ph]))
                give(bk, bs[-1])
            b = bs
            b = red(mx, sf, ALU.max, [b])
            b = ts(mx, mx, -1e20, None, ALU.max, None, [b])
            b = tt(sf, sf, bcast(mx, 15), ALU.subtract, [b])
            a = act(Sc_, Sc_, ACT.Exp, [b], scale=0.125)
            yield
            b = red(s8, sf, ALU.add, [a])
            b = ts(s8, s8, 1e-30, None, ALU.max, None, [b])
            b = rcp(s8, s8, [b])
            gv = gat.rearrange("p (x g) -> p x g", g=3)[:, :, 0]
            b = tt(s8, s8, gv, ALU.mult, [b, tk["tm2"]])
            b = tt(sf, sf, bcast(s8, 15), ALU.mult, [b])
            yield
            for hp in range(2):
                bk = ringB.get()
                for i in range(2):
                    for c in range(2):
                        w = tr(bk.ap[0:15, 256 * i + 128 * c:256 * i + 128 * c + 128], sv[:, c, 2 * hp + i, :], [b, bk.free])
                a = acp(PcT[:, 2 * hp:2 * hp + 2, :].rearrange("p h t -> p (h t)"), bk.ap[0:15, :], [w, ph])
                give(bk, a)
            tk["pct"] = a
            yield

        
        w1b = [post[:, :], fa(oX1, 1024)]
        w1_free = {}
        w1sem = [ctx.enter_context(nc.semaphore(f"w1_{i}")) for i in range(2)]

        def load_w1(q):
            dst, src = w1b[q % 2], dr["w1"][q]
            return Q.op(SP, lambda e: e.dma_start(dst, src), [w1_free.get(q - 2), w1_start],
                        sem=w1sem[q % 2], val=16 * (q // 2 + 1))

        w1_start = Q.now()

        DS = float(32 ** -0.5)

        def lam_part():
            l = S_("lam")
            v = lamt[:, 0:64].rearrange("p (a n) -> p a n", a=2)
            lv = l.rearrange("p (a b n) -> p a b n", a=2, b=2)
            b = tt(v, lv[:, :, 0, :], lv[:, :, 1, :], ALU.mult, [ph])
            b = red(lamt[:, 64:66], v, ALU.add, [b])
            a = act(lamt[:, 66:68], lamt[:, 64:66], ACT.Exp, [b])
            b = tt(lamt[:, 68:69], lamt[:, 67:68], lamt[:, 66:67], ALU.subtract, [a])
            tk["lam"] = ts(lamt[:, 69:70], lamt[:, 68:69], -LINIT, None, ALU.add, None, [b])

        LINIT = 0.8 - 0.6 * 1.0
        nlam = lamt[:, 69:70]
        tD = {}

        def diff_head(h):
            n, b0 = h // 2, 64 * (h % 2)
            sl, sl2_ = ringP.get(), ringP.get()
            aft = [tk[f"d{n}"], tk[f"d{2 + n}"]]
            bias = BI[:, 384 * h:384 * h + 384]
            m1 = maps(sl, dqk[b0:b0 + 32, n, :], dqk[b0:b0 + 32, 2 + n, :], bias, DS, aft, tBI[2])
            yield
            m2 = maps(sl2_, dqk[b0 + 32:b0 + 64, n, :], dqk[b0 + 32:b0 + 64, 2 + n, :], bias, DS, aft, tBI[2])
            e1_ = plain_exp(m1, DS)
            yield
            e2_ = plain_exp(m2, DS)
            yield
            tp = []
            for c in range(2):
                r1, r2 = stat(), stat()
                b = rcp(r1, m1[c][3], [e1_[c]])
                b = ts(m1[c][0], m1[c][0], r1, None, ALU.mult, None, [b])
                b2 = rcp(r2, m2[c][3], [e2_[c]])
                b2 = tt(r2, r2, nlam, ALU.mult, [b2, tk["lam"]])
                tp.append(stt(m1[c][0], m2[c][0], r2, m1[c][0], ALU.mult, ALU.add, [b, b2]))
            give(sl2_, tp)
            yield
            a = transp(sl, tp)
            yield
            bk = ringB.get()
            PT = sl.ap[1]
            V = [TM1[:, c, 256 + 64 * h:256 + 64 * h + 64] for c in range(2)]
            mm(bk.ap[:, 0:64], PT[:, 0:128], V[0], True, True, [a, bk.free, tk["tm1"]])
            mm(bk.ap[:, 64:128], PT[:, 128:256], V[0], True, False)
            w = mm(bk.ap[:, 64:128], PT[:, 256:384], V[1], False, True)
            give(sl, w)
            s2, v2, r2 = stat(2), stat(2), stat(2)
            ys = []
            for c in range(2):
                o_ = odn[:, c, 64 * h:64 * h + 64]
                ys.append(act(o_, bk.ap[:, 64 * c:64 * c + 64], ACT.Square, [w, ph], acc=s2[:, c:c + 1]))
            b = ts(v2, s2, 1.0 / 64, EPS, ALU.mult, ALU.add, ys)
            a = act(v2, v2, ACT.Sqrt, [b])
            b = rcp(r2, v2, [a])
            yield
            for c in range(2):
                o_ = odn[:, c, 64 * h:64 * h + 64]
                b2 = stt(o_, bk.ap[:, 64 * c:64 * c + 64], r2[:, c:c + 1], S_("subln"), ALU.mult, ALU.mult, [b, ys])
            give(bk, b2)
            b2 = ts(odn[:, :, 64 * h:64 * h + 64], odn[:, :, 64 * h:64 * h + 64], 1.0 - LINIT, None, ALU.mult, None, [b2])
            tD[h] = b2
            yield

        for _ in proj_a():
            pass
        tk["ph"] = ph
        lam_part()
        weave((pool_of([moba_head(h) for h in range(4)], 2), 2), (proj_b(), 1))
        moba_dead = Q.now()
        biases(2, BI, C("dmc"), DS, moba_dead)
        weave((nsa_cmp(), 1), (proj_c(), 1))
        for _ in pool_of([nsa_head(h) for h in range(4)], 2):
            pass
        biases(3, BI2, C("dms"), 0.125, Q.now())
        for _ in pool_of([diff_head(h) for h in range(4)], 2):
            pass
        for hp in range(2):
            bk = ringB.get()
            for c in range(2):
                w = tr(bk.ap[:, 128 * c:128 * c + 128], odn[:, c, 128 * hp:128 * hp + 128],
                       [tD[2 * hp], tD[2 * hp + 1], bk.free])
            x = split_act(bk.ap[:, 0:256], MIh[:, 4 + hp, :], MIl[:, 4 + hp, :], [w, mi_free])
            give(bk, x)
            tMI[4 + hp] = x
        for _ in pool_of([swa_head(h) for h in range(4)], 2):
            pass
        t_h = out_proj(MIh, MIl, lambda k: tMI[k], "attn_post")
        t_u2 = norm2("ffn_pre2", t_h)

        cw = S_("conv_w").rearrange("p (i n) -> p i n", i=3)

        def hidden2(i, bg, tg, bu, tu, s):
            g = bg.ap
            c = s.ap[0]
            b = ts(c, g[:, 0:256], cw[:, 2, i:i + 1], sc("conv_b", i), ALU.mult, ALU.add, [tg, s.free])
            b = stt(c[:, 1:256], g[:, 0:255], cw[:, 1, i:i + 1], c[:, 1:256], ALU.mult, ALU.add, [b])
            b = stt(c[:, 2:256], g[:, 0:254], cw[:, 0, i:i + 1], c[:, 2:256], ALU.mult, ALU.add, [b])
            give(bg, b)
            a = act(c, c, ACT.Gelu_apprx_tanh, [b])
            b = tt(s.ap[1], c, bu.ap[:, 0:256], ALU.mult, [a, tu])
            give(bu, b)
            return b

        t_x3 = ffn(HID2, t_u2, hidden2, "ffn_post2")
        s_out = ctx.enter_context(nc.semaphore("s_out"))
        t_out = Q.op(SP, lambda e: e.dma_start(dr["out"].rearrange("o (c p) d -> p (o c) d", p=128),
                                               X[:, :].rearrange("p (c d) -> p c d", c=2)),
                     [t_x3], sem=s_out, val=16)
        assert cur[0] == len(BLOCKS), (cur[0], len(BLOCKS))

        Q.count()
        block = ctx.enter_context(nc.Block())

        @block.sync
        def _(e):
            Q.emit("sp", e)
            e.wait_ge(s_out, 16)

        @block.tensor
        def _(e):
            Q.emit("pe", e)

        @block.scalar
        def _(e):
            Q.emit("act", e)

        @block.vector
        def _(e):
            Q.emit("dve", e)

        @block.gpsimd
        def _(e):
            Q.emit("pool", e)


def kernel(**inputs):
    import concourse.bacc as bacc
    from concourse.bass_utils import run_bass_kernel_spmd as run

    I = {k: np.asarray(v) for k, v in inputs.items()}
    f = np.float32
    mats = {n: I[n][0] for n in ("w_in", "w_hg_o", "w_q_b", "w_kv_b", "w_mla_o", "w_out", "w_ffn_in", "w_ffn_out",
                                 "w_in_2", "w_out_2", "ffn_w_gate_2", "ffn_w_up_2", "ffn_w_down_2")}
    W = np.zeros((NSLAB, 128, SLABW), f)
    for i, (n, r, cols) in enumerate(BLOCKS):
        keep = [c for c in cols if c >= 0]
        W[i // 16, :, 128 * (i % 16):128 * (i % 16) + len(keep)] = mats[n][r:r + 128][:, keep]
    sm = np.zeros((128, NSM), f)

    def put(n, v, p=slice(0, 128)):
        sm[p, SM[n][0]:SM[n][0] + SM[n][1]] = v

    def colv(v, n):
        return np.reshape(v, (n, 128)).T

    put("mix_pre", colv(I["mix_pre_g"], 8))
    put("ffn_pre", colv(I["ffn_pre_g"], 8))
    put("attn_pre", colv(I["attn_pre_norm_2"], 8))
    put("ffn_pre2", colv(I["ffn_pre_norm_2"], 8))
    put("b_gate", colv(I["b_gate"], 16))
    put("lb0", colv(I["lb_logits"][0], 8))
    put("lb1", colv(I["lb_logits"][1], 8))
    put("hg_g", colv(I["hg_norm_g"], 1))
    put("q_g", colv(I["q_a_norm_g"], 2))
    put("kv_g", colv(I["kv_a_norm_g"], 2))
    put("conv_w", np.concatenate([colv(I["ffn_conv_w_2"][0, i], 32) for i in range(3)], 1))
    put("conv_b", colv(I["ffn_conv_b_2"], 32))
    put("cmp_b1", np.stack([I["nsa_cmp_b1_k_2"][0], I["nsa_cmp_b1_v_2"][0]], 1))
    put("cmp_pos", I["nsa_cmp_pos_k_2"][0].T, slice(0, 64))
    put("cmp_pos", I["nsa_cmp_pos_v_2"][0].T, slice(64, 128))
    put("w2k", np.concatenate([I["nsa_cmp_w2_k_2"][0]] * 2, 1))
    put("w2v", I["nsa_cmp_w2_v_2"][0])
    put("subln", I["diff_subln_2"][0][None])
    put("lam", np.concatenate([I[n][0] for n in ("diff_lambda_q1_2", "diff_lambda_k1_2", "diff_lambda_q2_2",
                                                 "diff_lambda_k2_2")])[None])
    put("sinks", I["swa_sinks_2"][0][None])
    w1 = np.zeros((4, 128, 1024), f)
    for q in range(4):
        for half, n in enumerate(("nsa_cmp_w1_k_2", "nsa_cmp_w1_v_2")):
            w1[q, 64 * half:64 * half + 64] = I[n][0][8 * q:8 * q + 8].transpose(1, 0, 2).reshape(64, 1024)
    cst, lev = constants()
    arrays = {"x": I["x"], "meta": I["meta_tokens"], "cst": cst, "lev": lev, "sm": sm, "w": W, "w1": w1}
    for n, k in (("mix_post", "mix_post_g"), ("ffn_post", "ffn_post_g"), ("attn_post", "attn_post_norm_2"),
                 ("ffn_post2", "ffn_post_norm_2")):
        arrays[n] = np.ascontiguousarray(np.broadcast_to(I[k][0][None], (128, D)))
    nc = bacc.Bacc("TRN2", target_bir_lowering=False, num_devices=1)
    dr, sent = {}, {}
    for n, a in arrays.items():
        a = np.ascontiguousarray(a)
        sent["in_" + n] = a
        dr[n] = nc.dram_tensor("in_" + n, a.shape, mybir.dt.from_np(a.dtype), kind="ExternalInput").ap()
    dr["out"] = nc.dram_tensor("out_0", (1, 256, D), FP, kind="ExternalOutput").ap()
    program(nc, dr)
    r = run(nc, [sent], core_ids=[0])
    return r.results[0]["out_0"]
```

```python
import numpy as np
import concourse.bass as bass
from concourse import mybir
from concourse.alu_op_type import AluOpType as ALU
from contextlib import ExitStack

FP = mybir.dt.float32
FR = mybir.dt.float32r
U8 = mybir.dt.uint8
ACT = mybir.ActivationFunctionType
AX = mybir.AxisListType

D = 1024
NM = 16
T1 = 272
HID1 = 22
HID2 = 32
LAG = 3
EPS = 1e-6
NEG = -1e30
NRAW = 3
NUNIT = 4
SLABW = 2048
IN1 = dict(hq=0, hf=1024, hi=2048, hg=3072, cq=4096, ckv=4352, kpe=4608, gate=4672)
_o2 = np.cumsum([0, 256, 256, 256, 256, 64, 64, 64, 64, 64, 64, 12, 256, 256, 256, 256, 128, 128])
IN2 = dict(zip(["mq", "mk", "mv", "nq", "nkc", "nvc", "nks", "nvs", "nkw", "nvw", "ng",
                "dq", "dk", "dv", "sq", "sk", "sv"], [int(v) for v in _o2]))
SLOPES = [float(v) for v in
          np.power(np.float32(2.0), np.arange(1, 17, dtype=np.float32) * np.float32(-0.5))]



def stream_blocks():
    b = []

    def a_tile(name, kt, cols):
        for k in range(kt):
            b.append((name, 128 * k, list(cols)))

    def rng(o, n=128):
        return list(range(o, o + n))

    w = "w_in"
    for n in range(8):
        a_tile(w, 8, rng(IN1["hf"] + 128 * n))
    for nh in range(2):
        for k in range(8):
            for j in range(4):
                b.append((w, 128 * k, rng(IN1["hi"] + 512 * nh + 128 * j)))
    for n in range(8):
        a_tile(w, 8, rng(IN1["hq"] + 128 * n))
    for n in range(8):
        a_tile(w, 8, rng(IN1["hg"] + 128 * n))
    kp = rng(IN1["kpe"], 64)
    sw = kp[32:] + kp[:32]
    for n in range(2):
        a_tile(w, 8, rng(IN1["ckv"] + 128 * n))
    a_tile(w, 8, kp + kp)
    a_tile(w, 8, sw + sw)
    for n in range(2):
        a_tile(w, 8, rng(IN1["cq"] + 128 * n))
    for n in range(8):
        a_tile(w, 8, rng(IN1["gate"] + 128 * n))
    for n in range(8):
        a_tile("w_kv_b", 2, rng(256 * n))
    for nh in range(2):
        for k in range(2):
            for j in range(4):
                b.append(("w_kv_b", 128 * k, rng(256 * (4 * nh + j) + 128)))
    for n in range(8):
        a_tile("w_q_b", 2, rng(192 * n))
    for n in range(4):
        p0 = rng(192 * 2 * n + 128, 64)
        p1 = rng(192 * (2 * n + 1) + 128, 64)
        a_tile("w_q_b", 2, p0 + p1)
        a_tile("w_q_b", 2, p0[32:] + p0[:32] + p1[32:] + p1[:32])
    for n in range(8, 16):
        a_tile(w, 8, rng(IN1["gate"] + 128 * n))
    for n in range(8):
        a_tile("w_hg_o", 8, rng(128 * n))
    for n in range(8):
        a_tile("w_mla_o", 8, rng(128 * n))
    for k in range(8):
        for j in range(8):
            b.append(("w_out", 128 * k, rng(128 * j)))

    def ffn(first, up_name, up_off, down, nt):
        for i in range(nt + LAG):
            if i < nt:
                a_tile(first, 8, rng(128 * i))
                a_tile(up_name, 8, rng(up_off + 128 * i))
            if i >= LAG:
                for j in range(8):
                    b.append((down, 128 * (i - LAG), rng(128 * j)))

    ffn("w_ffn_in", "w_ffn_in", 128 * HID1, "w_ffn_out", HID1)
    w = "w_in_2"
    o = IN2
    for n in range(2):
        a_tile(w, 8, rng(o["mq"] + 128 * n))
    for n in range(2):
        a_tile(w, 8, rng(o["mk"] + 128 * n))
    for k in range(8):
        for c in (o["mv"], o["mv"] + 128, o["dv"], o["dv"] + 128):
            b.append((w, 128 * k, rng(c)))
    a_tile(w, 8, rng(o["nkc"]))
    for n in range(2):
        a_tile(w, 8, rng(o["nq"] + 128 * n))
    a_tile(w, 8, rng(o["nks"], 64) * 2)
    for k in range(8):
        b.append((w, 128 * k, rng(o["nvs"], 64) + rng(o["nvw"], 64)))
        b.append((w, 128 * k, rng(o["sv"])))
        b.append((w, 128 * k, rng(o["ng"], 12) + [-1] * 116))
        b.append((w, 128 * k, rng(o["nkw"], 64) * 2))
    for c in (o["dq"], o["dq"] + 128, o["dk"], o["dk"] + 128, o["sq"], o["sq"] + 128):
        a_tile(w, 8, rng(c))
    for g in range(2):
        a_tile(w, 8, rng(o["sk"] + 64 * g, 64) * 2)
    for k in range(8):
        for j in range(8):
            b.append(("w_out_2", 128 * k, rng(128 * j)))
    ffn("ffn_w_gate_2", "ffn_w_up_2", 0, "ffn_w_down_2", HID2)
    return b


BLOCKS = stream_blocks()
NSLAB = -(-len(BLOCKS) // 16)

SM = {}
_at = 0
for _n, _w in [("mix_pre", 8), ("ffn_pre", 8), ("attn_pre", 8), ("ffn_pre2", 8), ("b_gate", 16),
               ("lb0", 8), ("lb1", 8), ("hg_g", 1), ("q_g", 2), ("kv_g", 2), ("conv_w", 96),
               ("conv_b", 32), ("cmp_b1", 2), ("cmp_pos", 32), ("w2k", 128), ("w2v", 64),
               ("subln", 64), ("lam", 128), ("sinks", 4)]:
    SM[_n] = (_at, _w)
    _at += _w
NSM = _at

CO = {}
_at = 0
for _n, _w in [("ident", 128), ("ones", 128), ("esel", 16), ("cos", T1), ("sin", T1),
               ("m1", T1), ("dmc", 256), ("dms", 256), ("cmpb", 120)]:
    CO[_n] = (_at, _w)
    _at += _w
NCO = _at


def constants():
    c = np.zeros((128, NCO), np.float32)

    def put(n, v):
        c[:, CO[n][0]:CO[n][0] + CO[n][1]] = v

    p = np.arange(128)
    put("ident", np.eye(128))
    put("ones", 1.0)
    e = np.zeros((128, 16))
    e[:, 8] = 1.0
    put("esel", e)
    inv = (np.float32(1.0) / (np.float32(10000.0) ** (np.arange(0, 64, 2, dtype=np.float32) / np.float32(64))))
    ang = (np.arange(T1, dtype=np.float32)[:, None] * inv[None, :].astype(np.float32)).astype(np.float32)
    cs, sn = np.cos(ang).astype(np.float32), np.sin(ang).astype(np.float32)
    put("cos", cs.T[p % 32])
    put("sin", sn.T[p % 32] * np.where((p % 64) < 32, -1.0, 1.0)[:, None])
    q = p[:, None] + NM
    put("m1", np.where(np.arange(T1)[None] <= q + 128, 0.0, NEG))
    d = p[:, None] + 128 - np.arange(256)[None]
    put("dmc", np.where(d >= 0, -d, NEG))
    put("dms", np.where((d >= 0) & (d < 128), -d, NEG))
    cb = np.zeros((128, 2, 4, 15))
    end = np.arange(15) * 16 + 31
    for t in range(2):
        for h in range(4):
            dist = (p[:, None] + 128 * t) - end[None]
            cb[:, t, h] = np.where(dist >= 0, -SLOPES[1 + 4 * h] * dist * 8.0, NEG)
    put("cmpb", cb.reshape(128, 120))
    lev = np.zeros((128, 5, 64), np.float32)
    s, t = p[:, None], p[None]
    for j in range(5):
        m = ((s >> (j + 1)) == (t >> (j + 1))) & (((s >> j) & 1) == 0)
        lev[:, j] = m[:, ((p >> j) & 1) == 1]
    return c, lev.reshape(128, 320)


class Tok:

    def __init__(self, eng, fn, after, sem=None, val=0):
        self.eng, self.fn, self.after = eng, fn, after
        self.sem, self.val, self.used, self.inc = sem, val, sem is not None, 16 if sem is not None else 1
        self.end = 0.0


def flat(x):
    if x is None:
        return []
    if isinstance(x, Tok):
        return [x]
    out = []
    for y in x:
        out += flat(y)
    return out


class Queues:

    def __init__(self, sems):
        self.q = {e: [] for e in ("pe", "act", "dve", "pool", "sp")}
        self.sems = sems
        self.clock = {e: 0.0 for e in ("pe", "act", "dve", "pool", "sp", "dma")}
        self.step_end = 0.0
        self.gate = {}

    def when(self, eng, after, cost):
        return max([self.clock[eng]] + [a.end + 80.0 for a in flat(after)]) + cost

    def op(self, eng, fn, after=(), sem=None, val=0, cost=0.0):
        t = Tok(eng, fn, flat(after) + ([self.gate.pop(eng)] if eng in self.gate else []), sem, val)
        if sem is None:
            t.end = self.clock[eng] = self.when(eng, t.after, cost)
        else:
            first = self.when("sp", t.after, 60.0)
            self.clock["dma"] = max(self.clock["dma"], first) + cost
            t.end = self.clock["dma"] + 1500.0
        self.step_end = max(self.step_end, t.end)
        for a in t.after:
            a.used = True
        self.q[eng].append(t)
        return t

    def now(self):
        return [self.q[e][-1] for e in ("pe", "act", "dve", "pool") if self.q[e]]

    def count(self):
        for e, q in self.q.items():
            n = 0
            for t in q:
                if t.inc == 1 and t.used:
                    n += 1
                    t.sem, t.val = self.sems[e], n

    def emit(self, name, eng):
        seen = {}
        for t in self.q[name]:
            need = {}
            for a in t.after:
                if a.sem.name not in need or need[a.sem.name][1] < a.val:
                    need[a.sem.name] = (a.sem, a.val)
            for k, (s, v) in need.items():
                if seen.get(k, 0) < v:
                    eng.wait_ge(s, v)
                    seen[k] = v
            ins = t.fn(eng)
            if t.used:
                ins.then_inc(t.sem, t.inc)


class Slot:

    def __init__(self, ap):
        self.ap, self.free, self.busy = ap, [], False


class Ring:
    def __init__(self, slots):
        self.slots, self.n = slots, 0

    def idle(self):
        return sum(not s.busy for s in self.slots)

    def get(self):
        idle = [s for s in self.slots if not s.busy]
        assert idle, "every slot is taken"
        s = min(idle, key=lambda x: (max([t.end for t in x.free], default=0.0), self.slots.index(x)))
        s.busy = True
        return s


def give(s, *toks):
    s.free, s.busy = flat(toks), False


def weave(*gens):
    live = [g if isinstance(g, tuple) else (g, 1) for g in gens]
    while live:
        for item in list(live):
            for _ in range(item[1]):
                try:
                    next(item[0])
                except StopIteration:
                    live.remove(item)
                    break


def blend(Q, jobs, width, fill=()):
    jobs, fill = list(jobs), list(fill)
    live = []
    while jobs or live or fill:
        while jobs and len(live) < width:
            live.append([0.0, jobs.pop(0)])
        if live:
            live.sort(key=lambda x: x[0])
            if fill and live[0][0] > Q.clock["pe"] + 100.0:
                g = fill[0]
                try:
                    next(g)
                except StopIteration:
                    fill.pop(0)
                continue
            item = live[0]
            Q.step_end = 0.0
            try:
                next(item[1])
                item[0] = max(Q.step_end, item[0] + 1.0)
            except StopIteration:
                live.remove(item)
        elif fill:
            try:
                next(fill[0])
            except StopIteration:
                fill.pop(0)


def program(nc, dr):
    ctx = ExitStack()
    with ctx:
        def sb(name, cols, dt=FP):
            return ctx.enter_context(nc.sbuf_tensor(name, [128, cols], dt))

        Q = Queues({e: ctx.enter_context(nc.semaphore("done_" + e)) for e in ("pe", "act", "dve", "pool", "sp")})
        PE, AC, DV, PO, SP = "pe", "act", "dve", "pool", "sp"

        def size(ap):
            n = 1
            for v in ap.shape[1:]:
                n *= v
            return n

        def mm(out, l, r, start, stop, after=(), skip=False):
            c = size(r) / 2.4 * (1 if l.dtype == FR else 4)
            return Q.op(PE, lambda e: e.matmul(out, l, r, start=start, stop=stop, skip_group_check=skip), after, cost=c)

        def tr(out, i, after=()):
            k = i.shape[0]
            return Q.op(PE, lambda e: e.transpose(out, i, ident[0:k, 0:k]), [after, t_id], cost=54.0)

        def dcost(out, eng=DV, rate=1.04):
            return 90.0 + size(out) * (rate if eng == DV else 2.3)

        def tt(out, a, b, op, after=(), eng=DV):
            return Q.op(eng, lambda e: e.tensor_tensor(out, a, b, op), after, cost=dcost(out, eng))

        def ts(out, a, s1, s2, op0, op1=None, after=(), eng=DV):
            c = dcost(out, eng)
            if op1 is None:
                return Q.op(eng, lambda e: e.tensor_scalar(out, a, s1, None, op0), after, cost=c)
            return Q.op(eng, lambda e: e.tensor_scalar(out, a, s1, s2, op0, op1), after, cost=c)

        def stt(out, a, s, b, op0, op1, after=()):
            return Q.op(DV, lambda e: e.scalar_tensor_tensor(out, a, s, b, op0, op1), after, cost=dcost(out))

        def ttr(out, a, b, op0, op1, init, acc, after=()):
            return Q.op(DV, lambda e: e.tensor_tensor_reduce(out=out, in0=a, in1=b, scale=1.0, scalar=init,
                                                             op0=op0, op1=op1, accum_out=acc), after,
                        cost=dcost(out) + 60)

        def red(out, a, op, after=()):
            return Q.op(DV, lambda e: e.tensor_reduce(out, a, AX.X, op), after, cost=dcost(a))

        def vcp(out, a, after=()):
            return Q.op(DV, lambda e: e.tensor_copy(out, a), after, cost=dcost(out))

        def rcp(out, a, after=()):
            return Q.op(DV, lambda e: e.reciprocal(out, a), after, cost=dcost(out, rate=8.3))

        def act(out, a, f, after=(), bias=0.0, scale=1.0, acc=None):
            return Q.op(AC, lambda e: e.activation(out, a, f, bias=bias, scale=scale, accum_out=acc), after,
                        cost=190.0 + 0.833 * size(a))

        def acp(out, a, after=(), scale=1.0):
            return act(out, a, ACT.Copy if isinstance(scale, float) else ACT.Identity, after, scale=scale)

        def load(dst, src, after=(), eng=SP):
            s = ctx.enter_context(nc.semaphore(f"ld{len(loads)}"))
            loads.append(s)
            return Q.op(eng, lambda e: e.dma_start(dst, src), after, sem=s, val=16, cost=1500.0)

        loads = []

        def rf(ap):
            return ap.bitcast(FP)

        cst = sb("cst", NCO)
        lev = sb("lev", 320, U8)
        sm = sb("sm", NSM)
        st = sb("st", 256)
        post = sb("post", 1024)
        X = sb("X", 2048)
        raw = [sb(f"raw{i}", SLABW) for i in range(NRAW)]
        WH = [sb(f"wh{i}", 1024, FR) for i in range(NUNIT)]
        WL = [sb(f"wl{i}", 1024, FR) for i in range(NUNIT)]
        R1 = sb("R1", 2 * 8 * T1, FR)
        R2 = sb("R2", 4096, FR)
        R3 = sb("R3", 4096, FR)
        NFA = 19104
        FA = sb("FA", NFA)
        banks = [Slot(ctx.enter_context(nc.psum_tensor(f"pb{i}", [128, 512], FP))) for i in range(8)]

        def C(n):
            return cst[:, CO[n][0]:CO[n][0] + CO[n][1]]

        def S_(n):
            return sm[:, SM[n][0]:SM[n][0] + SM[n][1]]

        def sc(n, i):
            return sm[:, SM[n][0] + i:SM[n][0] + i + 1]

        ident = C("ident")
        ones = C("ones")

        def fa(off, n, p=128):
            assert off + n <= NFA, (off, n)
            return FA[0:p, off:off + n]

        stn = [0]

        def stat(n=1):
            if stn[0] + n > 256:
                stn[0] = 0
            stn[0] += n
            return st[:, stn[0] - n:stn[0]]

        t_x = [load(X[:, 1024 * c:1024 * c + 1024], dr["x"][0, 128 * c:128 * c + 128, :]) for c in range(2)]
        XM = fa(0, 1024, 16)
        t_xm = load(XM, dr["meta"])
        t_id = load(cst[:, 0:128], dr["cst"][:, 0:128])
        t_sm = load(sm[:, :], dr["sm"])
        t_cst = []

        NU = 2 * NSLAB
        slab_sem = [ctx.enter_context(nc.semaphore(f"slab{i}")) for i in range(NRAW)]
        slab_tok, split_tok, unit_free = {}, {}, {}

        def load_slab(s):
            if s >= NSLAB:
                return
            after = [split_tok[2 * (s - NRAW)], split_tok[2 * (s - NRAW) + 1]] if s >= NRAW else []
            dst, src = raw[s % NRAW][:, :], dr["w"][s]
            slab_tok[s] = Q.op(SP, lambda e: e.dma_start(dst, src), after,
                               sem=slab_sem[s % NRAW], val=16 * (s // NRAW + 1), cost=2900.0)

        def split(u, eng=DV):
            if u >= NU:
                return
            s, h = u // 2, u % 2
            r = raw[s % NRAW][:, 1024 * h:1024 * h + 1024]
            hi, lo = WH[u % NUNIT][:, :], WL[u % NUNIT][:, :]
            w = [slab_tok[s], unit_free.get(u - NUNIT)]
            if Q.when(AC, w, 1050.0) > Q.when(DV, w, 620.0) + 1500.0:
                a = Q.op(DV, lambda e: e.tensor_copy(hi, r), w, cost=620.0)
            else:
                a = act(hi, r, ACT.Copy, w)
            if eng == DV and Q.when(DV, [a], 1150.0) > Q.when(PO, [a], 2450.0) + 500.0:
                eng = PO
            b = tt(lo, r, rf(hi), ALU.subtract, [a], eng)
            split_tok[u] = [a, b]
            if h == 1:
                load_slab(s + NRAW)

        for s in range(NRAW):
            load_slab(s)
        t_cst.append(load(cst[:, 128:NCO], dr["cst"][:, 128:NCO]))
        t_lev = load(fa(5120, 320), dr["lev"])
        t_lev = Q.op(PO, lambda e: e.tensor_copy(lev[:, :], fa(5120, 320)), [t_lev])
        cur = [0]

        def take(n=1):
            i = cur[0]
            u, o = i // 8, i % 8
            assert o + n <= 8
            cur[0] += n
            sl = slice(128 * o, 128 * o + 128 * n)
            return WH[u % NUNIT][:, sl], WL[u % NUNIT][:, sl], split_tok[u], (u if o + n == 8 else None)

        def done(u, tok, eng=DV):
            if u is not None:
                unit_free[u] = [tok]
                split(u + NUNIT, eng)

        def prod3(out, lh, ll, rh, rl, first, last, after, skip=False):
            mm(out, lh, rh, first, False, after, skip)
            mm(out, lh, rl, False, False, (), skip)
            return mm(out, ll, rh, False, last, (), skip)

        def gemm_a(ntiles, kt, act_h, act_l, T, ready, evac, ring):
            for n in range(ntiles):
                bk = ring.get()
                for k in range(kt):
                    wh, wl, wt, end = take()
                    t = prod3(bk.ap[:, 0:T], wh, wl, act_h(k), act_l(k), k == 0, k == kt - 1,
                              [wt, bk.free if k == 0 else None, ready(k)])
                    done(end, t)
                evac(n, bk, t)
                yield

        def rstd(ssq, dim, after, p=128, n=1):
            v = stat(n)[0:p]
            r = stat(n)[0:p]
            a = ts(v, ssq, 1.0 / dim, EPS, ALU.mult, ALU.add, after)
            a = act(v, v, ACT.Sqrt, [a])
            return r, rcp(r, v, [a])

        def split_act(val, h, l, after, scale=1.0):
            a = acp(h, val, after, scale)
            if isinstance(scale, float) and scale == 1.0:
                b = tt(l, val, rf(h), ALU.subtract, [a])
            else:
                b = stt(l, val, scale, rf(h), ALU.mult, ALU.subtract, [a])
            return a, b

        def prenorm(tiles, gain, UH, UL, T, xn, ring):
            nt = []
            for (x, c0, p, (ss, rdy)), y in zip(tiles, xn):
                r, b = rstd(ss, D, [rdy], p)
                nt.append([acp(y[:, 0:512], x[:, 0:512], [b], r),
                           ts(y[:, 512:1024], x[:, 512:1024], r, None, ALU.mult, None, [b])])
            out = []
            for k in range(8):
                bk = ring.get()
                for i, ((x, c0, p, rdy), y) in enumerate(zip(tiles, xn)):
                    t = tr(bk.ap[:, c0:c0 + p], y[:, 128 * k:128 * k + 128],
                           [nt[i][k // 4], bk.free if i == 0 else None])
                a, b = split_act(bk.ap[:, 0:T], UH(k), UL(k), [t, t_sm], sc(gain, k))
                give(bk, b)
                out.append([a, b])
            return out

        def postnorm(c, banks_c, t_acc, gtok, free):
            y = [fa(1024 * c, 512), fa(1024 * c + 512, 512)]
            s2 = stat(2)
            a0 = act(y[0], banks_c[0].ap[:, :], ACT.Square, [t_acc, free], acc=s2[:, 0:1])
            a1 = act(y[1], banks_c[1].ap[:, :], ACT.Square, [], acc=s2[:, 1:2])
            s1, q2, q1 = stat(), stat(2), stat()
            b = tt(s1, s2[:, 0:1], s2[:, 1:2], ALU.add, [a0, a1])
            r, b = rstd(s1, D, [b])
            sq = []
            for h in range(2):
                b1 = stt(y[h], banks_c[h].ap[:, :], r, post[:, 512 * h:512 * h + 512], ALU.mult, ALU.mult,
                         [b, gtok])
                give(banks_c[h], b1)
                xs = X[:, 1024 * c + 512 * h:1024 * c + 512 * h + 512]
                b2 = tt(xs, y[h], xs, ALU.add, [b1], PO if h == 0 else DV)
                sq.append([b2, act(y[h], xs, ACT.Square, [b2], acc=q2[:, h:h + 1])])
            b = tt(q1, q2[:, 0:1], q2[:, 1:2], ALU.add, [sq[0][1], sq[1][1]])
            return q1, [b, sq]

        def set_sqrt():
            v = stat()
            act(v, ones[:, 0:1], ACT.Sqrt)

        def sumsq(x, y, p, rdy):
            ss = stat()[0:p]
            return ss, [act(y, x, ACT.Square, [rdy], acc=ss)]

        ringA = Ring(banks)
        UH1 = R1[:, 0:8 * T1].rearrange("p (k t) -> p k t", k=8)
        UL1 = R1[:, 8 * T1:16 * T1].rearrange("p (k t) -> p k t", k=8)
        x0, x1 = X[:, 0:1024], X[:, 1024:2048]
        xn = [fa(1024, 1024, 16), fa(2048, 1024), fa(3072, 1024)]
        sx0 = sumsq(x0, xn[1], 128, t_x[0])
        sx1 = sumsq(x1, xn[2], 128, t_x[1])
        sxm = sumsq(XM, xn[0], 16, t_xm)
        t_u = prenorm([(x0, 16, 128, sx0), (x1, 144, 128, sx1), (XM, 0, 16, sxm)], "mix_pre",
                      lambda k: UH1[:, k, :], lambda k: UL1[:, k, :], T1, [xn[1], xn[2], xn[0]], ringA)
        u_done = t_u
        for u in range(NUNIT):
            split(u)

        o = 0
        Fr = fa(o, 2048).rearrange("p (h t) -> p h t", h=8); oF = o; o += 2048
        Kr = fa(o, 2048).rearrange("p (h t) -> p h t", h=8); oK = o; o += 2048
        Qr = fa(o, 2048).rearrange("p (h t) -> p h t", h=8); oQ = o; o += 2048
        SG = fa(o, 2048).rearrange("p (h t) -> p h t", h=8); o += 2048
        Vt = fa(o, 2048).rearrange("p (c n) -> p c n", c=2); oV = o; o += 2048
        AT = fa(o, 2048).rearrange("p (x t) -> p x t", x=16); oA = o; o += 2048
        Vm = fa(o, 1024, 16); o += 1024
        KT = fa(o, 1024); KmT = fa(o, 1024, 16); o += 1024
        Fm = fa(o, 128).rearrange("p (h t) -> p h t", h=8); o += 128
        Km = fa(o, 128).rearrange("p (h t) -> p h t", h=8); o += 128
        Tt = [None] + [fa(o + 2048 - (4096 >> j), 2048 >> j) for j in range(1, 8)]; o += 2048
        sgr = Ring([Slot(Tt[1][:, i * T1:(i + 1) * T1]) for i in range(3)])
        lbt = fa(o, 24); o += 24
        assert o <= NFA

        mxl, e0, e1 = lbt[:, 0:8], lbt[:, 8:16], lbt[:, 16:24]
        for e_ in (PE, AC, DV, PO):
            Q.gate[e_] = t_cst[0]
        a = tt(mxl, S_("lb0"), S_("lb1"), ALU.max, [t_sm])
        a = [tt(e0, S_("lb0"), mxl, ALU.subtract, [a]), tt(e1, S_("lb1"), mxl, ALU.subtract, [a])]
        a = act(lbt[:, 8:24], lbt[:, 8:24], ACT.Exp, a)
        a = tt(e1, e0, e1, ALU.add, [a])
        a = rcp(e1, e1, [a])
        a = tt(e0, e0, e1, ALU.mult, [a])
        t_lb = ts(e1, e0, -1.0, 1.0, ALU.mult, ALU.add, [a])

        tF, tK, tKm, tQ, tG = {}, {}, {}, {}, {}
        first_f = [u_done, Q.now()]

        def ev_f(n, bk, t):
            s = sgr.get()
            a = act(s.ap, bk.ap[:, 0:T1], ACT.Sigmoid, [t, s.free, first_f])
            give(bk, a)
            b1 = ts(Fr[:, n, :], s.ap[:, NM:T1], e1[:, n:n + 1], e0[:, n:n + 1], ALU.mult, ALU.add, [a, t_lb, first_f])
            b2 = ts(Fm[:, n, :], s.ap[:, 0:NM], e1[:, n:n + 1], e0[:, n:n + 1], ALU.mult, ALU.add)
            b3 = ts(Kr[:, n, :], Fr[:, n, :], -1.0, 1.0, ALU.mult, ALU.add, [b1])
            b4 = ts(Km[:, n, :], Fm[:, n, :], -1.0, 1.0, ALU.mult, ALU.add, [b2])
            give(s, b2)
            tF[n], tK[n], tKm[n] = b2, b3, b4

        UHk, ULk = (lambda k: UH1[:, k, :]), (lambda k: UL1[:, k, :])
        UHr, ULr = (lambda k: UH1[:, k, NM:T1]), (lambda k: UL1[:, k, NM:T1])
        ready_u = lambda k: t_u[k]
        for _ in gemm_a(8, 8, UHk, ULk, T1, ready_u, ev_f, ringA):
            pass
        tV = []
        for nh in range(2):
            bk = [ringA.get() for _ in range(3)]
            cols = [(0, 128), (16, 128), (144, 128)]
            for k in range(8):
                wh, wl, wt, end = take(4)
                for i, (c0, m) in enumerate(cols):
                    t = prod3(bk[i].ap[:, :], UH1[:, k, c0:c0 + m], UL1[:, k, c0:c0 + m], wh, wl, k == 0, k == 7,
                              [wt, bk[i].free])
                done(end, t)
            a = acp(Vm[:, 512 * nh:512 * nh + 512], bk[0].ap[0:16, :], [t, first_f])
            give(bk[0], a)
            for c in range(2):
                a = acp(Vt[:, c, 512 * nh:512 * nh + 512], bk[c + 1].ap[:, :], [t, first_f])
                give(bk[c + 1], a)
            tV.append(a)

        def ev_silu(dst, tks):
            def ev(n, bk, t):
                a = act(dst[:, n, :], bk.ap[:, 0:256], ACT.Sigmoid, [t])
                b = tt(dst[:, n, :], bk.ap[:, 0:256], dst[:, n, :], ALU.mult, [a])
                give(bk, b)
                tks[n] = b
            return ev

        for _ in gemm_a(8, 8, UHr, ULr, 256, ready_u, ev_silu(Qr, tQ), ringA):
            pass

        ringB = Ring([banks[i] for i in (4, 5, 6, 7)])
        ringA = Ring([banks[i] for i in (0, 1, 2)])
        bSSQ = banks[3]
        S1 = fa(oF, 1024)
        S2 = fa(oF + 1024, 1024)
        t_S1, t_S2, t_KT, t_Q7 = {}, {}, {}, {}
        ssq_bank = bSSQ.ap

        def half(ap, j):
            return ap.rearrange("p (b two s) -> p b two s", two=2, s=1 << j)

        def bcast(ap, n):
            p, b = ap.shape
            return ap.rearrange("p (b o) -> p b o", o=1).broadcast_to([p, b, n])

        def until(ok):
            while not ok():
                Q.step_end = Q.clock["pe"] + 300.0
                yield

        def meta_part():
            t = [tF[n] for n in range(8)] + [tKm[n] for n in range(8)]
            kf = Km.rearrange("p h t -> p (h t)")
            tot = Fm.rearrange("p h t -> p (h t)")
            for j in range(4):
                v = half(kf, j)
                tv = tot.rearrange("p (b two) -> p b two", two=2)
                w = tt(v[:, :, 0, :], v[:, :, 0, :], tv[:, :, 1:2].broadcast_to([128, v.shape[1], 1 << j]), ALU.mult, t)
                if j < 3:
                    nt = KT[:, 64 * j:64 * j + (64 >> j)]
                    t = [w, tt(nt, tv[:, :, 0], tv[:, :, 1], ALU.mult, t)]
                    tot = nt
                else:
                    t = [w]
                yield
            for g in range(2):
                bk = ringB.get()
                for i in range(4):
                    w = tr(bk.ap[0:16, 128 * i:128 * i + 128], Km[:, 4 * g + i, :], [t, bk.free])
                c = vcp(KmT[:, 512 * g:512 * g + 512], bk.ap[0:16, :], [w])
                give(bk, c)
                yield
                bk = ringB.get()
                for i in range(4):
                    h = 4 * g + i
                    w = mm(bk.ap[:, 128 * i:128 * i + 128], KmT[:, 128 * h:128 * h + 128], Vm[:, 128 * h:128 * h + 128],
                           True, True, [c, bk.free, tV])
                t_S1[g] = (bk, w)
                if g == 1:
                    m_dead.extend([w, c])
                yield

        def meta_store(g, after):
            bk, w = t_S1[g]
            c = vcp(S1[:, 512 * g:512 * g + 512], bk.ap[:, :], [w, after])
            give(bk, c)
            t_S1[g] = c

        def hgrn_group(g):
            hs = range(4 * g, 4 * g + 4)
            kf = Kr[:, 4 * g:4 * g + 4, :].rearrange("p h t -> p (h t)")
            qf = Qr[:, 4 * g:4 * g + 4, :].rearrange("p h t -> p (h t)")
            ff = Fr[:, 4 * g:4 * g + 4, :].rearrange("p h t -> p (h t)")
            tk, tq = [tK[h] for h in hs], [tQ[h] for h in hs]
            tot, ttot = ff, [tF[h] for h in hs]
            av = AT[:, 8 * g:8 * g + 8, :]
            last = None
            for lv in range(-1, 7):
                cps = []
                if lv < 0:
                    for b in range(2):
                        bk = ringB.get()
                        for i in range(4):
                            x = 4 * b + i
                            w = mm(bk.ap[:, 128 * i:128 * i + 128], kf[:, 128 * x:128 * x + 128],
                                   qf[:, 128 * x:128 * x + 128], True, True, [tk, tq, bk.free])
                        m = ident.rearrange("p (o t) -> p o t", o=1).broadcast_to([128, 4, 128])
                        c = tt(av[:, 4 * b:4 * b + 4, :], bk.ap[:, :].rearrange("p (x t) -> p x t", x=4), m,
                               ALU.mult, [w])
                        give(bk, c)
                        cps.append(c)
                else:
                    nb, sz = 64 >> lv, 1 << lv
                    qr = half(qf, lv)
                    bk = ringB.get()
                    for x in range(8):
                        w = mm(bk.ap[:, 64 * x:64 * x + 64], kf[:, 128 * x:128 * x + 128],
                               qr[:, nb * x:nb * x + nb, 1, :], True, True, [tk, tq, bk.free])
                    src = bk.ap[:, :].rearrange("p (x b s) -> p x b s", x=8, b=nb)
                    dst = av.rearrange("p x (b two s) -> p x b two s", two=2, s=sz)
                    if lv < 5:
                        m = lev[:, 64 * lv:64 * lv + 64].rearrange("p (o b s) -> p o b s", o=1, b=nb)
                        m = m.broadcast_to([128, 8, nb, sz])
                        dd = dst[:, :, :, 1, :]
                        cps.append(Q.op(DV, lambda e, dd=dd, m=m, src=src: e.copy_predicated(dd, m, src),
                                        [w, t_lev, last]))
                    else:
                        for b in range(nb):
                            r0 = 2 * sz * b
                            cps.append(acp(av[r0:r0 + sz, :, r0 + sz:r0 + 2 * sz], src[r0:r0 + sz, :, b, :],
                                           [w, last]))
                    give(bk, cps)
                yield
                last = cps
                if lv < 0:
                    tq = [tt(qf, qf, ff, ALU.mult, [w, tq, ttot])]
                else:
                    j = lv
                    kv, qv = half(kf, j), half(qf, j)
                    tv = tot.rearrange("p (b two) -> p b two", two=2)
                    nb = kv.shape[1]
                    tk = [tt(kv[:, :, 0, :], kv[:, :, 0, :], tv[:, :, 1:2].broadcast_to([128, nb, 1 << j]), ALU.mult, [w, ttot, tk])]
                    tq = [tt(qv[:, :, 1, :], qv[:, :, 1, :], tv[:, :, 0:1].broadcast_to([128, nb, 1 << j]), ALU.mult, [w, ttot, tq])]
                    nt = Tt[j + 1][:, (1024 >> (j + 1)) * g:(1024 >> (j + 1)) * (g + 1)]
                    ttot = [tt(nt, tv[:, :, 0], tv[:, :, 1], ALU.mult, [ttot])]
                    tot = nt
                    if j == 0:
                        f_dead[g] = [tk, tq, ttot]
                        if len(f_dead) == 2:
                            while len(t_S1) < 2:
                                Q.step_end = Q.clock["pe"] + 300.0
                                yield
                            meta_store(0, [f_dead[0], f_dead[1]])
                            meta_store(1, [f_dead[0], f_dead[1]])
                yield
            bk = ringB.get()
            for i in range(4):
                w = tr(bk.ap[:, 128 * i:128 * i + 128], Kr[:, 4 * g + i, 0:128], [tk, bk.free])
            c = acp(KT[:, 512 * g:512 * g + 512], bk.ap[:, :], [w, list(m_dead)])
            give(bk, c)
            k_dead[g] = w
            yield
            bk = ringB.get()
            for i in range(4):
                h = 4 * g + i
                w = mm(bk.ap[:, 128 * i:128 * i + 128], KT[:, 128 * h:128 * h + 128], Vt[:, 0, 128 * h:128 * h + 128],
                       True, True, [c, bk.free])
            assert isinstance(t_S1[g], Tok)
            s2 = S2[:, 512 * g:512 * g + 512].rearrange("p (h v) -> p h v", h=4)
            s1 = S1[:, 512 * g:512 * g + 512].rearrange("p (h v) -> p h v", h=4)
            tv = tot.rearrange("p (h c) -> p h c", c=2)
            c = tt(s2, s1, tv[:, :, 0:1].broadcast_to([128, 4, 128]), ALU.mult, [ttot, t_S1[g], f_dead[0], f_dead[1]])
            c = tt(s2, s2, bk.ap[:, :].rearrange("p (h v) -> p h v", h=4), ALU.add, [c, w])
            give(bk, c)
            t_S2[g] = c
            t_Q7[g] = [tq, last]
            yield
            yield from hgrn_out(g)

        f_dead, k_dead, m_dead = {}, {}, []
        OT = Kr
        nsq = [0]
        tO, tSq = {}, {}

        def hgrn_out(g):
            while any(4 * g + i not in tG for i in range(4)):
                Q.step_end = Q.clock["pe"] + 500.0
                yield
            sqr = Slot(Tt[1][:, 512 * g:512 * g + 512])
            sqr.free = [t_S2[g], t_Q7[g]]
            for b in range(2):
                bk = ringB.get()
                for i in range(2):
                    h = 4 * g + 2 * b + i
                    for c in range(2):
                        dst = bk.ap[:, 256 * i + 128 * c:256 * i + 128 * c + 128]
                        mm(dst, Vt[:, c, 128 * h:128 * h + 128], AT[:, 2 * h + c, :], True, False, [bk.free, t_Q7[g], tV])
                        S = S1 if c == 0 else S2
                        w = mm(dst, S[:, 128 * h:128 * h + 128], Qr[:, h, 128 * c:128 * c + 128], False, True,
                               [t_S1[g], t_S2[g]])
                h0 = 4 * g + 2 * b
                sq = sqr
                a = act(sq.ap, bk.ap[:, :], ACT.Square, [w, sq.free])
                c = stt(OT[:, h0:h0 + 2, :].rearrange("p h t -> p (h t)"), bk.ap[:, :], sc("hg_g", 0),
                        SG[:, h0:h0 + 2, :].rearrange("p h t -> p (h t)"), ALU.mult, ALU.mult,
                        [a, tG[h0], tG[h0 + 1], k_dead[g]])
                give(bk, c)
                tO[h0] = c
                for i in range(2):
                    h = h0 + i
                    es = cst[:, CO["esel"][0] + 8 - h:CO["esel"][0] + 16 - h]
                    w = mm(ssq_bank[0:8, 0:256], es, sq.ap[:, 256 * i:256 * i + 256], nsq[0] == 0, nsq[0] == 7,
                           [a, bSSQ.free])
                    nsq[0] += 1
                give(sq, w)
                tSq[0] = w
                yield

        g1 = gemm_a(8, 8, UHr, ULr, 256, ready_u, ev_silu(SG, tG), ringA)
        CK = post[:, 0:2 * T1]
        CQ = sb("CQ", 512)
        KP = sb("KP", T1)
        tCK, tCQ, tKP = {}, {}, {}

        def ev_c(n, bk, t):
            if n < 2:
                a = acp(CK[:, T1 * n:T1 * n + T1], bk.ap[:, 0:T1], [t])
                give(bk, a)
                tCK[n] = a
            elif n == 2:
                b = tt(KP[:, :], bk.ap[:, 0:T1], C("cos"), ALU.mult, [t])
                give(bk, b)
                tKP[0] = b
            else:
                s = kps.get()
                b = tt(s.ap, bk.ap[:, 0:T1], C("sin"), ALU.mult, [t, s.free])
                give(bk, b)
                b = tt(KP[:, :], KP[:, :], s.ap, ALU.add, [b, tKP[0]])
                give(s, b)
                tKP[0] = b

        kps = Ring([Slot(post[:, 2 * T1:3 * T1])])

        def ev_cq(n, bk, t):
            a = acp(CQ[:, 256 * n:256 * n + 256], bk.ap[:, 0:256], [t])
            give(bk, a)
            tCQ[n] = a

        KN = fa(8192, 8 * T1).rearrange("p (h t) -> p h t", h=8)
        GA0 = fa(16672, 2048).rearrange("p (n t) -> p n t", n=8)
        GA1 = fa(10368, 2048).rearrange("p (n t) -> p n t", n=8)
        r8 = FA[0:8, 18848:19104]
        ringT = kps

        def latent_norm(src, T, n_t, gain, H, L, res):
            bk = ringA.get()
            s = ringT.get()
            for n in range(2):
                a = act(s.ap[:, 0:T], src[:, T * n:T * n + T], ACT.Square, [s.free, n_t[n]])
                w = mm(bk.ap[:, 0:T], ones, s.ap[:, 0:T], n == 0, n == 1, [a, bk.free])
                s.free = [w]
            a = ts(s.ap[:, 0:T], bk.ap[:, 0:T], 1.0 / 256, EPS, ALU.mult, ALU.add, [w])
            give(bk, a)
            a = act(s.ap[:, 0:T], s.ap[:, 0:T], ACT.Sqrt, [a])
            a = rcp(s.ap[:, 0:T], s.ap[:, 0:T], [a])
            for n in range(2):
                v = src[:, T * n:T * n + T]
                b = stt(v, v, sc(gain, n), s.ap[:, 0:T], ALU.mult, ALU.mult, [a])
                res.append(split_act(v, H(n), L(n), [b]))
            give(s, b)

        ckh = R3[:, 0:2 * T1].rearrange("p (k t) -> p k t", k=2)
        ckl = R3[:, 2 * T1:4 * T1].rearrange("p (k t) -> p k t", k=2)
        cqh = R3[:, 1088:1600].rearrange("p (k t) -> p k t", k=2)
        cql = R3[:, 1600:2112].rearrange("p (k t) -> p k t", k=2)
        t_ck, t_cq = [], []
        tKN, tQN, tQP = {}, {}, {}

        def ev_copy(dst, T, tks, first):
            def ev(n, bk, t):
                a = acp(dst[:, n, :], bk.ap[:, 0:T], [t, first])
                give(bk, a)
                tks[n] = a
            return ev

        def lat():
            yield from gemm_a(4, 8, UHk, ULk, T1, ready_u, ev_c, ringA)
            yield from gemm_a(1, 8, UHr, ULr, 256, ready_u, ev_cq, ringA)
            latent_norm(CK, T1, tCK, "kv_g", lambda n: ckh[:, n, :], lambda n: ckl[:, n, :], t_ck)
            yield from gemm_a(1, 8, UHr, ULr, 256, ready_u, lambda n, bk, t: ev_cq(1, bk, t), ringA)
            latent_norm(CQ, 256, tCQ, "q_g", lambda n: cqh[:, n, :], lambda n: cql[:, n, :], t_cq)

        tGate = {}
        t_hb = ts(S_("b_gate"), S_("b_gate"), 0.5, None, ALU.mult, None, [t_sm])

        def gates(GA, n0, after):
            def ev(n, bk, t):
                a = act(GA[:, n, :], bk.ap[:, 0:256], ACT.Tanh, [t, after, t_hb], bias=sc("b_gate", n0 + n), scale=0.5)
                give(bk, a)
                tGate[n0 + n] = a
            return gemm_a(8, 8, UHr, ULr, 256, ready_u, ev, ringA)

        blend(Q, [meta_part(), hgrn_group(0), hgrn_group(1)], 3, [g1, lat(), gates(GA0, 0, None)])
        ph = Q.now()
        OHh = R2[:, 0:2048].rearrange("p (k t) -> p k t", k=8)
        OHl = R2[:, 2048:4096].rearrange("p (k t) -> p k t", k=8)
        tOH = {}

        def hgrn_norm():
            a = ts(r8, ssq_bank[0:8, 0:256], 1.0 / 128, EPS, ALU.mult, ALU.add, [tSq[0]])
            give(bSSQ, a)
            a = act(r8, r8, ACT.Sqrt, [a])
            a = rcp(r8, r8, [a])
            yield
            for h0 in range(0, 8, 2):
                bk = ringB.get()
                for i in range(2):
                    w = mm(bk.ap[:, 256 * i:256 * i + 256], ident[0:8, h0 + i:h0 + i + 1].broadcast_to([8, 128]), r8,
                           True, True, [a, bk.free])
                ov = OT[:, h0:h0 + 2, :].rearrange("p h t -> p (h t)")
                b = tt(ov, ov, bk.ap[:, :], ALU.mult, [w, tO[h0]])
                give(bk, b)
                x = split_act(ov, OHh[:, h0:h0 + 2, :].rearrange("p h t -> p (h t)"),
                              OHl[:, h0:h0 + 2, :].rearrange("p h t -> p (h t)"), [b])
                tOH[h0] = tOH[h0 + 1] = x
                yield

        QN = fa(0, 2048).rearrange("p (h t) -> p h t", h=8)
        QP = fa(4096, 1024).rearrange("p (h t) -> p h t", h=4)
        VMm = fa(5120, 1024, 16)
        VM = fa(6144, 2048).rearrange("p (c n) -> p c n", c=2)
        o = 12416
        sP, sT = [], []
        for i in range(4):
            sP.append(Slot(fa(o, 416))); o += 416
        for i in range(3):
            sT.append(Slot((fa(o, 384), fa(o + 384, 256, 16)))); o += 640
        tmp = [Slot(fa(o + i * T1, T1)) for i in range(2)]; o += 2 * T1
        assert o <= 16672
        for s in sP + sT + tmp:
            s.free = ph
        ringP, ringPT = Ring(sP), Ring(sT)
        ringT = Ring(tmp)
        ringA = Ring([banks[i] for i in (0, 1, 2)])
        ringB = Ring([banks[i] for i in (4, 5, 6, 7, 3)])

        def kv_values():
            for nh in range(2):
                bks = [ringA.get() for _ in range(3)]
                for k in range(2):
                    wh, wl, wt, end = take(4)
                    for i, c0 in enumerate((0, 16, 144)):
                        t = prod3(bks[i].ap[:, :], ckh[:, k, c0:c0 + 128], ckl[:, k, c0:c0 + 128], wh, wl, k == 0,
                                  k == 1, [wt, bks[i].free, t_ck])
                    done(end, t)
                a = acp(VMm[:, 512 * nh:512 * nh + 512], bks[0].ap[0:16, :], [t, ph])
                give(bks[0], a)
                for c in range(2):
                    a = acp(VM[:, c, 512 * nh:512 * nh + 512], bks[c + 1].ap[:, :], [t, ph])
                    give(bks[c + 1], a)
                tKN["v"] = a
                yield

        def ev_rope(n, bk, t):
            i = n // 2
            if n % 2 == 0:
                b = tt(QP[:, i, :], bk.ap[:, 0:256], C("cos")[:, NM:T1], ALU.mult, [t, ph])
                give(bk, b)
                tQP[i] = b
            else:
                s = ringT.get()
                b = tt(s.ap[:, 0:256], bk.ap[:, 0:256], C("sin")[:, NM:T1], ALU.mult, [t, s.free])
                give(bk, b)
                b = tt(QP[:, i, :], QP[:, i, :], s.ap[:, 0:256], ALU.add, [b, tQP[i]])
                give(s, b)
                tQP[i] = b

        def latents_out():
            yield from gemm_a(8, 2, lambda k: ckh[:, k, :], lambda k: ckl[:, k, :], T1, lambda k: t_ck[k],
                              ev_copy(KN, T1, tKN, ph), ringA)
            yield from kv_values()
            yield from gemm_a(8, 2, lambda k: cqh[:, k, :], lambda k: cql[:, k, :], 256, lambda k: t_cq[k],
                              ev_copy(QN, 256, tQN, ph), ringA)
            yield from gemm_a(8, 2, lambda k: cqh[:, k, :], lambda k: cql[:, k, :], 256, lambda k: t_cq[k], ev_rope,
                              ringA)
            c_dead.append(Q.q[PE][-1])

        c_dead = []
        OMh = R3[:, 0:2048].rearrange("p (k t) -> p k t", k=8)
        OMl = R3[:, 2048:4096].rearrange("p (k t) -> p k t", k=8)
        tOM = {}

        MS = float(192 ** -0.5)

        def mla_head(h):
            yield from until(lambda: c_dead and ringP.idle())
            sl = ringP.get()
            S = sl.ap
            base = 64 * (h % 2)
            w_ = (144, 272)
            off = (0, 144)
            mx, nm_, sm_, ri = stat(2), stat(2), stat(2), stat(2)
            bs = []
            for c in range(2):
                bk = ringB.get()
                nk = w_[c]
                mm(bk.ap[:, 0:nk], QN[:, h, 128 * c:128 * c + 128], KN[:, h, 0:nk], True, False,
                   [bk.free, tKN[h], tQN[h]])
                w = mm(bk.ap[:, 0:nk], QP[base:base + 64, h // 2, 128 * c:128 * c + 128], KP[base:base + 64, 0:nk],
                       False, True, [tKP[0], tQP[h // 2]])
                b = ttr(S[:, off[c]:off[c] + nk], bk.ap[:, 0:nk], C("m1")[:, 272 - nk:272], ALU.add, ALU.max,
                        2 * NEG, mx[:, c:c + 1], [w, sl.free])
                give(bk, b)
                bs.append(b)
            b = ts(nm_, mx, -MS, None, ALU.mult, None, bs)
            yield
            es = []
            for c in range(2):
                Sc = S[:, off[c]:off[c] + w_[c]]
                es.append(act(Sc, Sc, ACT.Exp, [b], bias=nm_[:, c:c + 1], scale=MS, acc=sm_[:, c:c + 1]))
            b = rcp(ri, sm_, es)
            tp = []
            for c in range(2):
                Sc = S[:, off[c]:off[c] + w_[c]]
                tp.append(ts(Sc, Sc, ri[:, c:c + 1], None, ALU.mult, None, [b]))
            yield
            yield from until(ringPT.idle)
            pt = ringPT.get()
            PT, PTm = pt.ap
            bk, bm = ringB.get(), ringB.get()
            tr(bk.ap[:, 0:128], S[:, 16:144], [tp[0], bk.free])
            tr(bm.ap[0:16, 0:128], S[:, 0:16], [bm.free])
            tr(bk.ap[:, 128:256], S[:, 160:288], [tp[1]])
            tr(bk.ap[:, 256:384], S[:, 288:416])
            w = tr(bm.ap[0:16, 128:256], S[:, 144:160])
            give(sl, w)
            a1 = acp(PT, bk.ap[:, 0:384], [w, pt.free])
            a2 = vcp(PTm, bm.ap[0:16, 0:256], [w, pt.free])
            give(bk, a1)
            give(bm, a2)
            yield
            bk = ringB.get()
            vh = slice(128 * h, 128 * h + 128)
            mm(bk.ap[:, 0:256], VM[:, 0, vh], PT[:, 0:256], True, False, [a1, a2, bk.free, tKN["v"]])
            mm(bk.ap[:, 0:256], VMm[:, vh], PTm, False, False)
            w = mm(bk.ap[:, 128:256], VM[:, 1, vh], PT[:, 256:384], False, True)
            x = split_act(bk.ap[:, 0:256], OMh[:, h, :], OMl[:, h, :], [w, c_dead])
            give(bk, x)
            give(pt, w)
            tOM[h] = x
            yield

        MXh = R1[:, 0:2048].rearrange("p (k t) -> p k t", k=8)
        MXl = R1[:, 2048:4096].rearrange("p (k t) -> p k t", k=8)
        tYa, tMX = {}, {}

        def ev_ya(n, bk, t):
            b = stt(GA0[:, n, :], GA0[:, n, :], 1.0, bk.ap[:, 0:256], ALU.add, ALU.mult, [t, tGate[n]])
            give(bk, b)
            tYa[n] = b

        def ev_yb(n, bk, t):
            g = GA1[:, n, :]
            b = stt(g, g, 1.0, bk.ap[:, 0:256], ALU.add, ALU.mult, [t, tGate[8 + n]])
            give(bk, b)
            b = tt(g, g, GA0[:, n, :], ALU.add, [b, tYa[n]])
            tMX[n] = split_act(g, MXh[:, n, :], MXl[:, n, :], [b, ga_dead], 0.5)

        def ya():
            yield from gemm_a(8, 8, lambda k: OHh[:, k, :], lambda k: OHl[:, k, :], 256, lambda k: tOH[k], ev_ya, ringA)

        blend(Q, [hgrn_norm()] + [mla_head(h) for h in range(8)], 5, [latents_out(), gates(GA1, 8, ph), ya()])
        ga_dead = Q.now()
        for _ in gemm_a(8, 8, lambda k: OMh[:, k, :], lambda k: OMl[:, k, :], 256, lambda k: tOM[k], ev_yb, ringA):
            pass

        def gemm_b(ACC, ks, kt, H, L, rdy):
            ks = list(ks)
            got = [[take(4), take(4)] for _ in ks]
            t = [None, None]
            for c in range(2):
                for k, g in zip(ks, got):
                    for h in range(2):
                        wh, wl, wt, end = g[h]
                        t[c] = prod3(ACC[c][h].ap[:, :], H(k)[:, 128 * c:128 * c + 128], L(k)[:, 128 * c:128 * c + 128],
                                     wh, wl, k == 0, k == kt - 1, [wt, rdy(k), ACC[c][h].free if k == 0 else None])
            return t, [g[1][3] for g in got]

        ACC = [[banks[4], banks[5]], [banks[6], banks[7]]]
        ringA = Ring([banks[i] for i in (0, 1, 2, 3)])

        def out_proj(H, L, rdy, gname):
            g = load(post[:, :], dr[gname], [Q.now()])
            fr = Q.now()
            for k in range(4):
                t, ends = gemm_b(ACC, [k], 8, H, L, rdy)
                done(ends[0], t)
            set_sqrt()
            t, ends = gemm_b(ACC, range(4, 8), 8, H, L, rdy)
            r = [postnorm(0, ACC[0], t[0], g, fr), postnorm(1, ACC[1], t[1], g, fr)]
            for u in ends:
                done(u, t[1], PO)
            return r

        t_h = out_proj(lambda k: MXh[:, k, :], lambda k: MXl[:, k, :], lambda k: tMX[k], "mix_post")
        U2h = R2[:, 0:2048].rearrange("p (k t) -> p k t", k=8)
        U2l = R2[:, 2048:4096].rearrange("p (k t) -> p k t", k=8)

        def norm2(gain, xr):
            return prenorm([(x0, 0, 128, xr[0]), (x1, 128, 128, xr[1])], gain,
                           lambda k: U2h[:, k, :], lambda k: U2l[:, k, :], 256,
                           [fa(2048, 1024), fa(3072, 1024)], ringA)

        t_u2 = norm2("ffn_pre", t_h)

        def ffn(nt, t_u2, hidden, gname):
            g = load(post[:, :], dr[gname], [Q.now()])
            ph = Q.now()
            hid = Ring([Slot((R3[:, 512 * i:512 * i + 256], R3[:, 512 * i + 256:512 * i + 512])) for i in range(8)])
            scr = Ring([Slot((fa(4096 + 512 * i, 256), fa(4096 + 512 * i + 256, 256))) for i in range(4)])
            for s in hid.slots + scr.slots:
                s.free = ph
            made = {}
            for i in range(nt):
                if True:
                    pair = []
                    gen = gemm_a(2, 8, lambda k: U2h[:, k, :], lambda k: U2l[:, k, :], 256, lambda k: t_u2[k],
                                 lambda n, bk, t: pair.append((bk, t)), ringA)
                    for _ in gen:
                        pass
                    s = scr.get()
                    hs = hid.get()
                    (bg, tg), (bu, tu) = pair
                    b = hidden(i, bg, tg, bu, tu, s)
                    give(s, b)
                    x = split_act(s.ap[1], hs.ap[0], hs.ap[1], [b, hs.free])
                    give(s, x)
                    made[i] = (hs, x)
                if i >= LAG:
                    k = i - LAG
                    t, ends = gemm_b(ACC, [k], nt, lambda k: made[k][0].ap[0], lambda k: made[k][0].ap[1],
                                     lambda k: [made[k][1]])
                    give(made[k][0], t)
                    done(ends[0], t)
            set_sqrt()
            t, ends = gemm_b(ACC, range(nt - LAG, nt), nt, lambda k: made[k][0].ap[0], lambda k: made[k][0].ap[1],
                             lambda k: [made[k][1]])
            r = [postnorm(0, ACC[0], t[0], g, ph), postnorm(1, ACC[1], t[1], g, ph)]
            for u in ends:
                done(u, t[1], PO)
            return r

        def hidden1(i, bg, tg, bu, tu, s):
            a = act(s.ap[0], bg.ap[:, 0:256], ACT.Silu, [tg, s.free])
            give(bg, a)
            b = tt(s.ap[1], s.ap[0], bu.ap[:, 0:256], ALU.mult, [a, tu])
            give(bu, b)
            return b

        t_x2 = ffn(HID1, t_u2, hidden1, "ffn_post")

        t_u2 = norm2("attn_pre", t_x2)
        ph = Q.now()
        o = 0
        mq = fa(o, 512).rearrange("p (n t) -> p n t", n=2); o += 512
        mk = fa(o, 512).rearrange("p (n t) -> p n t", n=2); o += 512
        TM1 = fa(o, 1024).rearrange("p (c n) -> p c n", c=2); o += 1024
        TM2 = fa(o, 768).rearrange("p (c n) -> p c n", c=2); o += 768
        nkc = fa(o, 256); o += 256
        nq = fa(o, 512).rearrange("p (n t) -> p n t", n=2); o += 512
        nks = fa(o, 256); o += 256
        nkw = fa(o, 256); o += 256
        dqk = fa(o, 1024).rearrange("p (n t) -> p n t", n=4); o += 1024
        sqk = fa(o, 1024).rearrange("p (n t) -> p n t", n=4); o += 1024
        BI = fa(o, 1024); o += 1024
        BI2 = fa(o, 1024); o += 1024
        win = fa(o, 480).rearrange("p (l n) -> p l n", l=32); o += 480
        hk = fa(o, 30); kcT = fa(o + 32, 15); vc = fa(o + 48, 64, 15); o += 112
        OM2 = fa(o, 2048).rearrange("p (c n) -> p c n", c=2); o += 2048
        Sc_ = fa(o, 120); o += 120
        PcT = fa(o, 1024, 15).rearrange("p (h t) -> p h t", h=4); o += 1024
        gat = fa(o, 24); o += 24
        lamt = fa(o, 88); o += 88
        sl2 = []
        for i in range(6):
            sl2.append(Slot((fa(o, 384), fa(o + 384, 384)))); o += 768
        assert o <= NFA, o
        oX1 = o; o += 1024
        assert o <= NFA, o
        for s in sl2:
            s.free = ph
        ringP = Ring(sl2)
        MIh = R3[:, 0:2048].rearrange("p (k t) -> p k t", k=8)
        MIl = R3[:, 2048:4096].rearrange("p (k t) -> p k t", k=8)
        tk = {}

        def tiles(names):
            def ev(n, bk, t):
                name, dst = names[n]
                a = acp(dst, bk.ap[:, 0:256], [t, ph])
                give(bk, a)
                tk[name] = a
            return gemm_a(len(names), 8, lambda k: U2h[:, k, :], lambda k: U2l[:, k, :], 256, lambda k: t_u2[k], ev, ringA)

        tBI = {}

        def biases(m, dst, base, scale, after):
            r = []
            for h in range(4):
                r.append(ts(dst[:, 256 * h:256 * h + 256], base, SLOPES[m + 4 * h] / scale, None, ALU.mult, None,
                            after, eng=PO))
            tBI[m] = r

        biases(0, BI, C("dmc"), 0.125, ph)
        biases(1, BI2, C("dmc"), 0.125, ph)

        def proj_a():
            yield from tiles([("mq0", mq[:, 0, :]), ("mq1", mq[:, 1, :]), ("mk0", mk[:, 0, :]), ("mk1", mk[:, 1, :])])
            bk = [ringA.get() for _ in range(2)]
            for k in range(8):
                wh, wl, wt, end = take(4)
                for c in range(2):
                    t = prod3(bk[c].ap[:, :], U2h[:, k, 128 * c:128 * c + 128], U2l[:, k, 128 * c:128 * c + 128],
                              wh, wl, k == 0, k == 7, [wt, bk[c].free])
                done(end, t)
            for c in range(2):
                a = acp(TM1[:, c, :], bk[c].ap[:, :], [t])
                give(bk[c], a)
            tk["tm1"] = a
            yield

        def proj_b():
            yield from tiles([("nkc", nkc), ("nq0", nq[:, 0, :]), ("nq1", nq[:, 1, :]), ("nks", nks)])
            bk = [ringA.get() for _ in range(3)]
            for k in range(8):
                wh, wl, wt, end = take(4)
                for c in range(2):
                    prod3(bk[c].ap[:, 0:268], U2h[:, k, 128 * c:128 * c + 128], U2l[:, k, 128 * c:128 * c + 128],
                          wh[:, 0:268], wl[:, 0:268], k == 0, k == 7, [wt, bk[c].free])
                t = prod3(bk[2].ap[:, 0:256], wh[:, 384:512], wl[:, 384:512], U2h[:, k, :], U2l[:, k, :],
                          k == 0, k == 7, [bk[2].free])
                done(end, t)
            for c in range(2):
                a = acp(TM2[:, c, 0:256], bk[c].ap[:, 0:256], [t])
                a = act(gat[:, 12 * c:12 * c + 12], bk[c].ap[:, 256:268], ACT.Tanh, [t], scale=0.5)
                give(bk[c], a)
            tk["tm2"] = ts(gat, gat, 0.5, 0.5, ALU.mult, ALU.add, [a])
            a = acp(nkw, bk[2].ap[:, 0:256], [t])
            give(bk[2], a)
            tk["nkw"] = a
            yield

        def proj_c():
            yield from tiles([(f"d{i}", dqk[:, i, :]) for i in range(4)] + [(f"s{i}", sqk[:, i, :]) for i in range(4)])

        ringA = Ring([banks[i] for i in (0, 1, 2)])
        ringB = Ring([banks[i] for i in (3, 4, 5, 6, 7)])
        tMI, tO2 = {}, {}
        cols = (slice(0, 128), slice(128, 384))

        def maps(S, q, k, bias, scale, after, free, tbias, sink=None):
            mx, nm_, sm_ = stat(2), stat(2), stat(2)
            bs = []
            for c in range(2):
                nk = 128 + 128 * c
                bk = ringB.get()
                w = mm(bk.ap[:, 0:nk], q[:, 128 * c:128 * c + 128], k[:, 0:nk], True, True, [bk.free, after])
                b = ttr(S[:, cols[c]], bk.ap[:, 0:nk], bias[:, 256 - nk:256], ALU.add, ALU.max, 2 * NEG,
                        mx[:, c:c + 1], [w, free, tbias])
                give(bk, b)
                bs.append(b)
            if sink is not None:
                b = ts(mx, mx, scale, sink, ALU.mult, ALU.max, bs)
                b = ts(nm_, mx, -1.0, None, ALU.mult, None, [b])
            else:
                b = ts(nm_, mx, -scale, None, ALU.mult, None, bs)
            yield
            es = []
            for c in range(2):
                es.append(act(S[:, cols[c]], S[:, cols[c]], ACT.Exp, [b], bias=nm_[:, c:c + 1], scale=scale,
                              acc=sm_[:, c:c + 1]))
            if sink is not None:
                e2 = stat(2)
                a = act(e2, nm_, ACT.Exp, [b], bias=sink)
                es = [es, tt(sm_, sm_, e2, ALU.add, [es, a])]
            return es, sm_

        ncopy = [0]

        def transp(S, PT, after):
            bk = ringB.get()
            tr(bk.ap[:, 0:128], S[:, 0:128], [after, bk.free])
            tr(bk.ap[:, 128:256], S[:, 128:256])
            w = tr(bk.ap[:, 256:384], S[:, 256:384])
            ncopy[0] += 1
            a = (vcp if ncopy[0] % 3 == 0 else acp)(PT, bk.ap[:, 0:384], [w])
            give(bk, a)
            return a

        def pv(PT, V, after):
            bk = ringB.get()
            mm(bk.ap[:, 0:64], PT[:, 0:128], V[0], True, True, [after, bk.free])
            mm(bk.ap[:, 64:128], PT[:, 128:256], V[0], True, False)
            w = mm(bk.ap[:, 64:128], PT[:, 256:384], V[1], False, True)
            return bk, w

        def to_features(kt):
            bk = ringB.get()
            for c in range(2):
                w = tr(bk.ap[:, 128 * c:128 * c + 128], OM2[:, c, 128 * kt:128 * kt + 128],
                       [tO2[2 * kt], tO2[2 * kt + 1], bk.free])
            x = split_act(bk.ap[:, 0:256], MIh[:, kt, :], MIl[:, kt, :], [w, ph])
            give(bk, x)
            tMI[kt] = x

        def head_done(gh, tok):
            tO2[gh] = tok
            if gh ^ 1 in tO2:
                to_features(gh // 2)

        def plain_head(gh, q, k, after, bias, tb, V, vt, sink=None):
            sl = ringP.get()
            S, PT = sl.ap
            e, sm_ = yield from maps(S, q, k, bias, 0.125, after, sl.free, tb, sink)
            yield
            a = transp(S, PT, e)
            ri = stat(2)
            br = rcp(ri, sm_, [e])
            yield
            bk, w = pv(PT, V, [a, vt])
            give(sl, w)
            yield
            for c in range(2):
                b = ts(OM2[:, c, 64 * gh:64 * gh + 64], bk.ap[:, 64 * c:64 * c + 64], ri[:, c:c + 1], None, ALU.mult,
                       None, [w, br, ph])
            give(bk, b)
            head_done(gh, b)
            yield

        def moba_head(h):
            b0 = 64 * (h % 2)
            return plain_head(h, mq[b0:b0 + 64, h // 2, :], mk[b0:b0 + 64, h // 2, :],
                              [tk[f"mq{h // 2}"], tk[f"mk{h // 2}"]], BI[:, 256 * h:256 * h + 256], tBI[0],
                              [TM1[:, c, 64 * h:64 * h + 64] for c in range(2)], tk["tm1"])

        def swa_head(h):
            b0 = 64 * (h % 2)
            g = h // 2
            yield from plain_head(12 + h, sqk[b0:b0 + 64, h // 2, :], sqk[b0:b0 + 64, 2 + g, :],
                                  [tk[f"s{h // 2}"], tk[f"s{2 + g}"]], BI2[:, 256 * h:256 * h + 256], tBI[3],
                                  [TM2[:, c, 128 + 64 * g:192 + 64 * g] for c in range(2)], tk["tm2"],
                                  sc("sinks", h))

        def nsa_head(h):
            b0 = 64 * (h % 2)
            gh = 4 + h
            q = nq[b0:b0 + 64, h // 2, :]
            prev = None
            for (k, kname, gi, voff) in ((nks, "nks", 1, 0), (nkw, "nkw", 2, 64)):
                sl = ringP.get()
                S, PT = sl.ap
                e, sm_ = yield from maps(S, q, k[b0:b0 + 64, :], BI2[:, 256 * h:256 * h + 256], 0.125,
                                         [tk[f"nq{h // 2}"], tk[kname]], sl.free, tBI[1])
                yield
                a = transp(S, PT, e)
                ri = stat(2)
                b = rcp(ri, sm_, [e])
                gv = gat.rearrange("p (c n) -> p c n", c=2)[:, :, 3 * h + gi]
                br = tt(ri, ri, gv, ALU.mult, [b, tk["tm2"]])
                yield
                bk, w = pv(PT, [TM2[:, c, voff:voff + 64] for c in range(2)], [a, tk["tm2"]])
                give(sl, w)
                yield
                n = []
                for c in range(2):
                    o_ = OM2[:, c, 64 * gh:64 * gh + 64]
                    p_ = bk.ap[:, 64 * c:64 * c + 64]
                    if prev is None:
                        n.append(ts(o_, p_, ri[:, c:c + 1], None, ALU.mult, None, [w, br, ph]))
                    else:
                        n.append(stt(o_, p_, ri[:, c:c + 1], o_, ALU.mult, ALU.add, [w, br, prev]))
                give(bk, n)
                prev = n
            while "pct" not in tk:
                Q.step_end = Q.clock["pe"] + 500.0
                yield
            bk = ringB.get()
            for c in range(2):
                w = mm(bk.ap[:, 64 * c:64 * c + 64], PcT[:, h, 128 * c:128 * c + 128], vc, True, True,
                       [bk.free, tk["pct"]])
            o_ = OM2[:, :, 64 * gh:64 * gh + 64]
            b = tt(o_, o_, bk.ap[:, 0:128].rearrange("p (c n) -> p c n", c=2), ALU.add, [w, prev])
            give(bk, b)
            head_done(gh, b)
            yield

        def nsa_cmp():
            pos = S_("cmp_pos")
            nv = nkc.rearrange("p (n l) -> p l n", l=16)
            ws = []
            for i in range(2):
                ws.append(tt(win[:, 16 * i:16 * i + 16, :], nv[:, :, i:i + 15],
                             pos[:, 16 * i:16 * i + 16].rearrange("p (l o) -> p l o", o=1).broadcast_to([128, 16, 15]),
                             ALU.add, [tk["nkc"], ph]))
            yield
            bk = [ringB.get(), ringB.get()]
            for q in range(4):
                c = w1_tok[q]
                for half_ in range(2):
                    p0 = 64 * half_
                    for l8 in range(8):
                        l = 8 * q + l8
                        t = mm(bk[half_].ap[:, 0:15], w1b[q % 2][p0:p0 + 64, 128 * l8:128 * l8 + 128],
                               win[p0:p0 + 64, l, :], l == 0, l == 31, [c, ws, bk[half_].free])
                w1_free[q] = [t]
                if q < 2:
                    load_w1(q + 2)
                yield
            for i in range(2):
                a = act(hk[:, 15 * i:15 * i + 15], bk[i].ap[:, 0:15], ACT.Gelu_apprx_tanh, [t, ph],
                        bias=sc("cmp_b1", i))
                give(bk[i], a)
            yield
            bk = ringB.get()
            w = mm(bk.ap[:, 0:15], S_("w2k"), hk[:, 0:15], True, True, [a, bk.free])
            w = mm(bk.ap[0:15, 64:128], hk[:, 15:30], S_("w2v"), True, True)
            a = acp(kcT, bk.ap[:, 0:15], [w, ph])
            a = acp(vc, bk.ap[0:15, 64:128], [w, ph])
            give(bk, a)
            yield
            sv = Sc_.rearrange("p (c h n) -> p c h n", c=2, h=4)
            cb = C("cmpb").rearrange("p (c h n) -> p c h n", c=2, h=4)
            sf = Sc_.rearrange("p (x n) -> p x n", n=15)
            mx, s8 = stat(8), stat(8)
            bs = []
            for par in range(2):
                bk = ringB.get()
                for c in range(2):
                    for hp in range(2):
                        x = 2 * c + hp
                        w = mm(bk.ap[:, 16 * x:16 * x + 15],
                               nq[64 * par:64 * par + 64, hp, 128 * c:128 * c + 128],
                               kcT[64 * par:64 * par + 64, :], True, True, [a, bk.free, tk["nq0"], tk["nq1"]])
                pv_ = bk.ap[:, 0:64].rearrange("p (x n) -> p x n", n=16)[:, :, 0:15]
                bs.append(tt(sf[:, par:8:2, :], pv_, C("cmpb").rearrange("p (x n) -> p x n", n=15)[:, par:8:2, :],
                             ALU.add, [w, ph]))
                give(bk, bs[-1])
            b = bs
            b = red(mx, sf, ALU.max, [b])
            b = ts(mx, mx, -1e20, None, ALU.max, None, [b])
            b = tt(sf, sf, bcast(mx, 15), ALU.subtract, [b])
            a = act(Sc_, Sc_, ACT.Exp, [b], scale=0.125)
            yield
            b = red(s8, sf, ALU.add, [a])
            b = ts(s8, s8, 1e-30, None, ALU.max, None, [b])
            b = rcp(s8, s8, [b])
            gv = gat.rearrange("p (x g) -> p x g", g=3)[:, :, 0]
            b = tt(s8, s8, gv, ALU.mult, [b, tk["tm2"]])
            b = tt(sf, sf, bcast(s8, 15), ALU.mult, [b])
            yield
            for hp in range(2):
                bk = ringB.get()
                for i in range(2):
                    for c in range(2):
                        w = tr(bk.ap[0:15, 256 * i + 128 * c:256 * i + 128 * c + 128], sv[:, c, 2 * hp + i, :], [b, bk.free])
                a = acp(PcT[:, 2 * hp:2 * hp + 2, :].rearrange("p h t -> p (h t)"), bk.ap[0:15, :], [w, ph])
                give(bk, a)
            tk["pct"] = a
            yield

        
        w1b = [post[:, :], fa(oX1, 1024)]
        w1_free = {}
        w1sem = [ctx.enter_context(nc.semaphore(f"w1_{i}")) for i in range(2)]

        def load_w1(q):
            dst, src = w1b[q % 2], dr["w1"][q]
            w1_tok[q] = Q.op(PO, lambda e: e.dma_start(dst, src), [w1_free.get(q - 2), w1_start],
                             sem=w1sem[q % 2], val=16 * (q // 2 + 1), cost=1500.0)

        w1_start = ph
        w1_tok = {}
        load_w1(0)
        load_w1(1)

        DS = float(32 ** -0.5)

        def lam_part():
            l = S_("lam")
            v = lamt[:, 0:64].rearrange("p (a n) -> p a n", a=2)
            lv = l.rearrange("p (a b n) -> p a b n", a=2, b=2)
            b = tt(v, lv[:, :, 0, :], lv[:, :, 1, :], ALU.mult, [ph])
            b = red(lamt[:, 64:66], v, ALU.add, [b])
            a = act(lamt[:, 66:68], lamt[:, 64:66], ACT.Exp, [b])
            b = tt(lamt[:, 68:69], lamt[:, 67:68], lamt[:, 66:67], ALU.subtract, [a])
            tk["lam"] = ts(lamt[:, 69:70], lamt[:, 68:69], -LINIT, None, ALU.add, None, [b])

        LINIT = 0.8 - 0.6 * 1.0
        nlam = lamt[:, 69:70]
        tD = {}

        def diff_head(h):
            n, b0 = h // 2, 64 * (h % 2)
            gh = 8 + h
            sl, slz = ringP.get(), ringP.get()
            aft = [tk[f"d{n}"], tk[f"d{2 + n}"]]
            bias = BI[:, 256 * h:256 * h + 256]
            S, PT = sl.ap
            Z = slz.ap[0]
            e1_, s1 = yield from maps(S, dqk[b0:b0 + 32, n, :], dqk[b0:b0 + 32, 2 + n, :], bias, DS, aft,
                                      sl.free, tBI[2])
            yield
            e2_, s2 = yield from maps(Z, dqk[b0 + 32:b0 + 64, n, :], dqk[b0 + 32:b0 + 64, 2 + n, :], bias, DS, aft,
                                      slz.free, tBI[2])
            yield
            r1, r2 = stat(2), stat(2)
            b1 = rcp(r1, s1, [e1_])
            b2 = rcp(r2, s2, [e2_])
            b2 = ts(r2, r2, nlam, None, ALU.mult, None, [b2, tk["lam"]])
            b1 = [ts(S[:, cols[c]], S[:, cols[c]], r1[:, c:c + 1], None, ALU.mult, None, [b1]) for c in range(2)]
            tp = [stt(S[:, cols[c]], Z[:, cols[c]], r2[:, c:c + 1], S[:, cols[c]], ALU.mult, ALU.add, [b1[c], b2])
                  for c in range(2)]
            give(slz, tp)
            yield
            a = transp(S, PT, tp)
            yield
            bk, w = pv(PT, [TM1[:, c, 256 + 64 * h:320 + 64 * h] for c in range(2)], [a, tk["tm1"]])
            give(sl, w)
            yield
            ys = []
            for c in range(2):
                ys.append(act(OM2[:, c, 64 * gh:64 * gh + 64], bk.ap[:, 64 * c:64 * c + 64], ACT.Square, [w, ph],
                              acc=dnr[:, 2 * h + c:2 * h + c + 1]))
            for c in range(2):
                b2 = stt(OM2[:, c, 64 * gh:64 * gh + 64], bk.ap[:, 64 * c:64 * c + 64], 1.0 - LINIT, S_("subln"),
                         ALU.mult, ALU.mult, [ys])
            give(bk, b2)
            tD[h] = [ys, b2]
            yield

        def diff_norm():
            b = ts(dnr[:, 8:16], dnr[:, 0:8], 1.0 / 64, EPS, ALU.mult, ALU.add, [tD[h] for h in range(4)])
            a = act(dnr[:, 8:16], dnr[:, 8:16], ACT.Sqrt, [b])
            b = rcp(dnr[:, 8:16], dnr[:, 8:16], [a])
            for h in range(4):
                for c in range(2):
                    o_ = OM2[:, c, 64 * (8 + h):64 * (8 + h) + 64]
                    b2 = ts(o_, o_, dnr[:, 8 + 2 * h + c:9 + 2 * h + c], None, ALU.mult, None, [b])
                head_done(8 + h, b2)

        dnr = lamt[:, 70:86]
        for _ in proj_a():
            pass
        lam_part()
        blend(Q, [moba_head(h) for h in range(4)], 4, [proj_b()])
        biases(2, BI, C("dmc"), DS, Q.now())
        ringA = Ring([banks[0], banks[1]])
        ringB = Ring([banks[i] for i in (2, 3, 4, 5, 6, 7)])
        blend(Q, [nsa_cmp()] + [nsa_head(h) for h in range(4)], 5, [proj_c()])
        biases(3, BI2, C("dms"), 0.125, Q.now())
        ringB = Ring(ringB.slots + ringA.slots)
        blend(Q, [x for h in range(4) for x in (diff_head(h), swa_head(h))], 4)
        diff_norm()
        ringA = Ring([banks[i] for i in (0, 1, 2, 3)])
        t_h = out_proj(lambda k: MIh[:, k, :], lambda k: MIl[:, k, :], lambda k: tMI[k], "attn_post")
        t_u2 = norm2("ffn_pre2", t_h)

        cw = S_("conv_w").rearrange("p (i n) -> p i n", i=3)

        def hidden2(i, bg, tg, bu, tu, s):
            g = bg.ap
            c = s.ap[0]
            b = ts(c, g[:, 0:256], cw[:, 2, i:i + 1], sc("conv_b", i), ALU.mult, ALU.add, [tg, s.free])
            b = stt(c[:, 1:256], g[:, 0:255], cw[:, 1, i:i + 1], c[:, 1:256], ALU.mult, ALU.add, [b])
            b = stt(c[:, 2:256], g[:, 0:254], cw[:, 0, i:i + 1], c[:, 2:256], ALU.mult, ALU.add, [b])
            give(bg, b)
            a = act(c, c, ACT.Gelu_apprx_tanh, [b])
            b = tt(s.ap[1], c, bu.ap[:, 0:256], ALU.mult, [a, tu])
            give(bu, b)
            return b

        t_x3 = ffn(HID2, t_u2, hidden2, "ffn_post2")
        s_out = ctx.enter_context(nc.semaphore("s_out"))
        for c in range(2):
            dst, src = dr["out"][0, 128 * c:128 * c + 128, :], X[:, 1024 * c:1024 * c + 1024]
            Q.op(SP, lambda e, dst=dst, src=src: e.dma_start(dst, src), [t_x3[c][1]], sem=s_out, val=16 * c + 16)
        assert cur[0] == len(BLOCKS), (cur[0], len(BLOCKS))

        Q.count()
        block = ctx.enter_context(nc.Block())

        @block.sync
        def _(e):
            Q.emit("sp", e)
            e.wait_ge(s_out, 32)

        @block.tensor
        def _(e):
            Q.emit("pe", e)

        @block.scalar
        def _(e):
            Q.emit("act", e)

        @block.vector
        def _(e):
            Q.emit("dve", e)

        @block.gpsimd
        def _(e):
            Q.emit("pool", e)


def kernel(**inputs):
    import concourse.bacc as bacc
    from concourse.bass_utils import run_bass_kernel_spmd as run

    I = {k: np.asarray(v) for k, v in inputs.items()}
    f = np.float32
    mats = {n: I[n][0] for n in ("w_in", "w_hg_o", "w_q_b", "w_kv_b", "w_mla_o", "w_out", "w_ffn_in", "w_ffn_out",
                                 "w_in_2", "w_out_2", "ffn_w_gate_2", "ffn_w_up_2", "ffn_w_down_2")}
    W = np.zeros((NSLAB, 128, SLABW), f)
    for i, (n, r, cols) in enumerate(BLOCKS):
        keep = [c for c in cols if c >= 0]
        W[i // 16, :, 128 * (i % 16):128 * (i % 16) + len(keep)] = mats[n][r:r + 128][:, keep]
    sm = np.zeros((128, NSM), f)

    def put(n, v, p=slice(0, 128)):
        sm[p, SM[n][0]:SM[n][0] + SM[n][1]] = v

    def colv(v, n):
        return np.reshape(v, (n, 128)).T

    put("mix_pre", colv(I["mix_pre_g"], 8))
    put("ffn_pre", colv(I["ffn_pre_g"], 8))
    put("attn_pre", colv(I["attn_pre_norm_2"], 8))
    put("ffn_pre2", colv(I["ffn_pre_norm_2"], 8))
    put("b_gate", colv(I["b_gate"], 16))
    put("lb0", colv(I["lb_logits"][0], 8))
    put("lb1", colv(I["lb_logits"][1], 8))
    put("hg_g", colv(I["hg_norm_g"], 1))
    put("q_g", colv(I["q_a_norm_g"], 2))
    put("kv_g", colv(I["kv_a_norm_g"], 2))
    put("conv_w", np.concatenate([colv(I["ffn_conv_w_2"][0, i], 32) for i in range(3)], 1))
    put("conv_b", colv(I["ffn_conv_b_2"], 32))
    put("cmp_b1", np.stack([I["nsa_cmp_b1_k_2"][0], I["nsa_cmp_b1_v_2"][0]], 1))
    put("cmp_pos", I["nsa_cmp_pos_k_2"][0].T, slice(0, 64))
    put("cmp_pos", I["nsa_cmp_pos_v_2"][0].T, slice(64, 128))
    put("w2k", np.concatenate([I["nsa_cmp_w2_k_2"][0]] * 2, 1))
    put("w2v", I["nsa_cmp_w2_v_2"][0])
    put("subln", I["diff_subln_2"][0][None])
    put("lam", np.concatenate([I[n][0] for n in ("diff_lambda_q1_2", "diff_lambda_k1_2", "diff_lambda_q2_2",
                                                 "diff_lambda_k2_2")])[None])
    put("sinks", I["swa_sinks_2"][0][None])
    w1 = np.zeros((4, 128, 1024), f)
    for q in range(4):
        for half, n in enumerate(("nsa_cmp_w1_k_2", "nsa_cmp_w1_v_2")):
            w1[q, 64 * half:64 * half + 64] = I[n][0][8 * q:8 * q + 8].transpose(1, 0, 2).reshape(64, 1024)
    cst, lev = constants()
    arrays = {"x": I["x"], "meta": I["meta_tokens"], "cst": cst, "lev": lev, "sm": sm, "w": W, "w1": w1}
    for n, k in (("mix_post", "mix_post_g"), ("ffn_post", "ffn_post_g"), ("attn_post", "attn_post_norm_2"),
                 ("ffn_post2", "ffn_post_norm_2")):
        arrays[n] = np.ascontiguousarray(np.broadcast_to(I[k][0][None], (128, D)))
    nc = bacc.Bacc("TRN2", target_bir_lowering=False, num_devices=1)
    dr, sent = {}, {}
    for n, a in arrays.items():
        a = np.ascontiguousarray(a)
        sent["in_" + n] = a
        dr[n] = nc.dram_tensor("in_" + n, a.shape, mybir.dt.from_np(a.dtype), kind="ExternalInput").ap()
    dr["out"] = nc.dram_tensor("out_0", (1, 256, D), FP, kind="ExternalOutput").ap()
    program(nc, dr)
    r = run(nc, [sent], core_ids=[0])
    return r.results[0]["out_0"]
```

```python
import numpy as np
import concourse.bass as bass
from concourse import mybir
from concourse.alu_op_type import AluOpType as ALU
from contextlib import ExitStack

FP = mybir.dt.float32
FR = mybir.dt.float32r
U8 = mybir.dt.uint8
ACT = mybir.ActivationFunctionType
AX = mybir.AxisListType

D = 1024
NM = 16
T1 = 272
HID1 = 22
HID2 = 32
LAG = 3
EPS = 1e-6
NEG = -1e30
NRAW = 3
NUNIT = 4
SLABW = 2048
IN1 = dict(hq=0, hf=1024, hi=2048, hg=3072, cq=4096, ckv=4352, kpe=4608, gate=4672)
_o2 = np.cumsum([0, 256, 256, 256, 256, 64, 64, 64, 64, 64, 64, 12, 256, 256, 256, 256, 128, 128])
IN2 = dict(zip(["mq", "mk", "mv", "nq", "nkc", "nvc", "nks", "nvs", "nkw", "nvw", "ng",
                "dq", "dk", "dv", "sq", "sk", "sv"], [int(v) for v in _o2]))
SLOPES = [float(v) for v in
          np.power(np.float32(2.0), np.arange(1, 17, dtype=np.float32) * np.float32(-0.5))]



KORD2 = [0, 1, 2, 3, 4, 5, 6, 7]


def stream_blocks():
    b = []

    def a_tile(name, kt, cols):
        for k in range(kt):
            b.append((name, 128 * k, list(cols)))

    def rng(o, n=128):
        return list(range(o, o + n))

    w = "w_in"
    for n in range(8):
        a_tile(w, 8, rng(IN1["hf"] + 128 * n))
    for nh in range(2):
        for k in range(8):
            for j in range(4):
                b.append((w, 128 * k, rng(IN1["hi"] + 512 * nh + 128 * j)))
    for n in range(8):
        a_tile(w, 8, rng(IN1["hq"] + 128 * n))
    for n in range(8):
        a_tile(w, 8, rng(IN1["hg"] + 128 * n))
    kp = rng(IN1["kpe"], 64)
    sw = kp[32:] + kp[:32]
    for n in range(2):
        a_tile(w, 8, rng(IN1["ckv"] + 128 * n))
    a_tile(w, 8, kp + kp)
    a_tile(w, 8, sw + sw)
    for n in range(2):
        a_tile(w, 8, rng(IN1["cq"] + 128 * n))
    for n in range(8):
        a_tile(w, 8, rng(IN1["gate"] + 128 * n))
    for n in range(8):
        a_tile("w_kv_b", 2, rng(256 * n))
    for nh in range(2):
        for k in range(2):
            for j in range(4):
                b.append(("w_kv_b", 128 * k, rng(256 * (4 * nh + j) + 128)))
    for n in range(8):
        a_tile("w_q_b", 2, rng(192 * n))
    for n in range(4):
        p0 = rng(192 * 2 * n + 128, 64)
        p1 = rng(192 * (2 * n + 1) + 128, 64)
        a_tile("w_q_b", 2, p0 + p1)
        a_tile("w_q_b", 2, p0[32:] + p0[:32] + p1[32:] + p1[:32])
    for n in range(8, 16):
        a_tile(w, 8, rng(IN1["gate"] + 128 * n))
    for n in range(8):
        a_tile("w_hg_o", 8, rng(128 * n))
    for n in range(8):
        a_tile("w_mla_o", 8, rng(128 * n))
    for k in range(8):
        for j in range(8):
            b.append(("w_out", 128 * k, rng(128 * j)))

    def ffn(first, up_name, up_off, down, nt):
        for i in range(nt + LAG):
            if i < nt:
                a_tile(first, 8, rng(128 * i))
                a_tile(up_name, 8, rng(up_off + 128 * i))
            if i >= LAG:
                for j in range(8):
                    b.append((down, 128 * (i - LAG), rng(128 * j)))

    ffn("w_ffn_in", "w_ffn_in", 128 * HID1, "w_ffn_out", HID1)
    w = "w_in_2"
    o = IN2
    for n in range(2):
        a_tile(w, 8, rng(o["mq"] + 128 * n))
    for n in range(2):
        a_tile(w, 8, rng(o["mk"] + 128 * n))
    for k in range(8):
        for c in (o["mv"], o["mv"] + 128, o["dv"], o["dv"] + 128):
            b.append((w, 128 * k, rng(c)))
    a_tile(w, 8, rng(o["nkc"]))
    for n in range(2):
        a_tile(w, 8, rng(o["nq"] + 128 * n))
    for k in range(8):
        b.append((w, 128 * k, rng(o["nvs"], 64) + rng(o["nvw"], 64)))
        b.append((w, 128 * k, rng(o["sv"])))
        b.append((w, 128 * k, rng(o["ng"], 12) + [-1] * 116))
        b.append((w, 128 * k, rng(o["nks"], 64) + rng(o["nkw"], 64)))
    for c in (o["dq"], o["dq"] + 128, o["dk"], o["dk"] + 128, o["sq"], o["sq"] + 128, o["sk"]):
        a_tile(w, 8, rng(c))
    for k in KORD2:
        for j in range(8):
            b.append(("w_out_2", 128 * k, rng(128 * j)))
    ffn("ffn_w_gate_2", "ffn_w_up_2", 0, "ffn_w_down_2", HID2)
    return b


BLOCKS = stream_blocks()
NSLAB = -(-len(BLOCKS) // 16)

SM = {}
_at = 0
for _n, _w in [("mix_pre", 8), ("ffn_pre", 8), ("attn_pre", 8), ("ffn_pre2", 8), ("b_gate", 16),
               ("lb0", 8), ("lb1", 8), ("hg_g", 1), ("q_g", 2), ("kv_g", 2), ("conv_w", 96),
               ("conv_b", 32), ("cmp_b1", 2), ("cmp_pos", 32), ("w2k", 128), ("w2v", 64),
               ("subln", 64), ("lam", 128), ("sinks", 4)]:
    SM[_n] = (_at, _w)
    _at += _w
NSM = _at

CO = {}
_at = 0
for _n, _w in [("ident", 128), ("ones", 128), ("esel", 16), ("cos", T1), ("sin", T1),
               ("m1", T1), ("dmc", 256), ("dms", 256), ("cmpb", 120)]:
    CO[_n] = (_at, _w)
    _at += _w
NCO = _at


def constants():
    c = np.zeros((128, NCO), np.float32)

    def put(n, v):
        c[:, CO[n][0]:CO[n][0] + CO[n][1]] = v

    p = np.arange(128)
    put("ident", np.eye(128))
    put("ones", 1.0)
    e = np.zeros((128, 16))
    e[:, 8] = 1.0
    put("esel", e)
    inv = (np.float32(1.0) / (np.float32(10000.0) ** (np.arange(0, 64, 2, dtype=np.float32) / np.float32(64))))
    ang = (np.arange(T1, dtype=np.float32)[:, None] * inv[None, :].astype(np.float32)).astype(np.float32)
    cs, sn = np.cos(ang).astype(np.float32), np.sin(ang).astype(np.float32)
    put("cos", cs.T[p % 32])
    put("sin", sn.T[p % 32] * np.where((p % 64) < 32, -1.0, 1.0)[:, None])
    q = p[:, None] + NM
    put("m1", np.where(np.arange(T1)[None] <= q + 128, 0.0, NEG))
    d = p[:, None] + 128 - np.arange(256)[None]
    put("dmc", np.where(d >= 0, -d, NEG))
    put("dms", np.where((d >= 0) & (d < 128), -d, NEG))
    cb = np.zeros((128, 2, 4, 15))
    end = np.arange(15) * 16 + 31
    for t in range(2):
        for h in range(4):
            dist = (p[:, None] + 128 * t) - end[None]
            cb[:, t, h] = np.where(dist >= 0, -SLOPES[1 + 4 * h] * dist * 8.0, NEG)
    put("cmpb", cb.reshape(128, 120))
    lev = np.zeros((128, 5, 64), np.float32)
    s, t = p[:, None], p[None]
    for j in range(5):
        m = ((s >> (j + 1)) == (t >> (j + 1))) & (((s >> j) & 1) == 0)
        lev[:, j] = m[:, ((p >> j) & 1) == 1]
    return c, lev.reshape(128, 320)


class Tok:

    def __init__(self, eng, fn, after, sem=None, val=0):
        self.eng, self.fn, self.after = eng, fn, after
        self.sem, self.val, self.used, self.inc = sem, val, sem is not None, 16 if sem is not None else 1
        self.end = 0.0


def flat(x):
    if x is None:
        return []
    if isinstance(x, Tok):
        return [x]
    out = []
    for y in x:
        out += flat(y)
    return out


class Queues:

    LATE = {("pe", "dve"): 400.0, ("pe", "act"): 250.0, ("act", "pe"): 280.0, ("dve", "pe"): 260.0,
            ("act", "dve"): 142.0, ("dve", "act"): 128.0}

    def __init__(self, sems):
        self.beside = False
        self.q = {e: [] for e in ("pe", "act", "dve", "pool", "sp")}
        self.sems = sems
        self.clock = {e: 0.0 for e in ("pe", "act", "dve", "pool", "sp", "dma")}
        self.step_end = 0.0
        self.gate = {}

    def when(self, eng, after, cost):
        return max([self.clock[eng]] + [a.end + self.LATE.get((a.eng, eng), 70.0) for a in flat(after)]) + cost

    def op(self, eng, fn, after=(), sem=None, val=0, cost=0.0):
        t = Tok(eng, fn, flat(after) + ([self.gate.pop(eng)] if eng in self.gate else []), sem, val)
        if sem is None:
            t.end = self.clock[eng] = self.when(eng, t.after, cost)
        else:
            first = self.when("sp", t.after, 60.0)
            self.clock["dma"] = max(self.clock["dma"], first) + cost
            t.end = self.clock["dma"] + 1500.0
        self.step_end = max(self.step_end, t.end)
        for a in t.after:
            a.used = True
        self.q[eng].append(t)
        return t

    def now(self):
        return [self.q[e][-1] for e in ("pe", "act", "dve", "pool") if self.q[e]]

    def count(self):
        for e, q in self.q.items():
            n = 0
            for t in q:
                if t.inc == 1 and t.used:
                    n += 1
                    t.sem, t.val = self.sems[e], n

    def emit(self, name, eng):
        seen = {}
        for t in self.q[name]:
            need = {}
            for a in t.after:
                if a.sem.name not in need or need[a.sem.name][1] < a.val:
                    need[a.sem.name] = (a.sem, a.val)
            for k, (s, v) in need.items():
                if seen.get(k, 0) < v:
                    eng.wait_ge(s, v)
                    seen[k] = v
            ins = t.fn(eng)
            if t.used:
                ins.then_inc(t.sem, t.inc)


class Slot:

    def __init__(self, ap):
        self.ap, self.free, self.busy = ap, [], False


class Ring:
    def __init__(self, slots):
        self.slots, self.n = slots, 0

    def idle(self):
        return sum(not s.busy for s in self.slots)

    def get(self):
        idle = [s for s in self.slots if not s.busy]
        assert idle, "every slot is taken"
        s = min(idle, key=lambda x: (max([t.end for t in x.free], default=0.0), self.slots.index(x)))
        s.busy = True
        return s


def give(s, *toks):
    s.free, s.busy = flat(toks), False


def blend(Q, jobs, width, fill=()):
    jobs, fill = list(jobs), list(fill)
    live = []
    Q.beside = True
    while jobs or live or fill:
        while jobs and len(live) < width:
            live.append([0.0, jobs.pop(0)])
        if live:
            live.sort(key=lambda x: x[0])
            if fill and live[0][0] > Q.clock["pe"] + 100.0:
                try:
                    if next(fill[0]) is None:
                        continue
                except StopIteration:
                    fill.pop(0)
                    continue
            item = live[0]
            Q.step_end = 0.0
            try:
                next(item[1])
                item[0] = max(Q.step_end, item[0] + 1.0)
            except StopIteration:
                live.remove(item)
        elif fill:
            Q.beside = False
            try:
                next(fill[0])
            except StopIteration:
                fill.pop(0)
    Q.beside = False


def program(nc, dr):
    ctx = ExitStack()
    with ctx:
        def sb(name, cols, dt=FP):
            return ctx.enter_context(nc.sbuf_tensor(name, [128, cols], dt))

        Q = Queues({e: ctx.enter_context(nc.semaphore("done_" + e)) for e in ("pe", "act", "dve", "pool", "sp")})
        PE, AC, DV, PO, SP = "pe", "act", "dve", "pool", "sp"

        def size(ap):
            n = 1
            for v in ap.shape[1:]:
                n *= v
            return n

        def mm(out, l, r, start, stop, after=(), skip=False):
            c = max(size(r), size(l)) / 2.4 * (1 if l.dtype == FR else 4)
            return Q.op(PE, lambda e: e.matmul(out, l, r, start=start, stop=stop, skip_group_check=skip), after, cost=c)

        def tr(out, i, after=()):
            k = i.shape[0]
            return Q.op(PE, lambda e: e.transpose(out, i, ident[0:k, 0:k]), [after, t_id], cost=109.0)

        def dcost(out, eng=DV, rate=1.04):
            return 90.0 + size(out) * (rate if eng == DV else 2.3)

        def tt(out, a, b, op, after=(), eng=DV):
            return Q.op(eng, lambda e: e.tensor_tensor(out, a, b, op), after, cost=dcost(out, eng))

        def ts(out, a, s1, s2, op0, op1=None, after=(), eng=DV):
            c = dcost(out, eng)
            if op1 is None:
                return Q.op(eng, lambda e: e.tensor_scalar(out, a, s1, None, op0), after, cost=c)
            return Q.op(eng, lambda e: e.tensor_scalar(out, a, s1, s2, op0, op1), after, cost=c)

        def stt(out, a, s, b, op0, op1, after=()):
            return Q.op(DV, lambda e: e.scalar_tensor_tensor(out, a, s, b, op0, op1), after, cost=dcost(out))

        def ttr(out, a, b, op0, op1, init, acc, after=()):
            return Q.op(DV, lambda e: e.tensor_tensor_reduce(out=out, in0=a, in1=b, scale=1.0, scalar=init,
                                                             op0=op0, op1=op1, accum_out=acc), after,
                        cost=dcost(out) + 60)

        def red(out, a, op, after=()):
            return Q.op(DV, lambda e: e.tensor_reduce(out, a, AX.X, op), after, cost=dcost(a))

        def vcp(out, a, after=()):
            return Q.op(DV, lambda e: e.tensor_copy(out, a), after, cost=dcost(out))

        def rcp(out, a, after=()):
            return Q.op(DV, lambda e: e.reciprocal(out, a), after, cost=dcost(out, rate=8.3))

        def act(out, a, f, after=(), bias=0.0, scale=1.0, acc=None):
            return Q.op(AC, lambda e: e.activation(out, a, f, bias=bias, scale=scale, accum_out=acc), after,
                        cost=(95.0 if acc is None else 280.0) + 0.833 * size(a))

        def acp(out, a, after=(), scale=1.0):
            return act(out, a, ACT.Copy if isinstance(scale, float) else ACT.Identity, after, scale=scale)

        def cp(out, a, after=()):
            f = vcp if Q.when(DV, after, 90.0 + 1.04 * size(a)) < Q.when(AC, after, 95.0 + 0.833 * size(a)) else acp
            return f(out, a, after)

        def load(dst, src, after=(), eng=SP):
            s = ctx.enter_context(nc.semaphore(f"ld{len(loads)}"))
            loads.append(s)
            return Q.op(eng, lambda e: e.dma_start(dst, src), after, sem=s, val=16, cost=1500.0)

        loads = []

        def rf(ap):
            return ap.bitcast(FP)

        cst = sb("cst", NCO)
        lev = sb("lev", 320, U8)
        sm = sb("sm", NSM)
        st = sb("st", 256)
        post = sb("post", 1024)
        X = sb("X", 2048)
        raw = [sb(f"raw{i}", SLABW) for i in range(NRAW)]
        WH = [sb(f"wh{i}", 1024, FR) for i in range(NUNIT)]
        WL = [sb(f"wl{i}", 1024, FR) for i in range(NUNIT)]
        R1 = sb("R1", 2 * 8 * T1, FR)
        R2 = sb("R2", 4096, FR)
        R3 = sb("R3", 4096, FR)
        NFA = 19104
        FA = sb("FA", NFA)
        banks = [Slot(ctx.enter_context(nc.psum_tensor(f"pb{i}", [128, 512], FP))) for i in range(8)]

        def C(n):
            return cst[:, CO[n][0]:CO[n][0] + CO[n][1]]

        def S_(n):
            return sm[:, SM[n][0]:SM[n][0] + SM[n][1]]

        def sc(n, i):
            return sm[:, SM[n][0] + i:SM[n][0] + i + 1]

        ident = C("ident")
        ones = C("ones")

        def fa(off, n, p=128):
            assert off + n <= NFA, (off, n)
            return FA[0:p, off:off + n]

        stn = [0]

        def stat(n=1):
            if stn[0] + n > 256:
                stn[0] = 0
            stn[0] += n
            return st[:, stn[0] - n:stn[0]]

        t_x = [load(X[:, 1024 * c:1024 * c + 1024], dr["x"][0, 128 * c:128 * c + 128, :]) for c in range(2)]
        XM = fa(0, 1024, 16)
        t_xm = load(XM, dr["meta"])
        t_id = load(cst[:, 0:128], dr["cst"][:, 0:128])
        t_sm = load(sm[:, :], dr["sm"])
        t_cst = []

        NU = 2 * NSLAB
        slab_sem = [ctx.enter_context(nc.semaphore(f"slab{i}")) for i in range(NRAW)]
        slab_tok, split_tok, unit_free = {}, {}, {}

        def load_slab(s):
            if s >= NSLAB:
                return
            after = [split_tok[2 * (s - NRAW)], split_tok[2 * (s - NRAW) + 1]] if s >= NRAW else []
            dst, src = raw[s % NRAW][:, :], dr["w"][s]
            slab_tok[s] = Q.op(SP, lambda e: e.dma_start(dst, src), after,
                               sem=slab_sem[s % NRAW], val=16 * (s // NRAW + 1), cost=2900.0)

        def split(u, eng=DV, first=AC):
            if u >= NU:
                return
            s, h = u // 2, u % 2
            r = raw[s % NRAW][:, 1024 * h:1024 * h + 1024]
            hi, lo = WH[u % NUNIT][:, :], WL[u % NUNIT][:, :]
            w = [slab_tok[s], unit_free.get(u - NUNIT)]
            if first == DV or Q.when(AC, w, 1050.0) > Q.when(DV, w, 620.0) + 500.0:
                a = Q.op(DV, lambda e: e.tensor_copy(hi, r), w, cost=620.0)
            else:
                a = act(hi, r, ACT.Copy, w)
            if eng == DV and Q.when(DV, [a], 1150.0) > Q.when(PO, [a], 2450.0) + (-1500.0 if Q.beside else 500.0):
                eng = PO
            b = tt(lo, r, rf(hi), ALU.subtract, [a], eng)
            split_tok[u] = [a, b]
            if h == 1:
                load_slab(s + NRAW)

        for s in range(NRAW):
            load_slab(s)
        t_cst.append(load(cst[:, 128:NCO], dr["cst"][:, 128:NCO]))
        t_lev = load(fa(5120, 320), dr["lev"])
        cur = [0]

        def take(n=1):
            i = cur[0]
            u, o = i // 8, i % 8
            assert o + n <= 8
            cur[0] += n
            sl = slice(128 * o, 128 * o + 128 * n)
            return WH[u % NUNIT][:, sl], WL[u % NUNIT][:, sl], split_tok[u], (u if o + n == 8 else None)

        def done(u, tok, eng=DV, first=AC):
            if u is not None:
                unit_free[u] = [tok]
                split(u + NUNIT, eng, first)

        def prod3(out, lh, ll, rh, rl, first, last, after, skip=False):
            mm(out, lh, rh, first, False, after, skip)
            mm(out, lh, rl, False, False, (), skip)
            return mm(out, ll, rh, False, last, (), skip)

        def gemm_a(ntiles, kt, act_h, act_l, T, ready, evac, ring):
            for n in range(ntiles):
                bk = ring.get()
                for k in range(kt):
                    wh, wl, wt, end = take()
                    t = prod3(bk.ap[:, 0:T], wh, wl, act_h(k), act_l(k), k == 0, k == kt - 1,
                              [wt, bk.free if k == 0 else None, ready(k)])
                    done(end, t)
                    if k == 3 and kt == 8:
                        yield
                evac(n, bk, t)
                yield

        def rstd(ssq, dim, after, p=128, n=1):
            v = stat(n)[0:p]
            r = stat(n)[0:p]
            a = ts(v, ssq, 1.0 / dim, EPS, ALU.mult, ALU.add, after)
            a = act(v, v, ACT.Sqrt, [a])
            return r, rcp(r, v, [a])

        def split_act(val, h, l, after, scale=1.0):
            a = acp(h, val, after, scale)
            if isinstance(scale, float) and scale == 1.0:
                b = tt(l, val, rf(h), ALU.subtract, [a])
            else:
                b = stt(l, val, scale, rf(h), ALU.mult, ALU.subtract, [a])
            return a, b

        def xnorm(x, y, p, ss, rdy):
            r, b = rstd(ss, D, [rdy], p)
            return [acp(y[:, 0:512], x[:, 0:512], [b], r),
                    ts(y[:, 512:1024], x[:, 512:1024], r, None, ALU.mult, None, [b])]

        def prenorm(tiles, gain, UH, UL, T):
            bks = [ringAll.get() for _ in range(8)]
            for y, c0, p, rdy in tiles[:-1]:
                for k, bk in enumerate(bks):
                    tr(bk.ap[:, c0:c0 + p], y[:, 128 * k:128 * k + 128], [rdy[k // 4], bk.free])
            y, c0, p, rdy = tiles[-1]
            out = []
            for k, bk in enumerate(bks):
                t = tr(bk.ap[:, c0:c0 + p], y[:, 128 * k:128 * k + 128], [rdy[k // 4]])
                a, b = split_act(bk.ap[:, 0:T], UH(k), UL(k), [t, t_sm], sc(gain, k))
                give(bk, b)
                out.append([a, b])
            return out

        def post_a(c, banks_c, t_acc, gtok, free):
            y = [fa(1024 * c, 512), fa(1024 * c + 512, 512)]
            s2 = stat(2)
            a, z, w = [None, None], [None, None], [t_acc, free]
            for h in range(2):
                a[h] = act(fa(6144 + 512 * (2 * c + h), 512), banks_c[h].ap[:, :], ACT.Square, [w, z[h]], acc=s2[:, h:h + 1])
                z[1 - h] = tt(y[1 - h], banks_c[1 - h].ap[:, :], post[:, 512 * (1 - h):512 * (2 - h)], ALU.mult,
                              [w, gtok, a[1 - h]])
            for h in range(2):
                give(banks_c[h], a[h], z[h])
            s1 = stat()
            b = tt(s1, s2[:, 0:1], s2[:, 1:2], ALU.add, a)
            r, b = rstd(s1, D, [b])
            return y, z, r, b

        def post_b(c, y, z, r, b, last, between):
            q2, q1 = stat(2), stat()
            xs = [X[:, 1024 * c + 512 * h:1024 * c + 512 * h + 512] for h in range(2)]
            t = [stt(xs[h], y[h], r, xs[h], ALU.mult, ALU.add, [z[h], b]) for h in range(2)]
            done(*between, PO, DV)
            if last:
                return t
            sq = [act(fa(8192 + 512 * (2 * c + h), 512), xs[h], ACT.Square, [t[h]], acc=q2[:, h:h + 1]) for h in range(2)]
            b = tt(q1, q2[:, 0:1], q2[:, 1:2], ALU.add, sq)
            return xnorm(X[:, 1024 * c:1024 * c + 1024], fa(2048 + 1024 * c, 1024), 128, q1, b)

        def set_sqrt():
            v = stat()
            b = Q.op(DV, lambda e: e.memset(v, 1.0), cost=70.0)
            act(v, v, ACT.Sqrt, [b])

        def sumsq(x, y, p, rdy):
            ss = stat()[0:p]
            return ss, [act(y, x, ACT.Square, [rdy], acc=ss)]

        ringAll = Ring(banks)

        ringA = Ring(banks)
        UH1 = R1[:, 0:8 * T1].rearrange("p (k t) -> p k t", k=8)
        UL1 = R1[:, 8 * T1:16 * T1].rearrange("p (k t) -> p k t", k=8)
        x0, x1 = X[:, 0:1024], X[:, 1024:2048]
        xn = [fa(1024, 1024, 16), fa(2048, 1024), fa(3072, 1024)]
        set_sqrt()
        n0 = xnorm(x0, xn[1], 128, *sumsq(x0, xn[1], 128, t_x[0]))
        sx1 = stat()
        t_s1 = ttr(xn[2], x1, x1, ALU.mult, ALU.add, 0.0, sx1, [t_x[1]])
        sxm = sumsq(XM, xn[0], 16, t_xm)
        n1 = xnorm(x1, xn[2], 128, sx1, t_s1)
        nm = xnorm(XM, xn[0], 16, *sxm)
        split(0, PO, DV)
        t_u = prenorm([(xn[1], 16, 128, n0), (xn[2], 144, 128, n1), (xn[0], 0, 16, nm)], "mix_pre",
                      lambda k: UH1[:, k, :], lambda k: UL1[:, k, :], T1)
        u_done = t_u
        for u in range(1, NUNIT):
            split(u)
        t_lev = Q.op(PO, lambda e: e.tensor_copy(lev[:, :], fa(5120, 320)), [t_lev])

        o = 0
        Fr = fa(o, 2048).rearrange("p (h t) -> p h t", h=8); oF = o; o += 2048
        Kr = fa(o, 2048).rearrange("p (h t) -> p h t", h=8); oK = o; o += 2048
        Qr = fa(o, 2048).rearrange("p (h t) -> p h t", h=8); oQ = o; o += 2048
        SG = fa(o, 2048).rearrange("p (h t) -> p h t", h=8); o += 2048
        Vt = fa(o, 2048).rearrange("p (c n) -> p c n", c=2); oV = o; o += 2048
        AT = fa(o, 2048).rearrange("p (x t) -> p x t", x=16); oA = o; o += 2048
        Vm = fa(o, 1024, 16); o += 1024
        KT = fa(o, 1024); KmT = fa(o, 1024, 16); o += 1024
        Fm = fa(o, 128).rearrange("p (h t) -> p h t", h=8); o += 128
        Km = fa(o, 128).rearrange("p (h t) -> p h t", h=8); o += 128
        Tt = [None] + [fa(o + 2048 - (4096 >> j), 2048 >> j) for j in range(1, 8)]; o += 2048
        sgr = Ring([Slot(Tt[1][:, i * T1:(i + 1) * T1]) for i in range(3)])
        lbt = fa(o, 24); o += 24
        assert o <= NFA

        mxl, e0, e1 = lbt[:, 0:8], lbt[:, 8:16], lbt[:, 16:24]
        a = tt(mxl, S_("lb0"), S_("lb1"), ALU.max, [t_sm])
        a = [tt(e0, S_("lb0"), mxl, ALU.subtract, [a]), tt(e1, S_("lb1"), mxl, ALU.subtract, [a])]
        a = act(lbt[:, 8:24], lbt[:, 8:24], ACT.Exp, a)
        a = tt(e1, e0, e1, ALU.add, [a])
        a = rcp(e1, e1, [a])
        a = tt(e0, e0, e1, ALU.mult, [a])
        t_lb = ts(e1, e0, -1.0, 1.0, ALU.mult, ALU.add, [a])

        tF, tK, tKm, tQ, tG = {}, {}, {}, {}, {}
        first_f = [u_done, Q.now()]

        def ev_f(n, bk, t):
            s = sgr.get()
            a = act(s.ap, bk.ap[:, 0:T1], ACT.Sigmoid, [t, s.free, first_f])
            give(bk, a)
            b1 = ts(Fr[:, n, :], s.ap[:, NM:T1], e1[:, n:n + 1], e0[:, n:n + 1], ALU.mult, ALU.add, [a, t_lb, first_f])
            b2 = ts(Fm[:, n, :], s.ap[:, 0:NM], e1[:, n:n + 1], e0[:, n:n + 1], ALU.mult, ALU.add)
            b3 = ts(Kr[:, n, :], Fr[:, n, :], -1.0, 1.0, ALU.mult, ALU.add, [b1])
            b4 = ts(Km[:, n, :], Fm[:, n, :], -1.0, 1.0, ALU.mult, ALU.add, [b2])
            give(s, b2)
            tF[n], tK[n], tKm[n] = b2, b3, b4

        UHk, ULk = (lambda k: UH1[:, k, :]), (lambda k: UL1[:, k, :])
        UHr, ULr = (lambda k: UH1[:, k, NM:T1]), (lambda k: UL1[:, k, NM:T1])
        ready_u = lambda k: t_u[k]
        for _ in gemm_a(8, 8, UHk, ULk, T1, ready_u, ev_f, ringA):
            pass
        for e_ in (PE, AC, DV, PO):
            Q.gate[e_] = t_cst[0]
        tV = []
        for nh in range(2):
            bk = [ringA.get() for _ in range(3)]
            cols = [(0, 128), (16, 128), (144, 128)]
            for k in range(8):
                wh, wl, wt, end = take(4)
                for i, (c0, m) in enumerate(cols):
                    t = prod3(bk[i].ap[:, :], UH1[:, k, c0:c0 + m], UL1[:, k, c0:c0 + m], wh, wl, k == 0, k == 7,
                              [wt, bk[i].free])
                done(end, t)
            a = acp(Vm[:, 512 * nh:512 * nh + 512], bk[0].ap[0:16, :], [t, first_f])
            give(bk[0], a)
            for c in range(2):
                a = acp(Vt[:, c, 512 * nh:512 * nh + 512], bk[c + 1].ap[:, :], [t, first_f])
                give(bk[c + 1], a)
            tV.append(a)

        def ev_silu(dst, tks):
            def ev(n, bk, t):
                a = act(dst[:, n, :], bk.ap[:, 0:256], ACT.Sigmoid, [t])
                b = tt(dst[:, n, :], bk.ap[:, 0:256], dst[:, n, :], ALU.mult, [a])
                give(bk, b)
                tks[n] = b
            return ev

        for _ in gemm_a(8, 8, UHr, ULr, 256, ready_u, ev_silu(Qr, tQ), ringA):
            pass

        ringB = Ring([banks[i] for i in (4, 5, 6, 7)])
        ringA = Ring([banks[i] for i in (0, 1, 2)])
        bSSQ = banks[3]
        S1 = fa(oF, 1024)
        S2 = fa(oF + 1024, 1024)
        t_S1, t_S2, t_KT, t_Q7 = {}, {}, {}, {}
        ssq_bank = bSSQ.ap

        def half(ap, j):
            return ap.rearrange("p (b two s) -> p b two s", two=2, s=1 << j)

        def bcast(ap, n):
            p, b = ap.shape
            return ap.rearrange("p (b o) -> p b o", o=1).broadcast_to([p, b, n])

        def until(ok):
            while not ok():
                Q.step_end = Q.clock["pe"] + 300.0
                yield

        def meta_part():
            t = [tF[n] for n in range(8)] + [tKm[n] for n in range(8)]
            kf = Km.rearrange("p h t -> p (h t)")
            tot = Fm.rearrange("p h t -> p (h t)")
            for j in range(4):
                v = half(kf, j)
                tv = tot.rearrange("p (b two) -> p b two", two=2)
                w = tt(v[:, :, 0, :], v[:, :, 0, :], tv[:, :, 1:2].broadcast_to([128, v.shape[1], 1 << j]), ALU.mult, t)
                if j < 3:
                    nt = KT[:, 64 * j:64 * j + (64 >> j)]
                    t = [w, tt(nt, tv[:, :, 0], tv[:, :, 1], ALU.mult, t)]
                    tot = nt
                else:
                    t = [w]
                yield
            for g in range(2):
                bk = ringB.get()
                for i in range(4):
                    w = tr(bk.ap[0:16, 128 * i:128 * i + 128], Km[:, 4 * g + i, :], [t, bk.free])
                c = vcp(KmT[:, 512 * g:512 * g + 512], bk.ap[0:16, :], [w])
                give(bk, c)
                yield
                bk = ringB.get()
                for i in range(4):
                    h = 4 * g + i
                    w = mm(bk.ap[:, 128 * i:128 * i + 128], KmT[:, 128 * h:128 * h + 128], Vm[:, 128 * h:128 * h + 128],
                           True, True, [c, bk.free, tV])
                t_S1[g] = (bk, w)
                if g == 1:
                    m_dead.extend([w, c])
                yield

        def meta_store(g, after):
            bk, w = t_S1[g]
            c = vcp(S1[:, 512 * g:512 * g + 512], bk.ap[:, :], [w, after])
            give(bk, c)
            t_S1[g] = c

        def hgrn_group(g):
            hs = range(4 * g, 4 * g + 4)
            kf = Kr[:, 4 * g:4 * g + 4, :].rearrange("p h t -> p (h t)")
            qf = Qr[:, 4 * g:4 * g + 4, :].rearrange("p h t -> p (h t)")
            ff = Fr[:, 4 * g:4 * g + 4, :].rearrange("p h t -> p (h t)")
            tk, tq = [tK[h] for h in hs], [tQ[h] for h in hs]
            tot, ttot = ff, [tF[h] for h in hs]
            av = AT[:, 8 * g:8 * g + 8, :]
            last = None
            for lv in range(-1, 7):
                cps = []
                if lv < 0:
                    for b in range(2):
                        bk = ringB.get()
                        for i in range(4):
                            x = 4 * b + i
                            w = mm(bk.ap[:, 128 * i:128 * i + 128], kf[:, 128 * x:128 * x + 128],
                                   qf[:, 128 * x:128 * x + 128], True, True, [tk, tq, bk.free])
                        m = ident.rearrange("p (o t) -> p o t", o=1).broadcast_to([128, 4, 128])
                        c = tt(av[:, 4 * b:4 * b + 4, :], bk.ap[:, :].rearrange("p (x t) -> p x t", x=4), m,
                               ALU.mult, [w])
                        give(bk, c)
                        cps.append(c)
                else:
                    nb, sz = 64 >> lv, 1 << lv
                    qr = half(qf, lv)
                    bk = ringB.get()
                    for x in range(8):
                        m = 128 if lv < 5 else 128 - sz
                        w = mm(bk.ap[0:m, 64 * x:64 * x + 64], kf[:, 128 * x:128 * x + m],
                               qr[:, nb * x:nb * x + nb, 1, :], True, True, [tk, tq, bk.free])
                    src = bk.ap[:, :].rearrange("p (x b s) -> p x b s", x=8, b=nb)
                    dst = av.rearrange("p x (b two s) -> p x b two s", two=2, s=sz)
                    if lv < 5:
                        m = lev[:, 64 * lv:64 * lv + 64].rearrange("p (o b s) -> p o b s", o=1, b=nb)
                        m = m.broadcast_to([128, 8, nb, sz])
                        dd = dst[:, :, :, 1, :]
                        cps.append(Q.op(DV, lambda e, dd=dd, m=m, src=src: e.copy_predicated(dd, m, src),
                                        [w, t_lev, last], cost=602.0))
                    else:
                        for b in range(nb):
                            r0 = 2 * sz * b
                            cps.append(acp(av[r0:r0 + sz, :, r0 + sz:r0 + 2 * sz], src[r0:r0 + sz, :, b, :],
                                           [w, last]))
                    give(bk, cps)
                yield
                last = cps
                if lv < 0:
                    tq = [tt(qf, qf, ff, ALU.mult, [w, tq, ttot])]
                else:
                    j = lv
                    kv, qv = half(kf, j), half(qf, j)
                    tv = tot.rearrange("p (b two) -> p b two", two=2)
                    nb = kv.shape[1]
                    tk = [tt(kv[:, :, 0, :], kv[:, :, 0, :], tv[:, :, 1:2].broadcast_to([128, nb, 1 << j]), ALU.mult, [w, ttot, tk])]
                    tq = [tt(qv[:, :, 1, :], qv[:, :, 1, :], tv[:, :, 0:1].broadcast_to([128, nb, 1 << j]), ALU.mult, [w, ttot, tq])]
                    nt = Tt[j + 1][:, (1024 >> (j + 1)) * g:(1024 >> (j + 1)) * (g + 1)]
                    ttot = [tt(nt, tv[:, :, 0], tv[:, :, 1], ALU.mult, [ttot])]
                    tot = nt
                    if j == 0:
                        f_dead[g] = [tk, tq, ttot]
                        if len(f_dead) == 2:
                            while len(t_S1) < 2:
                                Q.step_end = Q.clock["pe"] + 300.0
                                yield
                            meta_store(0, [f_dead[0], f_dead[1]])
                            meta_store(1, [f_dead[0], f_dead[1]])
                yield
            bk = ringB.get()
            for i in range(4):
                w = tr(bk.ap[:, 128 * i:128 * i + 128], Kr[:, 4 * g + i, 0:128], [tk, bk.free])
            c = acp(KT[:, 512 * g:512 * g + 512], bk.ap[:, :], [w, list(m_dead)])
            give(bk, c)
            k_dead[g] = w
            yield
            bk = ringB.get()
            for i in range(4):
                h = 4 * g + i
                w = mm(bk.ap[:, 128 * i:128 * i + 128], KT[:, 128 * h:128 * h + 128], Vt[:, 0, 128 * h:128 * h + 128],
                       True, True, [c, bk.free])
            assert isinstance(t_S1[g], Tok)
            s2 = S2[:, 512 * g:512 * g + 512].rearrange("p (h v) -> p h v", h=4)
            s1 = S1[:, 512 * g:512 * g + 512].rearrange("p (h v) -> p h v", h=4)
            tv = tot.rearrange("p (h c) -> p h c", c=2)
            c = tt(s2, s1, tv[:, :, 0:1].broadcast_to([128, 4, 128]), ALU.mult, [ttot, t_S1[g], f_dead[0], f_dead[1]])
            c = tt(s2, s2, bk.ap[:, :].rearrange("p (h v) -> p h v", h=4), ALU.add, [c, w])
            give(bk, c)
            t_S2[g] = c
            t_Q7[g] = [tq, last]
            yield
            yield from hgrn_out(g)

        f_dead, k_dead, m_dead = {}, {}, []
        OT = Kr
        nsq = [0]
        tO, tSq = {}, {}

        def hgrn_out(g):
            while any(4 * g + i not in tG for i in range(4)):
                Q.step_end = Q.clock["pe"] + 500.0
                yield
            sqr = Slot(Tt[1][:, 512 * g:512 * g + 512])
            sqr.free = [t_S2[g], t_Q7[g]]
            for b in range(2):
                bk = ringB.get()
                for i in range(2):
                    h = 4 * g + 2 * b + i
                    for c in range(2):
                        dst = bk.ap[:, 256 * i + 128 * c:256 * i + 128 * c + 128]
                        mm(dst, Vt[:, c, 128 * h:128 * h + 128], AT[:, 2 * h + c, :], True, False, [bk.free, t_Q7[g], tV])
                        S = S1 if c == 0 else S2
                        w = mm(dst, S[:, 128 * h:128 * h + 128], Qr[:, h, 128 * c:128 * c + 128], False, True,
                               [t_S1[g], t_S2[g]])
                h0 = 4 * g + 2 * b
                sq = sqr
                a = act(sq.ap, bk.ap[:, :], ACT.Square, [w, sq.free])
                c = stt(OT[:, h0:h0 + 2, :].rearrange("p h t -> p (h t)"), bk.ap[:, :], sc("hg_g", 0),
                        SG[:, h0:h0 + 2, :].rearrange("p h t -> p (h t)"), ALU.mult, ALU.mult,
                        [a, tG[h0], tG[h0 + 1], k_dead[g]])
                give(bk, c)
                tO[h0] = c
                yield
                for i in range(2):
                    h = h0 + i
                    es = cst[:, CO["esel"][0] + 8 - h:CO["esel"][0] + 16 - h]
                    w = mm(ssq_bank[0:8, 0:256], es, sq.ap[:, 256 * i:256 * i + 256], nsq[0] == 0, nsq[0] == 7,
                           [a, bSSQ.free])
                    nsq[0] += 1
                give(sq, w)
                tSq[0] = w
                yield

        g1 = gemm_a(8, 8, UHr, ULr, 256, ready_u, ev_silu(SG, tG), ringA)
        CK = post[:, 0:2 * T1]
        CQ = sb("CQ", 512)
        KP = sb("KP", T1)
        tCK, tCQ, tKP = {}, {}, {}

        def ev_c(n, bk, t):
            if n < 2:
                a = acp(CK[:, T1 * n:T1 * n + T1], bk.ap[:, 0:T1], [t])
                give(bk, a)
                tCK[n] = a
            elif n == 2:
                b = tt(KP[:, :], bk.ap[:, 0:T1], C("cos"), ALU.mult, [t])
                give(bk, b)
                tKP[0] = b
            else:
                s = kps.get()
                b = tt(s.ap, bk.ap[:, 0:T1], C("sin"), ALU.mult, [t, s.free])
                give(bk, b)
                b = tt(KP[:, :], KP[:, :], s.ap, ALU.add, [b, tKP[0]])
                give(s, b)
                tKP[0] = b

        kps = Ring([Slot(post[:, 2 * T1:3 * T1])])

        def ev_cq(n, bk, t):
            a = acp(CQ[:, 256 * n:256 * n + 256], bk.ap[:, 0:256], [t])
            give(bk, a)
            tCQ[n] = a

        KN = fa(8192, 8 * T1).rearrange("p (h t) -> p h t", h=8)
        GA0 = fa(16672, 2048).rearrange("p (n t) -> p n t", n=8)
        GA1 = fa(10368, 2048).rearrange("p (n t) -> p n t", n=8)
        r8 = FA[0:8, 18848:19104]
        ringT = kps

        def latent_norm(src, T, n_t, gain, H, L, res):
            yield from until(lambda: len(n_t) == 2 and ringT.idle())
            s = ringT.get()
            sq = (s.ap, sq2)
            a = []
            for n in range(2):
                a.append(act(sq[n][:, 0:T], src[:, T * n:T * n + T], ACT.Square, [s.free, n_t[n], sq2_free]))
            yield
            yield from until(ringB.idle)
            bk = ringB.get()
            for n in range(2):
                w = mm(bk.ap[:, 0:T], ones, sq[n][:, 0:T], n == 0, n == 1, [a[n], bk.free])
            sq2_free.append(w)
            a = ts(s.ap[:, 0:T], bk.ap[:, 0:T], 1.0 / 256, EPS, ALU.mult, ALU.add, [w])
            give(bk, a)
            a = act(s.ap[:, 0:T], s.ap[:, 0:T], ACT.Sqrt, [a])
            yield
            a = rcp(s.ap[:, 0:T], s.ap[:, 0:T], [a])
            for n in range(2):
                v = src[:, T * n:T * n + T]
                b = stt(v, v, sc(gain, n), s.ap[:, 0:T], ALU.mult, ALU.mult, [a])
                res.append(split_act(v, H(n), L(n), [b]))
            give(s, b)
            yield

        sq2, sq2_free = fa(18576, T1), []

        ckh = R3[:, 0:2 * T1].rearrange("p (k t) -> p k t", k=2)
        ckl = R3[:, 2 * T1:4 * T1].rearrange("p (k t) -> p k t", k=2)
        cqh = R3[:, 1088:1600].rearrange("p (k t) -> p k t", k=2)
        cql = R3[:, 1600:2112].rearrange("p (k t) -> p k t", k=2)
        t_ck, t_cq = [], []
        tKN, tQN, tQP = {}, {}, {}

        def ev_copy(dst, T, tks, first):
            def ev(n, bk, t):
                a = cp(dst[:, n, :], bk.ap[:, 0:T], [t, first])
                give(bk, a)
                tks[n] = a
            return ev

        def lat():
            yield from gemm_a(4, 8, UHk, ULk, T1, ready_u, ev_c, ringA)
            yield from gemm_a(1, 8, UHr, ULr, 256, ready_u, ev_cq, ringA)
            yield from gemm_a(1, 8, UHr, ULr, 256, ready_u, lambda n, bk, t: ev_cq(1, bk, t), ringA)

        tGate = {}
        t_hb = ts(S_("b_gate"), S_("b_gate"), 0.5, None, ALU.mult, None, [t_sm])

        def gates(GA, n0, after):
            def ev(n, bk, t):
                assert n < 7 or len(sq2_free) == 2
                a = act(GA[:, n, :], bk.ap[:, 0:256], ACT.Tanh, [t, after, t_hb, sq2_free if n == 7 else None], bias=sc("b_gate", n0 + n), scale=0.5)
                give(bk, a)
                tGate[n0 + n] = a
            return gemm_a(8, 8, UHr, ULr, 256, ready_u, ev, ringA)

        norms = [latent_norm(CK, T1, tCK, "kv_g", lambda n: ckh[:, n, :], lambda n: ckl[:, n, :], t_ck),
                 latent_norm(CQ, 256, tCQ, "q_g", lambda n: cqh[:, n, :], lambda n: cql[:, n, :], t_cq)]
        blend(Q, [meta_part(), hgrn_group(0), hgrn_group(1)] + norms, 5, [g1, lat(), gates(GA0, 0, None)])
        ph = Q.now()
        OHh = R2[:, 0:2048].rearrange("p (k t) -> p k t", k=8)
        OHl = R2[:, 2048:4096].rearrange("p (k t) -> p k t", k=8)
        tOH = {}

        def hgrn_norm():
            a = ts(r8, ssq_bank[0:8, 0:256], 1.0 / 128, EPS, ALU.mult, ALU.add, [tSq[0]])
            give(bSSQ, a)
            a = act(r8, r8, ACT.Sqrt, [a])
            a = rcp(r8, r8, [a])
            yield
            for h0 in range(0, 8, 2):
                bk = ringB.get()
                for i in range(2):
                    w = mm(bk.ap[:, 256 * i:256 * i + 256], ident[0:8, h0 + i:h0 + i + 1].broadcast_to([8, 128]), r8,
                           True, True, [a, bk.free])
                ov = OT[:, h0:h0 + 2, :].rearrange("p h t -> p (h t)")
                b = tt(ov, ov, bk.ap[:, :], ALU.mult, [w, tO[h0]])
                give(bk, b)
                x = split_act(ov, OHh[:, h0:h0 + 2, :].rearrange("p h t -> p (h t)"),
                              OHl[:, h0:h0 + 2, :].rearrange("p h t -> p (h t)"), [b])
                tOH[h0] = tOH[h0 + 1] = x
                yield

        QN = fa(0, 2048).rearrange("p (h t) -> p h t", h=8)
        QP = fa(4096, 1024).rearrange("p (h t) -> p h t", h=4)
        VMm = fa(5120, 1024, 16)
        VM = fa(6144, 2048).rearrange("p (c n) -> p c n", c=2)
        o = 12416
        sP, sT = [], []
        for i in range(4):
            sP.append(Slot(fa(o, 416))); o += 416
        for i in range(3):
            sT.append(Slot((fa(o, 384), fa(o + 384, 256, 16)))); o += 640
        tmp = [Slot(fa(o + i * T1, T1)) for i in range(2)]; o += 2 * T1
        assert o <= 16672
        for s in sP + sT + tmp:
            s.free = ph
        ringP, ringPT = Ring(sP), Ring(sT)
        ringT = Ring(tmp)
        ringA = Ring([banks[i] for i in (0, 1, 2)])
        ringB = Ring([banks[i] for i in (4, 5, 6, 7, 3)])

        tVM = []

        def kv_values():
            for nh in range(2):
                bks = [ringA.get() for _ in range(3)]
                for k in range(2):
                    wh, wl, wt, end = take(4)
                    for i, c0 in enumerate((0, 16, 144)):
                        t = prod3(bks[i].ap[:, :], ckh[:, k, c0:c0 + 128], ckl[:, k, c0:c0 + 128], wh, wl, k == 0,
                                  k == 1, [wt, bks[i].free, t_ck])
                    done(end, t)
                a = cp(VMm[:, 512 * nh:512 * nh + 512], bks[0].ap[0:16, :], [t, ph])
                give(bks[0], a)
                tVM.append(a)
                for c in range(2):
                    a = cp(VM[:, c, 512 * nh:512 * nh + 512], bks[c + 1].ap[:, :], [t, ph])
                    give(bks[c + 1], a)
                    tVM.append(a)
                yield

        def ev_rope(n, bk, t):
            i = n // 2
            if n % 2 == 0:
                b = tt(QP[:, i, :], bk.ap[:, 0:256], C("cos")[:, NM:T1], ALU.mult, [t, ph])
                give(bk, b)
                tQP[i] = b
            else:
                s = ringT.get()
                b = tt(s.ap[:, 0:256], bk.ap[:, 0:256], C("sin")[:, NM:T1], ALU.mult, [t, s.free])
                give(bk, b)
                b = tt(QP[:, i, :], QP[:, i, :], s.ap[:, 0:256], ALU.add, [b, tQP[i]])
                give(s, b)
                tQP[i] = b

        def latents_out():
            yield from gemm_a(8, 2, lambda k: ckh[:, k, :], lambda k: ckl[:, k, :], T1, lambda k: t_ck[k],
                              ev_copy(KN, T1, tKN, ph), ringA)
            yield from kv_values()
            yield from gemm_a(8, 2, lambda k: cqh[:, k, :], lambda k: cql[:, k, :], 256, lambda k: t_cq[k],
                              ev_copy(QN, 256, tQN, ph), ringA)
            yield from gemm_a(8, 2, lambda k: cqh[:, k, :], lambda k: cql[:, k, :], 256, lambda k: t_cq[k], ev_rope,
                              ringA)
            c_dead.append(Q.q[PE][-1])

        c_dead = []
        OMh = R3[:, 0:2048].rearrange("p (k t) -> p k t", k=8)
        OMl = R3[:, 2048:4096].rearrange("p (k t) -> p k t", k=8)
        tOM = {}

        MS = float(192 ** -0.5)

        def mla_head(h):
            yield from until(lambda: c_dead and ringP.idle())
            Q.step_end = max(t.end for t in (tKN[h], tQN[h], tQP[h // 2])) + 250.0
            yield
            yield from until(ringP.idle)
            sl = ringP.get()
            S = sl.ap
            base = 64 * (h % 2)
            w_ = (144, 272)
            off = (0, 144)
            mx, nm_, sm_, ri = stat(2), stat(2), stat(2), stat(2)
            bs = []
            for c in range(2):
                bk = ringB.get()
                nk = w_[c]
                mm(bk.ap[:, 0:nk], QN[:, h, 128 * c:128 * c + 128], KN[:, h, 0:nk], True, False,
                   [bk.free, tKN[h], tQN[h]])
                w = mm(bk.ap[:, 0:nk], QP[base:base + 64, h // 2, 128 * c:128 * c + 128], KP[base:base + 64, 0:nk],
                       False, True, [tKP[0], tQP[h // 2]])
                b = ttr(S[:, off[c]:off[c] + nk], bk.ap[:, 0:nk], C("m1")[:, 272 - nk:272], ALU.add, ALU.max,
                        2 * NEG, mx[:, c:c + 1], [w, sl.free])
                give(bk, b)
                bs.append(b)
            b = ts(nm_, mx, -MS, None, ALU.mult, None, bs)
            yield
            es = []
            for c in range(2):
                Sc = S[:, off[c]:off[c] + w_[c]]
                es.append(act(Sc, Sc, ACT.Exp, [b], bias=nm_[:, c:c + 1], scale=MS, acc=sm_[:, c:c + 1]))
            b = rcp(ri, sm_, es)
            tp = []
            for c in range(2):
                Sc = S[:, off[c]:off[c] + w_[c]]
                tp.append(ts(Sc, Sc, ri[:, c:c + 1], None, ALU.mult, None, [b]))
            yield
            yield from until(ringPT.idle)
            pt = ringPT.get()
            PT, PTm = pt.ap
            bk, bm = ringB.get(), ringB.get()
            tr(bk.ap[:, 0:128], S[:, 16:144], [tp[0], bk.free])
            tr(bm.ap[0:16, 0:128], S[:, 0:16], [bm.free])
            tr(bk.ap[:, 128:256], S[:, 160:288], [tp[1]])
            tr(bk.ap[:, 256:384], S[:, 288:416])
            w = tr(bm.ap[0:16, 128:256], S[:, 144:160])
            give(sl, w)
            a1 = cp(PT, bk.ap[:, 0:384], [w, pt.free])
            a2 = vcp(PTm, bm.ap[0:16, 0:256], [w, pt.free])
            give(bk, a1)
            give(bm, a2)
            yield
            bk = ringB.get()
            vh = slice(128 * h, 128 * h + 128)
            mm(bk.ap[:, 0:256], VM[:, 0, vh], PT[:, 0:256], True, False, [a1, a2, bk.free, tVM])
            mm(bk.ap[:, 0:256], VMm[:, vh], PTm, False, False)
            w = mm(bk.ap[:, 128:256], VM[:, 1, vh], PT[:, 256:384], False, True)
            x = split_act(bk.ap[:, 0:256], OMh[:, h, :], OMl[:, h, :], [w, c_dead])
            give(bk, x)
            give(pt, w)
            tOM[h] = x
            yield

        MXh = R1[:, 0:2048].rearrange("p (k t) -> p k t", k=8)
        MXl = R1[:, 2048:4096].rearrange("p (k t) -> p k t", k=8)
        tYa, tMX = {}, {}

        def ev_ya(n, bk, t):
            b = stt(GA0[:, n, :], GA0[:, n, :], 1.0, bk.ap[:, 0:256], ALU.add, ALU.mult, [t, tGate[n]])
            give(bk, b)
            tYa[n] = b

        def ev_yb(n, bk, t):
            g = GA1[:, n, :]
            b = stt(g, g, 1.0, bk.ap[:, 0:256], ALU.add, ALU.mult, [t, tGate[8 + n]])
            give(bk, b)
            b = tt(g, g, GA0[:, n, :], ALU.add, [b, tYa[n]])
            tMX[n] = split_act(g, MXh[:, n, :], MXl[:, n, :], [b, ga_dead], 0.5)

        def ya():
            yield from gemm_a(8, 8, lambda k: OHh[:, k, :], lambda k: OHl[:, k, :], 256, lambda k: tOH[k], ev_ya, ringA)

        blend(Q, [hgrn_norm()] + [mla_head(h) for h in range(8)], 5, [latents_out(), gates(GA1, 8, ph), ya()])
        ga_dead = Q.now()
        g_mix = load(post[:, :], dr["mix_post"], ga_dead)
        for _ in gemm_a(8, 8, lambda k: OMh[:, k, :], lambda k: OMl[:, k, :], 256, lambda k: tOM[k], ev_yb, ringA):
            pass

        def gemm_b(ACC, ks, kt, H, L, rdy, first=0, last=None):
            ks = list(ks)
            last = kt - 1 if last is None else last
            got = [[take(4), take(4)] for _ in ks]
            t = [None, None]
            for c in range(2):
                for k, g in zip(ks, got):
                    for h in range(2):
                        wh, wl, wt, end = g[h]
                        t[c] = prod3(ACC[c][h].ap[:, :], H(k)[:, 128 * c:128 * c + 128], L(k)[:, 128 * c:128 * c + 128],
                                     wh, wl, k == first, k == last, [wt, rdy(k), ACC[c][h].free if k == first else None])
            return t, [g[1][3] for g in got]

        ACC = [[banks[4], banks[5]], [banks[6], banks[7]]]
        ringA = Ring([banks[i] for i in (0, 1, 2, 3)])

        def out_head(H, L, rdy, kord):
            for k in range(4):
                while not rdy(kord[k]):
                    yield "wait"
                t, ends = gemm_b(ACC, [kord[k]], 8, H, L, rdy, kord[0], kord[7])
                done(ends[0], t)
                yield

        def tail(ks, kt, H, L, rdy, g, fr, first, last, final=False):
            ks = list(ks)
            got = [[take(4), take(4)] for _ in ks]
            t, end = [None, None], {}
            for c in range(2):
                for k, gt in zip(ks, got):
                    for h in range(2):
                        wh, wl, wt, _ = gt[h]
                        t[c] = prod3(ACC[c][h].ap[:, :], H(k)[:, 128 * c:128 * c + 128], L(k)[:, 128 * c:128 * c + 128],
                                     wh, wl, k == first, k == last, [wt, rdy(k)])
                    end[k] = t[c]
            units = [(gt[1][3], end[k]) for k, gt in zip(ks, got)]
            un = list(units)
            p = post_a(0, ACC[0], t[0], g, fr)
            if len(un) == 4:
                done(*un.pop(0), PO)
            n0 = post_b(0, *p, final, un.pop(0))
            p = post_a(1, ACC[1], t[1], g, fr)
            done(*un.pop(0), PO)
            return [n0, post_b(1, *p, final, un.pop(0))]

        def out_tail(H, L, rdy, g, kord):
            set_sqrt()
            return tail(kord[4:8], 8, H, L, rdy, g, Q.now(), kord[0], kord[7])

        mxa = (lambda k: MXh[:, k, :], lambda k: MXl[:, k, :], lambda k: tMX.get(k))
        KORD1 = list(range(8))
        for _ in out_head(*mxa, KORD1):
            pass
        t_h = out_tail(*mxa, g_mix, KORD1)
        U2h = R2[:, 0:2048].rearrange("p (k t) -> p k t", k=8)
        U2l = R2[:, 2048:4096].rearrange("p (k t) -> p k t", k=8)

        def norm2(gain, n):
            return prenorm([(fa(2048 + 1024 * c, 1024), 128 * c, 128, n[c]) for c in range(2)], gain,
                           lambda k: U2h[:, k, :], lambda k: U2l[:, k, :], 256)

        t_u2 = norm2("ffn_pre", t_h)

        def ffn(nt, t_u2, hidden, gname, final=False):
            g = load(post[:, :], dr[gname], [Q.now()])
            ph = Q.now()
            hid = Ring([Slot((R3[:, 512 * i:512 * i + 256], R3[:, 512 * i + 256:512 * i + 512])) for i in range(8)])
            scr = Ring([Slot((fa(4096 + 512 * i, 256), fa(4096 + 512 * i + 256, 256))) for i in range(4)])
            for s in hid.slots + scr.slots:
                s.free = ph
            made = {}
            for i in range(nt):
                pair = []
                gen = gemm_a(2, 8, lambda k: U2h[:, k, :], lambda k: U2l[:, k, :], 256, lambda k: t_u2[k],
                             lambda n, bk, t: pair.append((bk, t)), ringA)
                for _ in gen:
                    pass
                s = scr.get()
                hs = hid.get()
                (bg, tg), (bu, tu) = pair
                b = hidden(i, bg, tg, bu, tu, s)
                give(s, b)
                x = split_act(s.ap[1], hs.ap[0], hs.ap[1], [b, hs.free])
                give(s, x)
                made[i] = (hs, x)
                if i >= LAG:
                    k = i - LAG
                    t, ends = gemm_b(ACC, [k], nt, lambda k: made[k][0].ap[0], lambda k: made[k][0].ap[1],
                                     lambda k: [made[k][1]])
                    give(made[k][0], t)
                    done(ends[0], t)
            set_sqrt()
            return tail(range(nt - LAG, nt), nt, lambda k: made[k][0].ap[0], lambda k: made[k][0].ap[1],
                        lambda k: [made[k][1]], g, ph, 0, nt - 1, final)

        def hidden1(i, bg, tg, bu, tu, s):
            a = act(s.ap[0], bg.ap[:, 0:256], ACT.Silu, [tg, s.free])
            give(bg, a)
            b = tt(s.ap[1], s.ap[0], bu.ap[:, 0:256], ALU.mult, [a, tu])
            give(bu, b)
            return b

        t_x2 = ffn(HID1, t_u2, hidden1, "ffn_post")

        t_u2 = norm2("attn_pre", t_x2)
        ph = Q.now()
        o = 0
        mq = fa(o, 512).rearrange("p (n t) -> p n t", n=2); o += 512
        mk = fa(o, 512).rearrange("p (n t) -> p n t", n=2); o += 512
        TM1 = fa(o, 1024).rearrange("p (c n) -> p c n", c=2); o += 1024
        TM2 = fa(o, 768).rearrange("p (c n) -> p c n", c=2); o += 768
        nkc = fa(o, 256); o += 256
        nq = fa(o, 512).rearrange("p (n t) -> p n t", n=2); o += 512
        nka = fa(o, 256); o += 256
        nkb = fa(o, 256); o += 256
        dqk = fa(o, 1024).rearrange("p (n t) -> p n t", n=4); o += 1024
        sqk = fa(o, 1024).rearrange("p (n t) -> p n t", n=4); o += 1024
        BI = fa(o, 1024); o += 1024
        BI2 = fa(o, 1024); o += 1024
        BI3 = fa(o, 1024); o += 1024
        wins = [fa(o, 480).rearrange("p (l n) -> p l n", l=16), CQ[:, 0:480].rearrange("p (l n) -> p l n", l=16)]
        o += 480
        hk = fa(o, 30); kcT = fa(o + 32, 15); vc = fa(o + 48, 64, 15); o += 112
        hr = fa(o, 128, 30); o += 128
        OM2 = fa(o, 2048).rearrange("p (c n) -> p c n", c=2); o += 2048
        Sc_ = fa(o, 120); o += 120
        PcT = fa(o, 1024, 15).rearrange("p (h t) -> p h t", h=4); o += 1024
        gat = fa(o, 24); o += 24
        lamt = fa(o, 88); o += 88
        oS = o; o += 7 * 384
        oPT = o; o += 5 * 384
        oX1 = o; o += 1024
        assert o <= NFA, o
        ringP = Ring([Slot(fa(oS + 384 * i, 384)) for i in range(7)])
        ringPT = Ring([Slot(fa(oPT + 384 * i, 384)) for i in range(5)])
        for s in ringP.slots + ringPT.slots:
            s.free = ph
        MIh = R3[:, 0:2048].rearrange("p (k t) -> p k t", k=8)
        MIl = R3[:, 2048:4096].rearrange("p (k t) -> p k t", k=8)
        tk = {}

        def tiles(names):
            def ev(n, bk, t):
                name, dst = names[n]
                a = cp(dst, bk.ap[:, 0:256], [t, ph])
                give(bk, a)
                tk[name] = a
            return gemm_a(len(names), 8, lambda k: U2h[:, k, :], lambda k: U2l[:, k, :], 256, lambda k: t_u2[k], ev, ringA)

        tBI = {}

        def biases(m, dst, base, scale, after):
            r = []
            for h in range(4):
                r.append(ts(dst[:, 256 * h:256 * h + 256], base, SLOPES[m + 4 * h] / scale, None, ALU.mult, None,
                            after, eng=PO))
            tBI[m] = r

        biases(0, BI, C("dmc"), 0.125, ph)
        biases(1, BI2, C("dmc"), 0.125, ph)
        biases(3, BI3, C("dms"), 0.125, ph)
        t_win = [Q.op(PO, lambda e, x=x: e.memset(x, 0.0), [ph], cost=700.0) for x in wins]
        mapped = {}

        def have(*keys):
            yield from until(lambda: all(k in tk for k in keys))
            Q.step_end = max(t.end for k in keys for t in flat(tk[k])) + 250.0
            yield

        def proj_a():
            yield from tiles([("mq0", mq[:, 0, :]), ("mq1", mq[:, 1, :]), ("mk0", mk[:, 0, :]), ("mk1", mk[:, 1, :])])
            bk = [ringA.get() for _ in range(2)]
            for k in range(8):
                wh, wl, wt, end = take(4)
                for c in range(2):
                    t = prod3(bk[c].ap[:, :], U2h[:, k, 128 * c:128 * c + 128], U2l[:, k, 128 * c:128 * c + 128],
                              wh, wl, k == 0, k == 7, [wt, bk[c].free])
                done(end, t)
                if k % 2:
                    yield
            tm1 = []
            for c in range(2):
                tm1.append(cp(TM1[:, c, :], bk[c].ap[:, :], [t]))
                give(bk[c], tm1[c])
            tk["tm1"] = tm1
            yield

        def swapped(dst, src, after):
            return [load(dst[64:128, :], src[0:64, :], after), load(dst[0:64, :], src[64:128, :], after)]

        def proj_b():
            yield from tiles([("nkc", nkc), ("nq0", nq[:, 0, :]), ("nq1", nq[:, 1, :])])
            bk = [ringA.get() for _ in range(3)]
            for k in range(8):
                wh, wl, wt, end = take(4)
                for c in range(2):
                    prod3(bk[c].ap[:, 0:268], U2h[:, k, 128 * c:128 * c + 128], U2l[:, k, 128 * c:128 * c + 128],
                          wh[:, 0:268], wl[:, 0:268], k == 0, k == 7, [wt, bk[c].free])
                t = prod3(bk[2].ap[:, 0:256], wh[:, 384:512], wl[:, 384:512], U2h[:, k, :], U2l[:, k, :],
                          k == 0, k == 7, [bk[2].free])
                done(end, t)
                if k % 2:
                    yield
            for c in range(2):
                a = cp(TM2[:, c, 0:256], bk[c].ap[:, 0:256], [t])
                b = vcp(gat[:, 12 * c:12 * c + 12], bk[c].ap[:, 256:268], [t, a])
                give(bk[c], b)
            b = act(gat, gat, ACT.Tanh, [b], scale=0.5)
            t2 = ts(gat, gat, 0.5, 0.5, ALU.mult, ALU.add, [b])
            a = cp(nka, bk[2].ap[:, 0:256], [t])
            give(bk[2], a)
            tk["nka"] = a
            tk["nkb"] = swapped(nkb, nka, [a, ph])
            tk["tm2"] = t2
            yield

        def proj_c():
            yield from tiles([(f"d{i}", dqk[:, i, :]) for i in range(4)] + [(f"s{i}", sqk[:, i, :]) for i in range(3)])
            tk["s3"] = swapped(sqk[:, 3, :], sqk[:, 2, :], [tk["s2"]])

        ringA = Ring([banks[i] for i in (0, 1, 2)])
        ringB = Ring([banks[i] for i in (4, 5, 6, 7, 3)])
        tMI, tO2 = {}, {}
        cols = (slice(0, 128), slice(128, 384))

        def maps(S, q, k, bias, scale, after, free, tbias, sink=None, mark=None):
            yield from until(ringB.idle)
            mx, nm_, sm_ = stat(2), stat(2), stat(2)
            bs = []
            for c in range(2):
                nk = 128 + 128 * c
                bk = ringB.get()
                w = mm(bk.ap[:, 0:nk], q[:, 128 * c:128 * c + 128], k[:, 0:nk], True, True, [bk.free, after])
                b = ttr(S[:, cols[c]], bk.ap[:, 0:nk], bias[:, 256 - nk:256], ALU.add, ALU.max, 2 * NEG,
                        mx[:, c:c + 1], [w, free, tbias])
                give(bk, b)
                bs.append(b)
            if mark is not None:
                mapped[mark] = bs
            if sink is not None:
                b = ts(mx, mx, scale, sink, ALU.mult, ALU.max, bs)
                b = ts(nm_, mx, -1.0, None, ALU.mult, None, [b])
            else:
                b = ts(nm_, mx, -scale, None, ALU.mult, None, bs)
            yield
            es = []
            for c in range(2):
                es.append(act(S[:, cols[c]], S[:, cols[c]], ACT.Exp, [b], bias=nm_[:, c:c + 1], scale=scale,
                              acc=sm_[:, c:c + 1]))
            if sink is not None:
                e2 = stat(2)
                a = act(e2, nm_, ACT.Exp, [b], bias=sink)
                es = [es, tt(sm_, sm_, e2, ALU.add, [es, a])]
            return es, sm_

        def transp(sl, after):
            yield from until(lambda: ringB.idle() and ringPT.idle())
            S, pt = sl.ap, ringPT.get()
            bk = ringB.get()
            tr(bk.ap[:, 0:128], S[:, 0:128], [after, bk.free])
            tr(bk.ap[:, 128:256], S[:, 128:256])
            w = tr(bk.ap[:, 256:384], S[:, 256:384])
            a = cp(pt.ap, bk.ap[:, 0:384], [w, pt.free])
            give(bk, a)
            give(sl, w)
            return pt, a

        def pv(pt, V, after):
            yield from until(ringB.idle)
            PT = pt.ap
            bk = ringB.get()
            mm(bk.ap[:, 0:64], PT[:, 0:128], V[0], True, True, [after, bk.free])
            mm(bk.ap[:, 64:128], PT[:, 128:256], V[0], True, False)
            w = mm(bk.ap[:, 64:128], PT[:, 256:384], V[1], False, True)
            give(pt, w)
            return bk, w

        def to_features(kt):
            bk = ringB.get()
            for c in range(2):
                w = tr(bk.ap[:, 128 * c:128 * c + 128], OM2[:, c, 128 * kt:128 * kt + 128],
                       [tO2[2 * kt], tO2[2 * kt + 1], bk.free])
            x = split_act(bk.ap[:, 0:256], MIh[:, kt, :], MIl[:, kt, :], [w, ph])
            give(bk, x)
            tMI[kt] = x

        def head_done(gh, tok):
            tO2[gh] = tok
            yield
            if gh ^ 1 in tO2 and gh // 2 not in tMI:
                yield from until(ringB.idle)
                to_features(gh // 2)

        def plain_head(gh, q, k, keys, bias, tb, V, vt, sink=None, mark=None):
            yield from have(*keys)
            yield from until(ringP.idle)
            sl = ringP.get()
            e, sm_ = yield from maps(sl.ap, q, k, bias, 0.125, [tk[x] for x in keys], sl.free, tb, sink, mark)
            yield
            pt, a = yield from transp(sl, e)
            ri = stat(2)
            br = rcp(ri, sm_, [e])
            yield
            yield from have(vt)
            bk, w = yield from pv(pt, V, [a, tk[vt]])
            yield
            for c in range(2):
                b = ts(OM2[:, c, 64 * gh:64 * gh + 64], bk.ap[:, 64 * c:64 * c + 64], ri[:, c:c + 1], None, ALU.mult,
                       None, [w, br, ph])
            give(bk, b)
            yield from head_done(gh, b)

        def moba_head(h):
            b0 = 64 * (h % 2)
            return plain_head(h, mq[b0:b0 + 64, h // 2, :], mk[b0:b0 + 64, h // 2, :],
                              [f"mq{h // 2}", f"mk{h // 2}"], BI[:, 256 * h:256 * h + 256], tBI[0],
                              [TM1[:, c, 64 * h:64 * h + 64] for c in range(2)], "tm1", mark=h)

        def swa_head(h):
            b0 = 64 * (h % 2)
            g = h // 2
            kt = 2 if 64 * g == b0 else 3
            yield from plain_head(12 + h, sqk[b0:b0 + 64, h // 2, :], sqk[b0:b0 + 64, kt, :],
                                  [f"s{h // 2}", f"s{kt}"], BI3[:, 256 * h:256 * h + 256], tBI[3],
                                  [TM2[:, c, 128 + 64 * g:192 + 64 * g] for c in range(2)], "tm2",
                                  sc("sinks", h))

        def nsa_head(h):
            b0 = 64 * (h % 2)
            gh = 4 + h
            q = nq[b0:b0 + 64, h // 2, :]
            prev = None
            low, high = (nka, "nka"), (nkb, "nkb")
            for (k, kname), gi, voff in ((low if b0 == 0 else high, 1, 0), (high if b0 == 0 else low, 2, 64)):
                yield from have(f"nq{h // 2}", kname)
                yield from until(ringP.idle)
                sl = ringP.get()
                e, sm_ = yield from maps(sl.ap, q, k[b0:b0 + 64, :], BI2[:, 256 * h:256 * h + 256], 0.125,
                                         [tk[f"nq{h // 2}"], tk[kname]], sl.free, tBI[1])
                yield
                yield from have("tm2")
                pt, a = yield from transp(sl, e)
                ri = stat(2)
                b = rcp(ri, sm_, [e])
                gv = gat.rearrange("p (c n) -> p c n", c=2)[:, :, 3 * h + gi]
                br = tt(ri, ri, gv, ALU.mult, [b, tk["tm2"]])
                yield
                bk, w = yield from pv(pt, [TM2[:, c, voff:voff + 64] for c in range(2)], [a, tk["tm2"]])
                yield
                n = []
                for c in range(2):
                    o_ = OM2[:, c, 64 * gh:64 * gh + 64]
                    p_ = bk.ap[:, 64 * c:64 * c + 64]
                    if prev is None:
                        n.append(ts(o_, p_, ri[:, c:c + 1], None, ALU.mult, None, [w, br, ph]))
                    else:
                        n.append(stt(o_, p_, ri[:, c:c + 1], o_, ALU.mult, ALU.add, [w, br, prev]))
                give(bk, n)
                prev = n
            yield from have("pct")
            yield from until(ringB.idle)
            bk = ringB.get()
            for c in range(2):
                w = mm(bk.ap[:, 64 * c:64 * c + 64], PcT[:, h, 128 * c:128 * c + 128], vc, True, True,
                       [bk.free, tk["pct"]])
            o_ = OM2[:, :, 64 * gh:64 * gh + 64]
            b = tt(o_, o_, bk.ap[:, 0:128].rearrange("p (c n) -> p c n", c=2), ALU.add, [w, prev])
            give(bk, b)
            yield from head_done(gh, b)

        def nsa_cmp():
            yield from have("nkc")
            pos = S_("cmp_pos")
            nv = nkc.rearrange("p (n l) -> p l n", l=16)
            ws = []
            for i in range(2):
                for p0, c0 in ((0, 0), (64, 15)):
                    p = slice(p0, p0 + 64)
                    ws.append(tt(wins[i][p, :, c0:c0 + 15], nv[p, :, i:i + 15],
                                 pos[p, 16 * i:16 * i + 16].rearrange("p (l o) -> p l o", o=1).broadcast_to([64, 16, 15]),
                                 ALU.add, [tk["nkc"], ph, t_win]))
            yield
            yield from until(lambda: ringB.idle() > 1)
            bk = ringB.get()
            for q in range(4):
                c = w1_tok[q]
                for l8 in range(8):
                    l = 8 * q + l8
                    t = mm(bk.ap[0:30, 0:128], wins[l // 16][:, l % 16, :], w1b[q % 2][:, 128 * l8:128 * l8 + 128],
                           l == 0, l == 31, [c, ws, bk.free])
                    if l8 == 3:
                        yield
                w1_free[q] = [t]
                if q < 2:
                    load_w1(q + 2)
                yield
            c = vcp(hr, bk.ap[0:30, 0:128], [t, ph])
            give(bk, c)
            yield
            yield from until(ringB.idle)
            bk = ringB.get()
            w = tr(bk.ap[:, 0:30], hr, [c, bk.free])
            for i in range(2):
                a = act(hk[:, 15 * i:15 * i + 15], bk.ap[:, 15 * i:15 * i + 15], ACT.Gelu_apprx_tanh, [w, ph],
                        bias=sc("cmp_b1", i))
            give(bk, a)
            yield
            yield from until(ringB.idle)
            bk = ringB.get()
            w = mm(bk.ap[:, 0:15], S_("w2k"), hk[:, 0:15], True, True, [a, bk.free])
            w = mm(bk.ap[0:15, 64:128], hk[:, 15:30], S_("w2v"), True, True)
            a = acp(kcT, bk.ap[:, 0:15], [w, ph])
            a = acp(vc, bk.ap[0:15, 64:128], [w, ph])
            give(bk, a)
            yield
            yield from have("nq0", "nq1", "tm2")
            yield from until(ringB.idle)
            sv = Sc_.rearrange("p (c h n) -> p c h n", c=2, h=4)
            cb = C("cmpb").rearrange("p (c h n) -> p c h n", c=2, h=4)
            sf = Sc_.rearrange("p (x n) -> p x n", n=15)
            mx, s8 = stat(8), stat(8)
            bs = []
            for par in range(2):
                bk = ringB.get()
                for c in range(2):
                    for hp in range(2):
                        x = 2 * c + hp
                        w = mm(bk.ap[:, 16 * x:16 * x + 15],
                               nq[64 * par:64 * par + 64, hp, 128 * c:128 * c + 128],
                               kcT[64 * par:64 * par + 64, :], True, True, [a, bk.free, tk["nq0"], tk["nq1"]])
                pv_ = bk.ap[:, 0:64].rearrange("p (x n) -> p x n", n=16)[:, :, 0:15]
                bs.append(tt(sf[:, par:8:2, :], pv_, C("cmpb").rearrange("p (x n) -> p x n", n=15)[:, par:8:2, :],
                             ALU.add, [w, ph]))
                give(bk, bs[-1])
            b = bs
            b = red(mx, sf, ALU.max, [b])
            b = ts(mx, mx, -1e20, None, ALU.max, None, [b])
            b = tt(sf, sf, bcast(mx, 15), ALU.subtract, [b])
            a = act(Sc_, Sc_, ACT.Exp, [b], scale=0.125)
            yield
            b = red(s8, sf, ALU.add, [a])
            b = ts(s8, s8, 1e-30, None, ALU.max, None, [b])
            b = rcp(s8, s8, [b])
            gv = gat.rearrange("p (x g) -> p x g", g=3)[:, :, 0]
            b = tt(s8, s8, gv, ALU.mult, [b, tk["tm2"]])
            b = tt(sf, sf, bcast(s8, 15), ALU.mult, [b])
            yield
            yield from until(ringB.idle)
            for hp in range(2):
                bk = ringB.get()
                for i in range(2):
                    for c in range(2):
                        w = tr(bk.ap[0:15, 256 * i + 128 * c:256 * i + 128 * c + 128], sv[:, c, 2 * hp + i, :], [b, bk.free])
                a = acp(PcT[:, 2 * hp:2 * hp + 2, :].rearrange("p h t -> p (h t)"), bk.ap[0:15, :], [w, ph])
                give(bk, a)
            tk["pct"] = a
            yield

        w1b = [post[:, :], fa(oX1, 1024)]
        w1_free = {}
        w1sem = [ctx.enter_context(nc.semaphore(f"w1_{i}")) for i in range(2)]

        def load_w1(q):
            dst, src = w1b[q % 2], dr["w1"][q]
            w1_tok[q] = Q.op(PO, lambda e: e.dma_start(dst, src), [w1_free.get(q - 2), w1_start],
                             sem=w1sem[q % 2], val=16 * (q // 2 + 1), cost=1500.0)

        w1_start = ph
        w1_tok = {}
        load_w1(0)
        load_w1(1)

        DS = float(32 ** -0.5)

        def lam_part():
            l = S_("lam")
            v = lamt[:, 0:64].rearrange("p (a n) -> p a n", a=2)
            lv = l.rearrange("p (a b n) -> p a b n", a=2, b=2)
            b = tt(v, lv[:, :, 0, :], lv[:, :, 1, :], ALU.mult, [ph])
            b = red(lamt[:, 64:66], v, ALU.add, [b])
            a = act(lamt[:, 66:68], lamt[:, 64:66], ACT.Exp, [b])
            b = tt(lamt[:, 68:69], lamt[:, 67:68], lamt[:, 66:67], ALU.subtract, [a])
            tk["lam"] = ts(lamt[:, 69:70], lamt[:, 68:69], -LINIT, None, ALU.add, None, [b])

        LINIT = 0.8 - 0.6 * 1.0
        nlam = lamt[:, 69:70]
        tD = {}

        def diff_head(h):
            n, b0 = h // 2, 64 * (h % 2)
            gh = 8 + h
            yield from until(lambda: h in mapped)
            bias = BI[:, 256 * h:256 * h + 256]
            tb = ts(bias, C("dmc"), SLOPES[2 + 4 * h] / DS, None, ALU.mult, None, [mapped[h], tBI[0]], eng=PO)
            yield from have(f"d{n}", f"d{2 + n}")
            yield from until(lambda: ringP.idle() > 1)
            sl, slz = ringP.get(), ringP.get()
            aft = [tk[f"d{n}"], tk[f"d{2 + n}"]]
            S, Z = sl.ap, slz.ap
            e1_, s1 = yield from maps(S, dqk[b0:b0 + 32, n, :], dqk[b0:b0 + 32, 2 + n, :], bias, DS, aft,
                                      sl.free, tb)
            yield
            e2_, s2 = yield from maps(Z, dqk[b0 + 32:b0 + 64, n, :], dqk[b0 + 32:b0 + 64, 2 + n, :], bias, DS, aft,
                                      slz.free, tb)
            yield
            r1, r2 = stat(2), stat(2)
            b1 = rcp(r1, s1, [e1_])
            b2 = rcp(r2, s2, [e2_])
            b2 = ts(r2, r2, nlam, None, ALU.mult, None, [b2, tk["lam"]])
            b1 = [ts(S[:, cols[c]], S[:, cols[c]], r1[:, c:c + 1], None, ALU.mult, None, [b1]) for c in range(2)]
            tp = [stt(S[:, cols[c]], Z[:, cols[c]], r2[:, c:c + 1], S[:, cols[c]], ALU.mult, ALU.add, [b1[c], b2])
                  for c in range(2)]
            give(slz, tp)
            yield
            pt, a = yield from transp(sl, tp)
            yield
            bk, w = yield from pv(pt, [TM1[:, c, 256 + 64 * h:320 + 64 * h] for c in range(2)], [a, tk["tm1"]])
            yield
            ys = []
            for c in range(2):
                ys.append(act(OM2[:, c, 64 * gh:64 * gh + 64], bk.ap[:, 64 * c:64 * c + 64], ACT.Square, [w, ph],
                              acc=dnr[:, 2 * h + c:2 * h + c + 1]))
            for c in range(2):
                b2 = stt(OM2[:, c, 64 * gh:64 * gh + 64], bk.ap[:, 64 * c:64 * c + 64], 1.0 - LINIT, S_("subln"),
                         ALU.mult, ALU.mult, [ys])
            give(bk, b2)
            tD[h] = [ys, b2]
            yield
            if len(tD) == 4:
                yield from diff_norm()

        def diff_norm():
            b = ts(dnr[:, 8:16], dnr[:, 0:8], 1.0 / 64, EPS, ALU.mult, ALU.add, [tD[h] for h in range(4)])
            a = act(dnr[:, 8:16], dnr[:, 8:16], ACT.Sqrt, [b])
            b = rcp(dnr[:, 8:16], dnr[:, 8:16], [a])
            for h in range(4):
                for c in range(2):
                    o_ = OM2[:, c, 64 * (8 + h):64 * (8 + h) + 64]
                    b2 = ts(o_, o_, dnr[:, 8 + 2 * h + c:9 + 2 * h + c], None, ALU.mult, None, [b])
                tO2[8 + h] = b2
            yield
            for kt in (4, 5):
                yield from until(ringB.idle)
                to_features(kt)

        dnr = lamt[:, 70:86]
        mia = (lambda k: MIh[:, k, :], lambda k: MIl[:, k, :], lambda k: tMI.get(k))

        def out2():
            nonlocal ACC, ringA
            b3 = banks[3]
            while b3.busy:
                yield "wait"
            ringB.slots.remove(b3)
            for b in banks[0:4]:
                assert not b.busy
            ACC = [[banks[0], banks[1]], [banks[2], banks[3]]]
            ringA = Ring([banks[i] for i in (4, 5, 6, 7)])
            tk["post"] = load(post[:, :], dr["attn_post"], [w1_free[2]])
            yield from out_head(*mia, KORD2)

        lam_part()
        blend(Q, [moba_head(h) for h in range(4)] + [nsa_cmp()] + [nsa_head(h) for h in range(4)]
              + [diff_head(h) for h in range(4)] + [swa_head(h) for h in range(4)], 7, [proj_a(), proj_b(), proj_c(), out2()])
        t_h = out_tail(*mia, tk["post"], KORD2)
        t_u2 = norm2("ffn_pre2", t_h)

        cw = S_("conv_w").rearrange("p (i n) -> p i n", i=3)

        def hidden2(i, bg, tg, bu, tu, s):
            g = bg.ap
            c = s.ap[0]
            b = ts(c, g[:, 0:256], cw[:, 2, i:i + 1], sc("conv_b", i), ALU.mult, ALU.add, [tg, s.free])
            b = stt(c[:, 1:256], g[:, 0:255], cw[:, 1, i:i + 1], c[:, 1:256], ALU.mult, ALU.add, [b])
            b = stt(c[:, 2:256], g[:, 0:254], cw[:, 0, i:i + 1], c[:, 2:256], ALU.mult, ALU.add, [b])
            give(bg, b)
            a = act(c, c, ACT.Gelu_apprx_tanh, [b])
            b = tt(s.ap[1], c, bu.ap[:, 0:256], ALU.mult, [a, tu])
            give(bu, b)
            return b

        t_x3 = ffn(HID2, t_u2, hidden2, "ffn_post2", True)
        s_out = ctx.enter_context(nc.semaphore("s_out"))
        for c in range(2):
            for h in range(2):
                dst = dr["out"][0, 128 * c:128 * c + 128, 512 * h:512 * h + 512]
                src = X[:, 1024 * c + 512 * h:1024 * c + 512 * h + 512]
                Q.op(SP, lambda e, dst=dst, src=src: e.dma_start(dst, src), [t_x3[c][h]], sem=s_out,
                     val=16 * (2 * c + h) + 16)
        assert cur[0] == len(BLOCKS), (cur[0], len(BLOCKS))

        Q.count()
        block = ctx.enter_context(nc.Block())

        @block.sync
        def _(e):
            Q.emit("sp", e)
            e.wait_ge(s_out, 64)

        @block.tensor
        def _(e):
            Q.emit("pe", e)

        @block.scalar
        def _(e):
            Q.emit("act", e)

        @block.vector
        def _(e):
            Q.emit("dve", e)

        @block.gpsimd
        def _(e):
            Q.emit("pool", e)


def kernel(**inputs):
    import concourse.bacc as bacc
    from concourse.bass_utils import run_bass_kernel_spmd as run

    I = {k: np.asarray(v) for k, v in inputs.items()}
    f = np.float32
    mats = {n: I[n][0] for n in ("w_in", "w_hg_o", "w_q_b", "w_kv_b", "w_mla_o", "w_out", "w_ffn_in", "w_ffn_out",
                                 "w_in_2", "w_out_2", "ffn_w_gate_2", "ffn_w_up_2", "ffn_w_down_2")}
    W = np.zeros((NSLAB, 128, SLABW), f)
    for i, (n, r, cols) in enumerate(BLOCKS):
        keep = [c for c in cols if c >= 0]
        W[i // 16, :, 128 * (i % 16):128 * (i % 16) + len(keep)] = mats[n][r:r + 128][:, keep]
    sm = np.zeros((128, NSM), f)

    def put(n, v, p=slice(0, 128)):
        sm[p, SM[n][0]:SM[n][0] + SM[n][1]] = v

    def colv(v, n):
        return np.reshape(v, (n, 128)).T

    put("mix_pre", colv(I["mix_pre_g"], 8))
    put("ffn_pre", colv(I["ffn_pre_g"], 8))
    put("attn_pre", colv(I["attn_pre_norm_2"], 8))
    put("ffn_pre2", colv(I["ffn_pre_norm_2"], 8))
    put("b_gate", colv(I["b_gate"], 16))
    put("lb0", colv(I["lb_logits"][0], 8))
    put("lb1", colv(I["lb_logits"][1], 8))
    put("hg_g", colv(I["hg_norm_g"], 1))
    put("q_g", colv(I["q_a_norm_g"], 2))
    put("kv_g", colv(I["kv_a_norm_g"], 2))
    put("conv_w", np.concatenate([colv(I["ffn_conv_w_2"][0, i], 32) for i in range(3)], 1))
    put("conv_b", colv(I["ffn_conv_b_2"], 32))
    put("cmp_b1", np.stack([I["nsa_cmp_b1_k_2"][0], I["nsa_cmp_b1_v_2"][0]], 1))
    put("cmp_pos", I["nsa_cmp_pos_k_2"][0].T, slice(0, 64))
    put("cmp_pos", I["nsa_cmp_pos_v_2"][0].T, slice(64, 128))
    put("w2k", np.concatenate([I["nsa_cmp_w2_k_2"][0]] * 2, 1))
    put("w2v", I["nsa_cmp_w2_v_2"][0])
    put("subln", I["diff_subln_2"][0][None])
    put("lam", np.concatenate([I[n][0] for n in ("diff_lambda_q1_2", "diff_lambda_k1_2", "diff_lambda_q2_2",
                                                 "diff_lambda_k2_2")])[None])
    put("sinks", I["swa_sinks_2"][0][None])
    w1 = np.zeros((4, 128, 1024), f)
    for q in range(4):
        for half, n in enumerate(("nsa_cmp_w1_k_2", "nsa_cmp_w1_v_2")):
            w1[q, 64 * half:64 * half + 64] = I[n][0][8 * q:8 * q + 8].transpose(1, 0, 2).reshape(64, 1024)
    cst, lev = constants()
    arrays = {"x": I["x"], "meta": I["meta_tokens"], "cst": cst, "lev": lev, "sm": sm, "w": W, "w1": w1}
    for n, k in (("mix_post", "mix_post_g"), ("ffn_post", "ffn_post_g"), ("attn_post", "attn_post_norm_2"),
                 ("ffn_post2", "ffn_post_norm_2")):
        arrays[n] = np.ascontiguousarray(np.broadcast_to(I[k][0][None], (128, D)))
    nc = bacc.Bacc("TRN2", target_bir_lowering=False, num_devices=1)
    dr, sent = {}, {}
    for n, a in arrays.items():
        a = np.ascontiguousarray(a)
        sent["in_" + n] = a
        dr[n] = nc.dram_tensor("in_" + n, a.shape, mybir.dt.from_np(a.dtype), kind="ExternalInput").ap()
    dr["out"] = nc.dram_tensor("out_0", (1, 256, D), FP, kind="ExternalOutput").ap()
    program(nc, dr)
    r = run(nc, [sent], core_ids=[0])
    return r.results[0]["out_0"]
```
